# Optimizing a Trainium2 kernel written in Bass

```python
import jax, jax.numpy as jnp
from jax import lax
import numpy as np

D_MODEL = 1024
BATCH = 1
SEQ = 512
DEPTH = 1

CHUNK = 64
MEM_LEN = 256
CONV_DIM = D_MODEL
CONV_WIDTH = 3
SB_HEADS = 16
SB_HEAD_DIM = 64
SB_DIM = SB_HEADS * SB_HEAD_DIM
SB_BLOCK = 128
X_HEADS = 4
X_HEAD_DIM = 256
X_DIM = X_HEADS * X_HEAD_DIM
N_BRANCH = 3
D_FF = 4 * D_MODEL
EPS = 1e-6

IN_SPLITS = [CONV_DIM, CONV_DIM, CONV_DIM, SB_DIM, SB_DIM, SB_DIM, X_DIM, N_BRANCH * D_MODEL]
IN_COLS = int(sum(IN_SPLITS))


def rms_norm(x, g):
    xf = x.astype(jnp.float32)
    y = xf * lax.rsqrt(jnp.mean(xf * xf, axis=-1, keepdims=True) + EPS)
    return (y * g.astype(jnp.float32)).astype(x.dtype)

def causal_depthwise_conv(u, w):
    c = u.shape[-1]
    return lax.conv_general_dilated(
        u, w.astype(u.dtype)[:, None, :], window_strides=(1,),
        padding=[(CONV_WIDTH - 1, 0)],
        dimension_numbers=("NWC", "WIO", "NWC"),
        feature_group_count=c)

def stick_breaking_attention(q, k, v):
    seq = q.shape[2]
    scale = q.shape[-1] ** -0.5
    outs = []
    for start in range(0, seq, SB_BLOCK):
        end = start + SB_BLOCK
        qb = q[:, :, start:end]
        kb = k[:, :, :end]
        vb = v[:, :, :end]
        z = jnp.einsum("bhqd,bhkd->bhqk", qb, kb).astype(jnp.float32) * scale
        t_idx = start + jnp.arange(SB_BLOCK)[:, None]
        s_idx = jnp.arange(end)[None, :]
        past = s_idx < t_idx
        log_beta = jax.nn.log_sigmoid(z)
        log_1mb = jnp.where(past, jax.nn.log_sigmoid(-z), 0.0)
        between = lax.cumsum(log_1mb, axis=3, reverse=True) - log_1mb
        a = jnp.where(past, jnp.exp(log_beta + between), 0.0)
        outs.append(jnp.einsum("bhqk,bhkd->bhqd", a.astype(vb.dtype), vb))
    return jnp.concatenate(outs, axis=2)

def memory_cross_attention(xq, mem_n, w_mem_kv, q_norm_g, k_norm_g):
    b, s, _ = xq.shape
    m = mem_n.shape[1]
    q = xq.reshape(b, s, X_HEADS, X_HEAD_DIM)
    kv = mem_n @ w_mem_kv
    k, v = jnp.split(kv, 2, axis=-1)
    k = k.reshape(b, m, X_HEADS, X_HEAD_DIM)
    v = v.reshape(b, m, X_HEADS, X_HEAD_DIM)
    q = rms_norm(q, q_norm_g)
    k = rms_norm(k, k_norm_g)
    scores = jnp.einsum("bqhd,bkhd->bhqk", q, k).astype(jnp.float32) * (X_HEAD_DIM ** -0.5)
    p = jax.nn.softmax(scores, axis=-1).astype(v.dtype)
    o = jnp.einsum("bhqk,bkhd->bqhd", p, v)
    return o.reshape(b, s, X_DIM)

def first_inputs(seed: int = 0) -> dict:
    key = jax.random.key(seed)
    ks = jax.random.split(key, 20)
    f32 = jnp.float32

    def nrm(k, shape, fan_in):
        return jax.random.normal(k, shape, f32) * (fan_in ** -0.5)

    def gain(k, shape):
        return 1.0 + 0.02 * jax.random.normal(k, shape, f32)

    L = DEPTH
    return {
        "x": jax.random.normal(ks[0], (BATCH, SEQ, D_MODEL), f32),
        "mem": jax.random.normal(ks[1], (BATCH, MEM_LEN, D_MODEL), f32),
        "g_mix": gain(ks[2], (L, D_MODEL)),
        "g_mem": gain(ks[3], (L, D_MODEL)),
        "w_in": nrm(ks[4], (L, D_MODEL, IN_COLS), D_MODEL),
        "conv_w": nrm(ks[5], (L, CONV_WIDTH, CONV_DIM), CONV_WIDTH),
        "w_conv_out": nrm(ks[6], (L, CONV_DIM, D_MODEL), CONV_DIM),
        "w_sb_out": nrm(ks[7], (L, SB_DIM, D_MODEL), SB_DIM),
        "q_norm_g": gain(ks[8], (L, X_HEAD_DIM)),
        "k_norm_g": gain(ks[9], (L, X_HEAD_DIM)),
        "w_mem_kv": nrm(ks[10], (L, D_MODEL, 2 * X_DIM), D_MODEL),
        "w_x_out": nrm(ks[11], (L, X_DIM, D_MODEL), X_DIM),
        "w_out": nrm(ks[12], (L, D_MODEL, D_MODEL), D_MODEL),
        "g_mlp": gain(ks[13], (L, D_MODEL)),
        "w_up": nrm(ks[14], (L, D_MODEL, D_FF), D_MODEL),
        "w_down": nrm(ks[15], (L, D_FF, D_MODEL), D_FF),
    }

def first_block(x, mem, g_mix, g_mem, w_in, conv_w, w_conv_out, w_sb_out, q_norm_g,
              k_norm_g, w_mem_kv, w_x_out, w_out, g_mlp, w_up, w_down):
    b, s, d = x.shape
    split_idx = list(np.cumsum(IN_SPLITS)[:-1])
    for l in range(DEPTH):
        h = rms_norm(x, g_mix[l])
        proj = h @ w_in[l]
        c_h, c_b, c_c, sq, sk, sv, xq, gate_pre = jnp.split(proj, split_idx, axis=-1)

        y_conv = (c_b * causal_depthwise_conv(c_c * c_h, conv_w[l])) @ w_conv_out[l]

        to_heads = lambda t: t.reshape(b, s, SB_HEADS, SB_HEAD_DIM).transpose(0, 2, 1, 3)
        o_sb = stick_breaking_attention(to_heads(sq), to_heads(sk), to_heads(sv))
        y_sb = o_sb.transpose(0, 2, 1, 3).reshape(b, s, SB_DIM) @ w_sb_out[l]

        mem_n = rms_norm(mem, g_mem[l])
        y_x = memory_cross_attention(xq, mem_n, w_mem_kv[l], q_norm_g[l], k_norm_g[l]) @ w_x_out[l]

        gates = jax.nn.sigmoid(gate_pre.astype(jnp.float32)).astype(x.dtype)
        gates = gates.reshape(b, s, N_BRANCH, d)
        merged = gates[:, :, 0] * y_conv + gates[:, :, 1] * y_sb + gates[:, :, 2] * y_x
        x = x + merged @ w_out[l]

        h2 = rms_norm(x, g_mlp[l])
        x = x + jnp.square(jax.nn.relu(h2 @ w_up[l])) @ w_down[l]
    return x


DEPTH_2 = 2

HEAD_DIM = 64
H_A = D_MODEL // (2 * HEAD_DIM)
A_PREV_CHUNKS = 8
MAX_REL_DIST = 256
H_B = D_MODEL // (2 * HEAD_DIM)
H_B_KV = H_B // 4
B_WINDOW = 128
B_PREV_CHUNKS = B_WINDOW // CHUNK
ATTN_PROJ = 3 * H_A * HEAD_DIM + H_B * HEAD_DIM + 2 * H_B_KV * HEAD_DIM
D_INNER = 2 * D_MODEL
SSM_HEAD_DIM = 64
SSM_HEADS = D_INNER // SSM_HEAD_DIM
SSM_GROUPS = 4
SSM_STATE = 128
SSM_CONV = 4
SSD_CHUNK = 64
SSM_CONV_CH = D_INNER + 2 * SSM_GROUPS * SSM_STATE
SSM_PROJ = D_INNER + SSM_CONV_CH + SSM_HEADS
D_FF_2 = ((8 * D_MODEL // 3 + 127) // 128) * 128
FFN_CONV = 3


def rmsnorm(x, g):
    xf = x.astype(jnp.float32)
    y = xf * lax.rsqrt(jnp.mean(xf * xf, axis=-1, keepdims=True) + EPS)
    return (y * g.astype(jnp.float32)).astype(x.dtype)

def causal_dwconv(x, w, b):
    k = w.shape[0]
    y = lax.conv_general_dilated(
        x, w[:, None, :].astype(x.dtype), window_strides=(1,), padding=[(k - 1, 0)],
        dimension_numbers=("NWC", "WIO", "NWC"), feature_group_count=x.shape[-1])
    return y + b.astype(x.dtype)

def band_offsets(n_prev):
    band = (n_prev + 1) * CHUNK
    q_off = jnp.arange(CHUNK, dtype=jnp.int32)
    k_off = jnp.arange(band, dtype=jnp.int32) - n_prev * CHUNK
    return q_off[:, None] - k_off[None, :], k_off

def band_attention(q, k, v, n_prev, bias, sinks):
    b, s, hq, d = q.shape
    hkv = k.shape[2]
    grp = hq // hkv
    nc = s // CHUNK
    band = (n_prev + 1) * CHUNK
    pad = n_prev * CHUNK
    kp = jnp.pad(k, ((0, 0), (pad, 0), (0, 0), (0, 0)))
    vp = jnp.pad(v, ((0, 0), (pad, 0), (0, 0), (0, 0)))
    qc = jnp.moveaxis(q.reshape(b, nc, CHUNK, hkv, grp, d), 1, 0)
    _, k_off = band_offsets(n_prev)
    scale = d ** -0.5

    def one_chunk(args):
        c, qb = args
        start = c * CHUNK
        kb = lax.dynamic_slice_in_dim(kp, start, band, axis=1)
        vb = lax.dynamic_slice_in_dim(vp, start, band, axis=1)
        sc = jnp.einsum("bqkgd,bskd->bkgqs", qb, kb).astype(jnp.float32) * scale + bias
        valid = (start + k_off) >= 0
        sc = jnp.where(valid, sc, -jnp.inf)
        if sinks is None:
            p = jax.nn.softmax(sc, axis=-1)
        else:
            snk = sinks.astype(jnp.float32)[None, :, :, None, None]
            m = jnp.maximum(jnp.max(sc, axis=-1, keepdims=True), snk)
            e = jnp.exp(sc - m)
            p = e / (jnp.sum(e, axis=-1, keepdims=True) + jnp.exp(snk - m))
        return jnp.einsum("bkgqs,bskd->bqkgd", p.astype(vb.dtype), vb)

    out = lax.map(one_chunk, (jnp.arange(nc, dtype=jnp.int32), qc))
    return jnp.moveaxis(out, 0, 1).reshape(b, s, hq * d)

def attn_layer(h, w_in, w_out, relpos_table, q_norm_a, k_norm_a, q_norm_b, k_norm_b, sinks):
    b, s, _ = h.shape
    da, db, dkv = H_A * HEAD_DIM, H_B * HEAD_DIM, H_B_KV * HEAD_DIM
    cuts = [da, 2 * da, 3 * da, 3 * da + db, 3 * da + db + dkv]
    qa, ka, va, qb, kb, vb = jnp.split(h @ w_in, cuts, axis=-1)
    heads = lambda t, n: t.reshape(b, s, n, HEAD_DIM)
    qa = rmsnorm(heads(qa, H_A), q_norm_a)
    ka = rmsnorm(heads(ka, H_A), k_norm_a)
    rel_a, _ = band_offsets(A_PREV_CHUNKS)
    idx = jnp.clip(rel_a, -MAX_REL_DIST, MAX_REL_DIST) + MAX_REL_DIST
    bias_a = relpos_table.astype(jnp.float32)[:, idx][:, None]
    oa = band_attention(qa, ka, heads(va, H_A), A_PREV_CHUNKS, bias_a, None)
    qb = rmsnorm(heads(qb, H_B), q_norm_b)
    kb = rmsnorm(heads(kb, H_B_KV), k_norm_b)
    rel_b, _ = band_offsets(B_PREV_CHUNKS)
    slopes = 2.0 ** (-8.0 * jnp.arange(1, H_B + 1, dtype=jnp.float32) / H_B)
    bias_b = (-slopes[:, None, None] * jnp.abs(rel_b).astype(jnp.float32)).reshape(
        H_B_KV, H_B // H_B_KV, CHUNK, (B_PREV_CHUNKS + 1) * CHUNK)
    ob = band_attention(qb, kb, heads(vb, H_B_KV), B_PREV_CHUNKS, bias_b,
                        sinks.reshape(H_B_KV, H_B // H_B_KV))
    return jnp.concatenate([oa, ob], axis=-1) @ w_out

def ssd_scan(x, dt, a, bm, cm):
    b, s, h, p = x.shape
    g, n = bm.shape[2], bm.shape[3]
    r = h // g
    L = SSD_CHUNK
    nc = s // L

    def to_chunks(t):
        return jnp.moveaxis(t.reshape((b, nc, L) + t.shape[2:]), 1, 0)

    xc = to_chunks(x.reshape(b, s, g, r, p))
    dtc = to_chunks(dt.reshape(b, s, g, r))
    bc, cc = to_chunks(bm), to_chunks(cm)
    a = a.reshape(g, r)
    causal = jnp.tril(jnp.ones((L, L), dtype=bool))[None, :, :, None, None]

    def step(state, inp):
        xk, dtk, bk, ck = inp
        acs = jnp.cumsum(dtk * a, axis=1)
        seg = acs[:, :, None] - acs[:, None, :]
        decay = jnp.exp(jnp.where(causal, seg, -jnp.inf))
        cb = jnp.einsum("blgn,bsgn->bgls", ck, bk)
        y_intra = jnp.einsum("bgls,blsgr,bsgrp->blgrp", cb, decay, xk * dtk[..., None])
        y_state = jnp.einsum("blgn,bgrpn->blgrp", ck, state) * jnp.exp(acs)[..., None]
        last = acs[:, -1]
        w_in = jnp.exp(last[:, None] - acs) * dtk
        new_state = state * jnp.exp(last)[..., None, None] + jnp.einsum(
            "bsgn,bsgr,bsgrp->bgrpn", bk, w_in, xk)
        return new_state, y_intra + y_state

    state0 = jnp.zeros((b, g, r, p, n), jnp.float32)
    _, ys = lax.scan(step, state0, (xc, dtc, bc, cc))
    return jnp.moveaxis(ys, 0, 1).reshape(b, s, h, p)

def ssm_layer(h, w_in, conv_w, conv_b, dt_bias, a_log, d_skip, norm_w, w_out):
    b, s, _ = h.shape
    z, xbc, dt = jnp.split(h @ w_in, [D_INNER, D_INNER + SSM_CONV_CH], axis=-1)
    xbc = jax.nn.silu(causal_dwconv(xbc, conv_w, conv_b))
    xs, bm, cm = jnp.split(xbc, [D_INNER, D_INNER + SSM_GROUPS * SSM_STATE], axis=-1)
    xs = xs.reshape(b, s, SSM_HEADS, SSM_HEAD_DIM).astype(jnp.float32)
    bm = bm.reshape(b, s, SSM_GROUPS, SSM_STATE).astype(jnp.float32)
    cm = cm.reshape(b, s, SSM_GROUPS, SSM_STATE).astype(jnp.float32)
    dt = jax.nn.softplus(dt.astype(jnp.float32) + dt_bias.astype(jnp.float32))
    a = -jnp.exp(a_log.astype(jnp.float32))
    y = ssd_scan(xs, dt, a, bm, cm) + d_skip.astype(jnp.float32)[:, None] * xs
    y = y.reshape(b, s, D_INNER) * jax.nn.silu(z.astype(jnp.float32))
    yg = y.reshape(b, s, SSM_GROUPS, D_INNER // SSM_GROUPS)
    yg = yg * lax.rsqrt(jnp.mean(yg * yg, axis=-1, keepdims=True) + EPS)
    y = (yg.reshape(b, s, D_INNER) * norm_w.astype(jnp.float32)).astype(h.dtype)
    return y @ w_out

def conv_ffn(h, w_in, conv_w, conv_b, w_out):
    gate, up = jnp.split(h @ w_in, [D_FF_2], axis=-1)
    gate = causal_dwconv(gate, conv_w, conv_b)
    return (jax.nn.silu(gate) * up) @ w_out

def second_inputs(seed: int = 0) -> dict:
    key = jax.random.key(seed)
    ks = jax.random.split(key, 24)
    n_even, n_odd = (DEPTH_2 + 1) // 2, DEPTH_2 // 2
    nrm = lambda k, shape, scale: jax.random.normal(k, shape, jnp.float32) * scale
    dt0 = jnp.exp(jax.random.uniform(ks[15], (n_odd, SSM_HEADS), jnp.float32,
                                     np.log(1e-3), np.log(1e-1)))
    return {
        "x": nrm(ks[0], (BATCH, SEQ, D_MODEL), 1.0),
        "norm_mix": 1.0 + nrm(ks[1], (DEPTH_2, D_MODEL), 0.05),
        "norm_ffn": 1.0 + nrm(ks[2], (DEPTH_2, D_MODEL), 0.05),
        "attn_w_in": nrm(ks[3], (n_even, D_MODEL, ATTN_PROJ), D_MODEL ** -0.5),
        "attn_w_out": nrm(ks[4], (n_even, (H_A + H_B) * HEAD_DIM, D_MODEL), ((H_A + H_B) * HEAD_DIM) ** -0.5),
        "relpos_table": nrm(ks[5], (n_even, H_A, 2 * MAX_REL_DIST + 1), 0.2),
        "q_norm_a": 1.0 + nrm(ks[6], (n_even, HEAD_DIM), 0.05),
        "k_norm_a": 1.0 + nrm(ks[7], (n_even, HEAD_DIM), 0.05),
        "q_norm_b": 1.0 + nrm(ks[8], (n_even, HEAD_DIM), 0.05),
        "k_norm_b": 1.0 + nrm(ks[9], (n_even, HEAD_DIM), 0.05),
        "sinks": nrm(ks[10], (n_even, H_B), 0.5),
        "ssm_w_in": nrm(ks[11], (n_odd, D_MODEL, SSM_PROJ), D_MODEL ** -0.5),
        "ssm_conv_w": nrm(ks[12], (n_odd, SSM_CONV, SSM_CONV_CH), SSM_CONV ** -0.5),
        "ssm_conv_b": nrm(ks[13], (n_odd, SSM_CONV_CH), 0.02),
        "ssm_dt_bias": dt0 + jnp.log(-jnp.expm1(-dt0)),
        "ssm_a_log": jnp.log(jax.random.uniform(ks[14], (n_odd, SSM_HEADS), jnp.float32, 1.0, 16.0)),
        "ssm_d": 1.0 + nrm(ks[16], (n_odd, SSM_HEADS), 0.1),
        "ssm_norm": 1.0 + nrm(ks[17], (n_odd, D_INNER), 0.05),
        "ssm_w_out": nrm(ks[18], (n_odd, D_INNER, D_MODEL), D_INNER ** -0.5),
        "ffn_w_in": nrm(ks[19], (DEPTH_2, D_MODEL, 2 * D_FF_2), D_MODEL ** -0.5),
        "ffn_conv_w": nrm(ks[20], (DEPTH_2, FFN_CONV, D_FF_2), FFN_CONV ** -0.5),
        "ffn_conv_b": nrm(ks[21], (DEPTH_2, D_FF_2), 0.02),
        "ffn_w_out": nrm(ks[22], (DEPTH_2, D_FF_2, D_MODEL), D_FF_2 ** -0.5),
    }

def second_block(x, norm_mix, norm_ffn, attn_w_in, attn_w_out, relpos_table, q_norm_a, k_norm_a,
              q_norm_b, k_norm_b, sinks, ssm_w_in, ssm_conv_w, ssm_conv_b, ssm_dt_bias, ssm_a_log,
              ssm_d, ssm_norm, ssm_w_out, ffn_w_in, ffn_conv_w, ffn_conv_b, ffn_w_out):
    for layer in range(DEPTH_2):
        i = layer // 2
        h = rmsnorm(x, norm_mix[layer])
        if layer % 2 == 0:
            mix = attn_layer(h, attn_w_in[i], attn_w_out[i], relpos_table[i], q_norm_a[i],
                             k_norm_a[i], q_norm_b[i], k_norm_b[i], sinks[i])
        else:
            mix = ssm_layer(h, ssm_w_in[i], ssm_conv_w[i], ssm_conv_b[i], ssm_dt_bias[i],
                            ssm_a_log[i], ssm_d[i], ssm_norm[i], ssm_w_out[i])
        x = x + mix
        h = rmsnorm(x, norm_ffn[layer])
        x = x + conv_ffn(h, ffn_w_in[layer], ffn_conv_w[layer], ffn_conv_b[layer], ffn_w_out[layer])
    return x


def setup_inputs(seed=0):
    out = dict(first_inputs(seed))
    for name, value in second_inputs(seed + 1).items():
        if name != "x":
            out[name + "_2"] = value
    return out


def reference(
    x, mem, g_mix, g_mem, w_in, conv_w, w_conv_out, w_sb_out, q_norm_g, k_norm_g, w_mem_kv,
    w_x_out, w_out, g_mlp, w_up, w_down, norm_mix_2, norm_ffn_2, attn_w_in_2, attn_w_out_2,
    relpos_table_2, q_norm_a_2, k_norm_a_2, q_norm_b_2, k_norm_b_2, sinks_2, ssm_w_in_2,
    ssm_conv_w_2, ssm_conv_b_2, ssm_dt_bias_2, ssm_a_log_2, ssm_d_2, ssm_norm_2, ssm_w_out_2,
    ffn_w_in_2, ffn_conv_w_2, ffn_conv_b_2, ffn_w_out_2,
):
    x = first_block(
        x, mem, g_mix, g_mem, w_in, conv_w, w_conv_out, w_sb_out, q_norm_g, k_norm_g, w_mem_kv,
        w_x_out, w_out, g_mlp, w_up, w_down,
    )
    return second_block(
        x, norm_mix_2, norm_ffn_2, attn_w_in_2, attn_w_out_2, relpos_table_2, q_norm_a_2,
        k_norm_a_2, q_norm_b_2, k_norm_b_2, sinks_2, ssm_w_in_2, ssm_conv_w_2, ssm_conv_b_2,
        ssm_dt_bias_2, ssm_a_log_2, ssm_d_2, ssm_norm_2, ssm_w_out_2, ffn_w_in_2, ffn_conv_w_2,
        ffn_conv_b_2, ffn_w_out_2,
    )


_drawn_inputs = setup_inputs


def setup_inputs(seed=0):
    import zlib

    import numpy as np

    out = dict(_drawn_inputs(seed))
    spreads = {}
    factors = {'g_mem': 8.0,
     'q_norm_g': 8.0,
     'k_norm_g': 8.0,
     'g_mlp': 2.67,
     'relpos_table_2': 114.864,
     'q_norm_a_2': 26.733,
     'k_norm_a_2': 25.725,
     'q_norm_b_2': 25.92,
     'k_norm_b_2': 27.817,
     'sinks_2': 7.637,
     'ssm_conv_b_2': 20.656,
     'ffn_conv_b_2': 32.77,
     'norm_ffn_2': 8.0,
     'ssm_a_log_2': 25.368,
     'ssm_d_2': 26.99,
     'ssm_norm_2': 43.091,
     'ssm_dt_bias_2': 6.883}
    for name, (base, spread) in spreads.items():
        noise = np.random.default_rng([zlib.crc32(name.encode()), seed]).standard_normal(out[name].shape)
        drawn = base * np.exp(spread * noise) if base else spread * noise
        out[name] = __import__('jax').numpy.asarray(drawn.astype(out[name].dtype))
    for name, factor in factors.items():
        out[name] = (out[name] * factor).astype(out[name].dtype)
    return out
```

```python
from contextlib import ExitStack

import concourse.bass as bass
from concourse import mybir

F32 = mybir.dt.float32
F32R = mybir.dt.float32r
ALU = mybir.AluOpType
ACT = mybir.ActivationFunctionType
AX = mybir.AxisListType

P = 128
SEQ = 512
D = 1024
MEM = 256
KD = D // P
TB = SEQ // P
EPS = 1e-6
BIG = 1e30

SB_HEADS, SB_DIM = 16, 64
X_HEADS, X_DIM = 4, 256
FF1 = 4096
A_HEADS = B_HEADS = 8
B_KV = 2
HD = 64
SSM_G, SSM_N, SSM_HEADS, SSM_P = 4, 128, 32, 64
SSM_IN = SSM_HEADS * SSM_P
HPG = SSM_HEADS // SSM_G
TPG = HPG * SSM_P // P
FF2 = 2816
KF2 = FF2 // P
UNIT_K = 8
RAW, SPLIT = 3, 3
MLP_HALF = 16

PAR = {}
_at = 0
for _name, _n in (("g_mix", 8), ("g_mem", 8), ("conv_w", 24), ("q_norm_g", 2), ("k_norm_g", 2),
                  ("g_mlp", 8), ("norm_mix_2", 16), ("norm_ffn_2", 16),
                  ("ffn_conv_w_2", 2 * 3 * KF2), ("ffn_conv_b_2", 2 * KF2),
                  ("ssm_conv_w_2", 4 * 24), ("ssm_conv_b_2", 24), ("ssm_norm_2", 16),
                  ("ssm_d_2", 16), ("q_norm_a_2", 1), ("k_norm_a_2", 1), ("q_norm_b_2", 1),
                  ("k_norm_b_2", 1), ("sinks_2", B_HEADS), ("dt_bias", 1), ("a_log", 1)):
    PAR[_name] = _at
    _at += _n
NPAR = _at

CON = {}
_at = 0
for _name, _n in (("ident", P), ("neg_later", P), ("neg_ones", P), ("past", P), ("neg_future", P),
                  ("ones", P), ("head_ones", P), ("causal", P), ("dist_b", 2 * P), ("flip", P), ("eps", 1)):
    CON[_name] = _at
    _at += _n
NCON = _at
STRIP_E = 639


class Lane:

    def __init__(self, eng, step):
        self.eng, self.step, self.count, self.open = eng, step, {}, {}

    def did(self, ins, sem=None):
        s = sem or self.step
        ins.then_inc(s, 1)
        self.count[s.name] = self.count.get(s.name, 0) + 1
        self.open[s.name] = (s, self.count[s.name])

    def sync(self):
        for s, v in self.open.values():
            self.eng.wait_ge(s, v)
        self.open = {}


def two_block_kernel(nc, dram, out):
    ctx = ExitStack()
    with ctx:
        def sem(name):
            return ctx.enter_context(nc.semaphore(name))

        base = (nc.sbuf_base + 31) // 32 * 32
        room = nc.sbuf_usable_end - base
        arena = ctx.enter_context(nc.sbuf_tensor("arena", [P, (nc.sbuf_bytes_remaining - 64) // 4], F32))
        cursor = [base]

        def at(name, offset, shape, dt=F32):
            return nc.alloc_sbuf_tensor_at(name, [P] + list(shape), dt, offset=offset)

        def size(shape):
            n = 4
            for s in shape:
                n *= s
            return (n + 31) // 32 * 32

        def place(name, shape, dt=F32):
            t = at(name, cursor[0], shape, dt)
            cursor[0] += size(shape)
            return t

        par = place("par", [NPAR])
        con = place("con", [NCON])
        raw = [place(f"raw{i}", [UNIT_K, P]) for i in range(RAW)]
        w_hi = [place(f"w_hi{i}", [UNIT_K, P], F32R) for i in range(SPLIT)]
        w_lo = [place(f"w_lo{i}", [UNIT_K, P], F32R) for i in range(SPLIT)]
        x = place("x", [KD, SEQ])
        rstd = place("rstd", [SEQ])
        TILE = 2048
        a_off = cursor[0]
        b_off = a_off + 2 * KD * TILE
        c_off = b_off + 2 * KD * TILE
        d_off = c_off + 2 * KD * TILE
        t_off = d_off + 2 * KD * TILE
        cursor[0] = t_off
        opA = [at("opA_hi", a_off, [KD, SEQ], F32R), at("opA_lo", a_off + KD * TILE, [KD, SEQ], F32R)]
        opB = [at("opB_hi", b_off, [KD, SEQ], F32R), at("opB_lo", b_off + KD * TILE, [KD, SEQ], F32R)]
        opC = [at("opC_hi", c_off, [KD, SEQ], F32R), at("opC_lo", c_off + KD * TILE, [KD, SEQ], F32R)]
        sq = [place(f"sq{i}", [SEQ]) for i in range(2)]
        ss = place("ss", [SEQ])
        src = place("src", [SEQ])
        pad = place("pad", [SEQ + 4])
        tmp = place("tmp", [SEQ])
        tmp2 = place("tmp2", [SEQ])
        sig = place("sig", [SEQ])
        small = place("small", [64])
        dt_acsT = place("dt_acsT", [SEQ])
        dt_last = place("dt_last", [TB * SSM_HEADS])
        dt_tok = place("dt_tok", [3, TB, SSM_HEADS])
        e_last = place("e_last", [TB, SSM_HEADS])
        assert cursor[0] <= nc.sbuf_usable_end

        merged = at("merged", d_off + KD * TILE, [KD, SEQ])
        v_tok = at("v_tok", d_off, [TB, D])
        qT = at("qT", c_off, [KD, SEQ])
        kT = at("kT", c_off + KD * TILE, [KD, SEQ])
        SBW = 1280
        sb_e = at("sb_e", b_off, [SBW])
        sb_sp = [at(f"sb_sp{i}", b_off + (1 + i) * 5120, [SBW]) for i in range(2)]
        sb_a = [at(f"sb_a{i}", b_off + (3 + i) * 5120, [SBW]) for i in range(2)]
        opM = [at("opM_hi", b_off, [KD, MEM], F32R), at("opM_lo", b_off + KD * TILE // 2, [KD, MEM], F32R)]
        memx = at("memx", b_off + KD * TILE, [KD, MEM])
        xk = at("xk", d_off, [KD, MEM])
        xv_tok = at("xv_tok", d_off + KD * TILE // 2, [MEM // P, D])
        xq = at("xq", c_off, [KD, SEQ])
        x_p = [at(f"x_p{i}", c_off + KD * TILE + i * 4096, [TB, MEM]) for i in range(2)]
        x_pT = at("x_pT", c_off + KD * TILE + 8192, [MEM // P, SEQ])
        hid1 = [at("hid1_hi", b_off, [MLP_HALF, SEQ], F32R), at("hid1_lo", c_off, [MLP_HALF, SEQ], F32R)]
        qk2 = at("qk2", c_off, [12, SEQ])
        kb2 = at("kb2", c_off + 12 * TILE, [B_KV, SEQ])
        va_tok = at("va_tok", d_off, [TB, A_HEADS * HD])
        vb_tok = at("vb_tok", d_off + TB * TILE, [TB, B_KV * HD])
        vb_end = d_off + TB * TILE + TB * TILE // 4
        strip = at("strip", d_off + 16384, [A_HEADS, SEQ])
        at_s = [at(f"at_s{i}", vb_end + i * TILE, [SEQ]) for i in range(2)]
        at_pT = at("at_pT", c_off + 14 * TILE, [2, SEQ])
        hid2 = [at("hid2_hi", b_off, [KF2, SEQ], F32R), at("hid2_lo", b_off + KF2 * TILE, [KF2, SEQ], F32R)]
        opY = [at("opY_hi", b_off, [2 * KD, SEQ], F32R), at("opY_lo", c_off, [2 * KD, SEQ], F32R)]
        xs = at("xs", d_off, [TPG, SEQ])
        x_tok = at("x_tok", d_off + 8192, [TB, TPG * P])
        bT = at("bT", d_off + 16384, [SEQ])
        cT = at("cT", d_off + 18432, [SEQ])
        b_tok = at("b_tok", d_off + 20480, [TB, SSM_N])
        state = at("state", d_off + 22528, [TB - 1, TPG * P])
        cbm = at("cbm", d_off + 28672, [TB, P])
        xw = at("xw", d_off + 30720, [TPG * P])
        dt_dtT = at("dt_dtT", d_off + 22528, [SEQ])
        dt_wT = at("dt_wT", d_off + 24576, [SEQ])
        dt_e = at("dt_e", d_off + 26624, [SEQ])
        dt_d = at("dt_d", d_off + 28672, [SEQ])
        dt_m = at("dt_m", d_off + 30720, [SEQ])
        ssm_G, ssm_E, ssm_S = [tmp, tmp2], [sq[0], sq[1]], [sig, src]
        rstd_m = at("rstd_m", b_off + 24 * 1024, [MEM])

        def col(name, i=0, n=1):
            return par[:, PAR[name] + i:PAR[name] + i + n]

        def const(name, n=P):
            return con[:, CON[name]:CON[name] + n]

        ident = const("ident")
        bank = [ctx.enter_context(nc.psum_tensor(f"bank{i}", [P, SEQ], F32)) for i in range(8)]

        units, tiles, stage = [], [], {}

        def add_tile(w, c0, k0, kt, width=P):
            first = len(units)
            for k in range(0, kt, UNIT_K):
                n = min(UNIT_K, kt - k)
                rows = w[(k0 + k) * P:(k0 + k + n) * P, c0:c0 + width]
                units.append((rows.rearrange("(k p) c -> p k c", p=P), n, width))
            tiles.append((first, len(units) - first, kt, width))

        def begin(name):
            stage[name] = len(tiles)

        w_in = dram["w_in"]
        begin("conv")
        for i in range(KD):
            for part in (0, 2, 1):
                add_tile(w_in, part * D + i * P, 0, KD)

        def gated(name, gate, w_branch):
            begin(name)
            for i in range(KD):
                add_tile(w_in, (7 + gate) * D + i * P, 0, KD)
                add_tile(w_branch, i * P, 0, KD)

        gated("conv_out", 0, dram["w_conv_out"])
        begin("qkv")
        for part in (3, 4, 5):
            for i in range(KD):
                add_tile(w_in, part * D + i * P, 0, KD)
        gated("sb_out", 1, dram["w_sb_out"])
        begin("mem_kv")
        for i in range(2 * KD):
            add_tile(dram["w_mem_kv"], i * P, 0, KD)
        begin("xq")
        for i in range(KD):
            add_tile(w_in, 6 * D + i * P, 0, KD)
        gated("x_out", 2, dram["w_x_out"])
        begin("w_out")
        for i in range(KD):
            add_tile(dram["w_out"], i * P, 0, KD)
        for half in range(FF1 // P // MLP_HALF):
            begin(f"up{half}")
            for i in range(MLP_HALF):
                add_tile(dram["w_up"], (half * MLP_HALF + i) * P, 0, KD)
            begin(f"down{half}")
            for i in range(KD):
                add_tile(dram["w_down"], i * P, half * MLP_HALF, MLP_HALF)
        begin("attn_in")
        AW = A_HEADS * HD // P
        for c in list(range(0, 2 * AW)) + list(range(3 * AW, 4 * AW)) + [4 * AW] + list(range(2 * AW, 3 * AW)) + [4 * AW + 1]:
            add_tile(dram["attn_w_in_2"], c * P, 0, KD)
        begin("attn_out")
        for i in range(KD):
            add_tile(dram["attn_w_out_2"], i * P, 0, KD)

        def ffn_plan(layer):
            w = dram["ffn_w_in_2"]
            begin(f"ffn_in{layer}")
            for i in range(KF2):
                add_tile(w[layer], i * P, 0, KD)
                add_tile(w[layer], FF2 + i * P, 0, KD)
            begin(f"ffn_out{layer}")
            for i in range(KD):
                add_tile(dram["ffn_w_out_2"][layer], i * P, 0, KF2)

        ffn_plan(0)
        begin("dt")
        ssm_w = dram["ssm_w_in_2"]
        add_tile(ssm_w, 2 * SSM_IN + 2 * SSM_G * SSM_N, 0, KD, SSM_HEADS)
        for g in range(SSM_G):
            begin(f"ssm_bcx{g}")
            add_tile(ssm_w, 2 * SSM_IN + g * P, 0, KD)
            add_tile(ssm_w, 2 * SSM_IN + (SSM_G + g) * P, 0, KD)
            for i in range(TPG):
                add_tile(ssm_w, SSM_IN + (g * TPG + i) * P, 0, KD)
            begin(f"ssm_z{g}")
            for i in range(TPG):
                add_tile(ssm_w, (g * TPG + i) * P, 0, KD)
        begin("ssm_out")
        for i in range(KD):
            add_tile(dram["ssm_w_out_2"], i * P, 0, 2 * KD)
        ffn_plan(1)
        begin("end")
        NU = len(units)

        def last_unit(t):
            return tiles[t][0] + tiles[t][1] - 1

        params_in = sem("params_in")
        x_in = sem("x_in")
        mem_in = sem("mem_in")
        strip_in = sem("strip_in")
        strip_zone_free = sem("strip_zone_free")
        strip_flipped, strip_turned = sem("strip_flipped"), sem("strip_turned")
        unit_loaded = [sem(f"unit_loaded{i}") for i in range(RAW)]
        hi_ready = sem("hi_ready")
        lo_ready = sem("lo_ready")
        unit_used = sem("unit_used")
        pe_step, dve_step, act_step = sem("pe_step"), sem("dve_step"), sem("act_step")
        op_hi_done = sem("op_hi_done")
        op_ready = sem("op_ready")
        src_ready = sem("src_ready")
        sq_in, sq_ready, sq_used, ss_added, ss_summed = sem("sq_in"), sem("sq_ready"), sem("sq_used"), sem("ss_added"), sem("ss_summed")
        r0_ready, rstd_ready = sem("r0_ready"), sem("rstd_ready")
        sig_in, sig_ready = sem("sig_in"), sem("sig_ready")
        vT_ready, v_turned, v_tok_ready = sem("vT_ready"), sem("v_turned"), sem("v_tok_ready")
        sb_scored, sb_abs_done, sb_exp_ready, sb_sp_ready = sem("sb_scored"), sem("sb_abs_done"), sem("sb_exp_ready"), sem("sb_sp_ready")
        sb_summed, sb_a_ready, sb_pv_done, sb_o_read = sem("sb_summed"), sem("sb_a_ready"), sem("sb_pv_done"), sem("sb_o_read")
        xk_ready, xq_ready = sem("xk_ready"), sem("xq_ready")
        x_scored, x_max_ready, x_exp_ready, x_p_ready = sem("x_scored"), sem("x_max_ready"), sem("x_exp_ready"), sem("x_p_ready")
        x_turned, x_pT_ready, x_pv_done, x_o_read = sem("x_turned"), sem("x_pT_ready"), sem("x_pv_done"), sem("x_o_read")
        at_q_ready = sem("at_q_ready")
        at_scored, at_max_ready, at_exp_ready, at_p_ready = sem("at_scored"), sem("at_max_ready"), sem("at_exp_ready"), sem("at_p_ready")
        at_turned, at_pT_ready, at_pv_done, at_o_read = sem("at_turned"), sem("at_pT_ready"), sem("at_pv_done"), sem("at_o_read")
        dt_in, dt_exp, dt_ln_in, dt_ln, dt_acs, dt_w = sem("dt_in"), sem("dt_exp"), sem("dt_ln_in"), sem("dt_ln"), sem("dt_acs"), sem("dt_w")
        dt_ready, dt_turned, dt_elast = sem("dt_ready"), sem("dt_turned"), sem("dt_elast")
        xs_ready, xs_turned, x_tok_ready = sem("xs_ready"), sem("xs_turned"), sem("x_tok_ready")
        cb_done, xw_ready, upd_done, state_ready, cb_ready = sem("cb_done"), sem("xw_ready"), sem("upd_done"), sem("state_ready"), sem("cb_ready")
        row_done, dec_in, dec_exp, g_ready, y_done, y_read = sem("row_done"), sem("dec_in"), sem("dec_exp"), sem("g_ready"), sem("y_done"), sem("y_read")
        dt_tok_ready, dt_elast_in = sem("dt_tok_ready"), sem("dt_elast_in")
        out_ready, stored = sem("out_ready"), sem("stored")

        generation, made = {}, [0]

        def operand(name, n):
            generation[name] = made[0]
            made[0] += n

        for name, n in (("x1", KD), ("conv", KD), ("sb", KD), ("mem", KD), ("xo", KD), ("merged", KD), ("x2", KD),
                        ("hid1_0", MLP_HALF), ("hid1_1", MLP_HALF), ("x3", KD), ("attn", KD), ("x4", KD),
                        ("ffn0", KF2), ("x5", KD), ("ssm", 2 * KD), ("x6", KD), ("ffn1", KF2)):
            operand(name, n)

        SB_OFF = (0, 512, 1024, 896)
        SB_BANK = ((0, 0), (1, 0), (2, 0), (1, 384))

        block = ctx.enter_context(nc.Block())

        @block.sync
        def _(sp):
            sp.dma_start(par[:, :], dram["par"]).then_inc(params_in, 16)
            sp.dma_start(con[:, :], dram["con"]).then_inc(params_in, 16)
            for k in range(0, KD, 2):
                sp.dma_start(x[:, k:k + 2, :], dram["xT"][:, k:k + 2, :]).then_inc(x_in, 16)

            for u, (rows, n, width) in enumerate(units):
                if u >= RAW:
                    sp.wait_ge(lo_ready, u - RAW + 1)
                sp.dma_start(raw[u % RAW][:, 0:n, 0:width], rows).then_inc(unit_loaded[u % RAW], 16)
                if u == tiles[stage["sb_out"]][0] + 4:
                    sp.wait_ge(sb_a_ready, 3 * SB_HEADS)
                    sp.wait_ge(sb_pv_done, SB_HEADS)
                    sp.dma_start(memx[:, :, :], dram["memT"]).then_inc(mem_in, 16)
                if u == tiles[stage["up0"]][0] + 4:
                    E = dram["rel"]
                    sp.wait_ge(strip_zone_free, 1)
                    sp.dma_start(strip[:, :, :], bass.AP(E.tensor, 0, [[1, P], [STRIP_E, A_HEADS], [1, SEQ]])).then_inc(strip_in, 16)
            for k in range(KD):
                sp.wait_ge(out_ready, k + 1)
                sp.dma_start(out[:, k, :], x[:, k, :]).then_inc(stored, 16)
            sp.wait_ge(stored, 16 * KD)

        @block.tensor
        def _(pe):
            lane = Lane(pe, pe_step)
            seen = {"op": 0, "sum": 0}

            def tile(t, op, gen, n=SEQ):
                u0, nu, kt, width = tiles[t]
                dst = bank[t % 4][0:width, 0:n]
                for j in range(nu):
                    u = u0 + j
                    pe.wait_ge(lo_ready, u + 1)
                    for k in range(units[u][1]):
                        kk = j * UNIT_K + k
                        need = generation[gen] + kk + 1
                        if need > seen["op"]:
                            pe.wait_ge(op_ready, need)
                            seen["op"] = need
                        wh, wl = w_hi[u % SPLIT][:, k, 0:width], w_lo[u % SPLIT][:, k, 0:width]
                        pe.matmul(dst, wh, op[0][:, kk, 0:n], start=(kk == 0), stop=False)
                        pe.matmul(dst, wh, op[1][:, kk, 0:n], start=False, stop=False)
                        mm = pe.matmul(dst, wl, op[0][:, kk, 0:n], start=False, stop=(kk == kt - 1))
                    mm.then_inc(unit_used, 1)

            def norm_sum(n=SEQ, ones="ones"):
                i = seen["sum"]
                seen["sum"] += 1
                pe.wait_ge(ss_added, i + 1)
                if i:
                    pe.wait_ge(rstd_ready, i)
                pe.matmul(bank[4][:, 0:n], const(ones), ss[:, 0:n], start=True, stop=True).then_inc(ss_summed, 1)

            def turn(srcs, dst, ready, ready_n, free, free_n, done):
                pe.wait_ge(ready, ready_n)
                if free_n > 0:
                    pe.wait_ge(free, free_n)
                for i, s in enumerate(srcs):
                    mm = pe.transpose(dst[:, i * P:(i + 1) * P], s, ident)
                mm.then_inc(done, 1)

            pe.wait_ge(params_in, 32)
            t = stage["conv"]
            for i in range(3 * KD):
                tile(t + i, opA, "x1")
                if i == 0:
                    norm_sum()
            t = stage["conv_out"]
            for i in range(KD):
                tile(t + 2 * i, opA, "x1")
                tile(t + 2 * i + 1, opB, "conv")
            t = stage["qkv"]
            vi = 0

            def turn_v(n, blocks):
                vt = tmp if n % 2 == 0 else tmp2
                turn([vt[:, b * P:(b + 1) * P] for b in range(blocks)], bank[5 + n % 2], vT_ready, n + 1, v_tok_ready, n - 1, v_turned)

            for i in range(3 * KD):
                tile(t + i, opA, "x1")
                if i > 2 * KD:
                    turn_v(vi, TB)
                    vi += 1
            turn_v(vi, TB)
            vi += 1

            def sb_scores(h):
                r, j, s = HD * (h % 2), h // 2, 4 * (h % 2)
                if h >= 2:
                    pe.wait_ge(sb_a_ready, 3 * (h - 1))
                for kb in range(TB):
                    b, c = SB_BANK[kb]
                    mm = pe.matmul(bank[s + b][:, c:c + SEQ - kb * P], kT[r:r + HD, j, kb * P:(kb + 1) * P],
                                   qT[r:r + HD, j, kb * P:SEQ], start=(c == 0), stop=False, skip_group_check=True)
                mm.then_inc(sb_scored, 1)

            def sb_sums(h):
                s = 4 * (h % 2)
                pe.wait_ge(sb_sp_ready, h + 1)
                sp_ = sb_sp[h % 2]
                for kb in range(TB):
                    b, c = SB_BANK[kb]
                    n = SEQ - kb * P
                    dst = bank[s + b]
                    pe.matmul(dst[:, c:c + n], const("neg_later"), sp_[:, SB_OFF[kb]:SB_OFF[kb] + n], start=False, stop=False, skip_group_check=True)
                    for later in range(kb + 1, TB):
                        m = SEQ - later * P
                        pe.matmul(dst[:, c + n - m:c + n], const("neg_ones"), sp_[:, SB_OFF[later]:SB_OFF[later] + m], start=False, stop=False, skip_group_check=True)
                    mm = pe.matmul(dst[:, c:c + P], ident, const("neg_future"), start=False, stop=True, skip_group_check=True)
                mm.then_inc(sb_summed, 1)

            def sb_values(h):
                pe.wait_ge(sb_a_ready, 3 * (h + 1))
                if h >= 2:
                    pe.wait_ge(sb_o_read, h - 1)
                dst = bank[3 + 4 * (h % 2)]
                for kb in range(TB):
                    n = SEQ - kb * P
                    mm = pe.matmul(dst[0:HD, kb * P:SEQ], v_tok[:, kb, h * HD:(h + 1) * HD], sb_a[h % 2][:, SB_OFF[kb]:SB_OFF[kb] + n],
                                   start=(kb == 0), stop=(kb == TB - 1))
                mm.then_inc(sb_pv_done, 1)

            pe.wait_ge(v_tok_ready, vi)
            pe.wait_ge(vT_ready, vi)
            pe.wait_ge(rstd_ready, seen["sum"])
            sb_scores(0)
            for h in range(SB_HEADS):
                if h + 1 < SB_HEADS:
                    sb_scores(h + 1)
                sb_sums(h)
                if h >= 1:
                    sb_values(h - 1)
            sb_values(SB_HEADS - 1)
            pe.wait_ge(sb_o_read, SB_HEADS)
            t = stage["sb_out"]
            for i in range(KD):
                tile(t + 2 * i, opA, "x1")
                tile(t + 2 * i + 1, opC, "sb")
            t = stage["mem_kv"]
            for i in range(2 * KD):
                tile(t + i, opM, "mem", MEM)
                if i == 0 or (i <= KD and i % 2 == 0):
                    norm_sum(MEM)
                if i > KD:
                    turn_v(vi, MEM // P)
                    vi += 1
            turn_v(vi, MEM // P)
            vi += 1
            t = stage["xq"]
            for i in range(KD):
                tile(t + i, opA, "x1")
                if i and i % 2 == 0:
                    norm_sum()
            norm_sum()
            pe.wait_ge(xq_ready, KD)
            pe.wait_ge(v_tok_ready, vi)

            def x_scores(h):
                if h >= 1:
                    pe.wait_ge(x_exp_ready, TB * h)
                for qb in range(TB):
                    for d in range(2):
                        mm = pe.matmul(bank[qb // 2][:, (qb % 2) * MEM:(qb % 2 + 1) * MEM], xq[:, 2 * h + d, qb * P:(qb + 1) * P],
                                       xk[:, 2 * h + d, :], start=(d == 0), stop=(d == 1))
                mm.then_inc(x_scored, 1)

            x_scores(0)
            for h in range(X_HEADS):
                if h + 1 < X_HEADS:
                    x_scores(h + 1)
                pe.wait_ge(x_p_ready, h + 1)
                if h >= 1:
                    pe.wait_ge(x_pT_ready, 2 * h)
                for kb in range(2):
                    for qb in range(TB):
                        mm = pe.transpose(bank[2 + kb][:, qb * P:(qb + 1) * P], x_p[h % 2][:, qb, kb * P:(kb + 1) * P], ident)
                    mm.then_inc(x_turned, 1)
                pe.wait_ge(x_pT_ready, 2 * h + 2)
                for d in range(2):
                    n = 2 * h + d
                    if n >= 2:
                        pe.wait_ge(x_o_read, n - 1)
                    for kb in range(2):
                        mm = pe.matmul(bank[5 + d][:, :], xv_tok[:, kb, n * P:(n + 1) * P], x_pT[:, kb, :], start=(kb == 0), stop=(kb == 1))
                    mm.then_inc(x_pv_done, 1)
            t = stage["x_out"]
            for i in range(KD):
                tile(t + 2 * i, opA, "x1")
                tile(t + 2 * i + 1, opB, "xo")
            t = stage["w_out"]
            for i in range(KD):
                tile(t + i, opC, "merged")
            for half in range(FF1 // P // MLP_HALF):
                t = stage[f"up{half}"]
                for i in range(MLP_HALF):
                    tile(t + i, opA, "x2")
                    if half == 0 and i == 0:
                        norm_sum()
                if half == 0:
                    pe.wait_ge(strip_in, 16)
                    for h in range(A_HEADS):
                        if h >= 2:
                            pe.wait_ge(strip_turned, h - 1)
                        pe.matmul(bank[5 + h % 2][:, :], const("flip"), strip[:, h, :], start=True, stop=True).then_inc(strip_flipped, 1)
                t = stage[f"down{half}"]
                for i in range(KD):
                    tile(t + i, hid1, f"hid1_{half}")
            t = stage["attn_in"]
            order = [0] * (3 * AW + 1) + [1] * (AW + 1)
            for i, is_v in enumerate(order):
                tile(t + i, opA, "x3")
                if i == 0:
                    norm_sum()
                if 1 <= i <= 3 * AW + 1:
                    norm_sum(SEQ, "head_ones")
                if i > 3 * AW + 1:
                    turn_v(vi, TB)
                    vi += 1
            turn_v(vi, TB)
            vi += 1
            pe.wait_ge(at_q_ready, 3 * AW + 1)
            pe.wait_ge(v_tok_ready, vi)
            pe.wait_ge(vT_ready, vi)

            items = [(h, qb) for h in range(A_HEADS + B_HEADS) for qb in range(TB)]

            def keys_of(h, qb):
                return (0, qb + 1) if h < A_HEADS else (max(0, qb - 1), min(2, qb + 1))

            def at_scores(n):
                h, qb = items[n]
                k0, nk = keys_of(h, qb)
                r = HD * (h % 2)
                if n >= 2:
                    pe.wait_ge(at_max_ready, n - 1)
                if h < A_HEADS:
                    q, k = qk2[r:r + HD, h // 2, :], qk2[r:r + HD, AW + h // 2, :]
                else:
                    q, k = qk2[r:r + HD, 2 * AW + (h - A_HEADS) // 2, :], kb2[r:r + HD, (h - A_HEADS) // (B_HEADS // B_KV), :]
                pe.matmul(bank[n % 2][:, 0:nk * P], q[:, qb * P:(qb + 1) * P], k[:, k0 * P:(k0 + nk) * P], start=True, stop=True).then_inc(at_scored, 1)

            def at_turn(n):
                h, qb = items[n]
                _, nk = keys_of(h, qb)
                pe.wait_ge(at_p_ready, n + 1)
                if n >= 2:
                    pe.wait_ge(at_pT_ready, n - 1)
                for i in range(nk):
                    mm = pe.transpose(bank[2 + n % 2][:, i * P:(i + 1) * P], at_s[n % 2][:, i * P:(i + 1) * P], ident)
                mm.then_inc(at_turned, 1)

            def at_values(n):
                h, qb = items[n]
                k0, nk = keys_of(h, qb)
                pe.wait_ge(at_pT_ready, n + 1)
                if qb == 0 and h >= 2:
                    pe.wait_ge(at_o_read, h - 1)
                for i in range(nk):
                    if h < A_HEADS:
                        v = va_tok[:, k0 + i, h * HD:(h + 1) * HD]
                    else:
                        g = (h - A_HEADS) // (B_HEADS // B_KV)
                        v = vb_tok[:, k0 + i, g * HD:(g + 1) * HD]
                    mm = pe.matmul(bank[5 + h % 2][0:HD, qb * P:(qb + 1) * P], v, at_pT[:, n % 2, i * P:(i + 1) * P], start=(i == 0), stop=(i == nk - 1))
                mm.then_inc(at_pv_done, 1)

            at_scores(0)
            for n in range(len(items)):
                if n + 1 < len(items):
                    at_scores(n + 1)
                at_turn(n)
                if n >= 1:
                    at_values(n - 1)
            at_values(len(items) - 1)
            pe.wait_ge(at_pT_ready, len(items))
            t = stage["attn_out"]
            for i in range(KD):
                tile(t + i, opB, "attn")

            def ffn(layer, gen_in, gen_mid):
                t = stage[f"ffn_in{layer}"]
                for i in range(2 * KF2):
                    tile(t + i, opA, gen_in)
                    if i == 0:
                        norm_sum()
                t = stage[f"ffn_out{layer}"]
                for i in range(KD):
                    tile(t + i, hid2, gen_mid)

            ffn(0, "x4", "ffn0")
            tile(stage["dt"], opA, "x5")
            norm_sum()
            for g in range(SSM_G):
                t = stage[f"ssm_bcx{g}"]
                bank_x = g * 5

                def turn_x(j):
                    n = bank_x + j
                    s = bT if j == 0 else xs[:, j - 1, :]
                    pe.wait_ge(xs_ready, g * 6 + (1 if j == 0 else j + 2))
                    if n >= 2:
                        pe.wait_ge(x_tok_ready, n - 1)
                    for c in range(TB):
                        mm = pe.transpose(bank[5 + n % 2][:, c * P:(c + 1) * P], s[:, c * P:(c + 1) * P], ident)
                    mm.then_inc(xs_turned, 1)

                for j in range(2 + TPG):
                    tile(t + j, opA, "x5")
                    if j == 0 and g:
                        norm_sum()
                    if j == 1:
                        turn_x(0)
                    if j >= 3:
                        turn_x(j - 2)
                turn_x(TPG)
                pe.wait_ge(xs_ready, g * 6 + 6)
                pe.wait_ge(x_tok_ready, bank_x + 5)
                if g == 0:
                    pe.wait_ge(dt_ready, 1)
                    for c in range(TB):
                        for j, row in enumerate((dt_acsT, dt_dtT, dt_wT)):
                            o = (j * TB + c) * SSM_HEADS
                            mm = pe.transpose(bank[1][:, o:o + SSM_HEADS], row[0:SSM_HEADS, c * P:(c + 1) * P], ident[0:SSM_HEADS, 0:SSM_HEADS])
                    mm.then_inc(dt_turned, 1)
                    pe.matmul(bank[2][:, 0:TB * SSM_HEADS], const("ones")[0:SSM_HEADS, :], dt_last[0:SSM_HEADS, :], start=True, stop=True).then_inc(dt_elast, 1)
                    pe.wait_ge(dt_tok_ready, 2)
                for c in range(TB):
                    mm = pe.matmul(bank[0][:, c * P:(c + 1) * P], bT[:, c * P:(c + 1) * P], cT[:, c * P:(c + 1) * P], start=True, stop=True)
                mm.then_inc(cb_done, 1)
                for c in range(TB - 1):
                    pe.wait_ge(xw_ready, g * (TB - 1) + c + 1)
                    if c >= 2:
                        pe.wait_ge(state_ready, g * (TB - 1) + c - 1)
                    pe.matmul(bank[1 + c % 2][:, :], b_tok[:, c, :], xw[:, :], start=True, stop=True).then_inc(upd_done, 1)

                def head_row(h):
                    n = g * HPG + h
                    if n >= 2:
                        pe.wait_ge(g_ready, n - 1)
                    sel = ident[0:SSM_HEADS, n:n + 1].to_broadcast([SSM_HEADS, P])
                    pe.matmul(bank[4 if n % 2 else 3][:, :], sel, dt_acsT[0:SSM_HEADS, :], start=True, stop=True).then_inc(row_done, 1)

                def head_out(h):
                    n = g * HPG + h
                    pe.wait_ge(g_ready, n + 1)
                    pe.wait_ge(state_ready, (g + 1) * (TB - 1))
                    if n >= 2:
                        pe.wait_ge(y_read, n - 1)
                    for c in range(TB):
                        dst = bank[5 + n % 2][0:SSM_P, c * P:(c + 1) * P]
                        mm = pe.matmul(dst, x_tok[:, c, h * SSM_P:(h + 1) * SSM_P], ssm_G[n % 2][:, c * P:(c + 1) * P], start=True, stop=(c == 0))
                        if c:
                            mm = pe.matmul(dst, state[:, c - 1, h * SSM_P:(h + 1) * SSM_P], ssm_E[n % 2][:, c * P:(c + 1) * P], start=False, stop=True)
                    mm.then_inc(y_done, 1)

                pe.wait_ge(rstd_ready, seen["sum"])
                head_row(0)
                for h in range(HPG):
                    if h + 1 < HPG:
                        head_row(h + 1)
                    head_out(h)
                pe.wait_ge(state_ready, (g + 1) * (TB - 1))
                t = stage[f"ssm_z{g}"]
                for j in range(TPG):
                    tile(t + j, opA, "x5")
            norm_sum()
            t = stage["ssm_out"]
            for i in range(KD):
                tile(t + i, opY, "ssm")
            ffn(1, "x6", "ffn1")

        @block.scalar
        def _(act):
            lane = Lane(act, act_step)
            n_ = {"src": 0, "sq": 0, "used": 0, "norm": 0, "sig": 0, "v": 0, "sq_in": 0, "hi": 0}
            act.preload_act_table_set("natural_log_exp_and_others")

            def split(u):
                if u >= NU:
                    return
                _, kt, width = units[u]
                act.wait_ge(unit_loaded[u % RAW], 16 * (u // RAW + 1))
                if u >= SPLIT:
                    act.wait_ge(unit_used, u - SPLIT + 1)
                act.activation(w_hi[u % SPLIT][:, 0:kt, 0:width], raw[u % RAW][:, 0:kt, 0:width], ACT.Copy).then_inc(hi_ready, 1)

            def ahead(t):
                u0, nu, _, _ = tiles[t]
                for u in range(u0, u0 + nu):
                    split(u + 2)

            def high(dst, source, ready=None, ready_n=None):
                if ready is None:
                    n_["src"] += 1
                    act.wait_ge(src_ready, n_["src"])
                else:
                    act.wait_ge(ready, ready_n)
                act.activation(dst, source, ACT.Copy).then_inc(op_hi_done, 1)

            def square(source, m):
                if m == 0 and n_["norm"]:
                    act.wait_ge(rstd_ready, n_["norm"])
                if m >= 2:
                    act.wait_ge(sq_used, n_["used"] + m - 1)
                n = source.shape[-1]
                act.activation(sq[m % 2][:, 0:n], source, ACT.Square).then_inc(sq_ready, 1)

            def root(n, count, width):
                n_["norm"] += 1
                n_["used"] += count - 1
                act.wait_ge(ss_summed, n_["norm"])
                lane.did(act.activation(sq[0][:, 0:n], bank[4][:, 0:n], ACT.Ln, bias=con[:, CON["eps"]:CON["eps"] + 1], scale=1.0 / width))
                lane.sync()
                act.activation(sq[1][:, 0:n], sq[0][:, 0:n], ACT.Exp, scale=-0.5).then_inc(r0_ready, 1)

            def prepare(k, gain, source=None, dst=opA, first=False):
                if source is None:
                    if not first:
                        n_["src"] += 1
                        act.wait_ge(src_ready, n_["src"])
                    source = x[:, k, :]
                act.activation(dst[0][:, k, :], source, ACT.Copy, scale=gain).then_inc(op_hi_done, 1)
                square(source, k)

            def gate():
                n_["sig"] += 1
                act.wait_ge(sig_in, n_["sig"])
                act.activation(sig[:, :], tmp[:, :], ACT.Sigmoid).then_inc(sig_ready, 1)

            def gated(name, last=False):
                t = stage[name]
                for i in range(KD):
                    ahead(t + 2 * i)
                    gate()
                    ahead(t + 2 * i + 1)
                    if last:
                        high(opC[0][:, i, :], src[:, :])

            def v_out(dst, blocks):
                n = n_["v"]
                n_["v"] += 1
                act.wait_ge(v_turned, n + 1)
                act.activation(dst, bank[5 + n % 2][:, 0:blocks * P].rearrange("p (b c) -> p b c", c=P), ACT.Copy).then_inc(v_tok_ready, 1)

            act.wait_ge(params_in, 32)
            split(0)
            split(1)
            act.wait_ge(x_in, 16 * (KD // 2))
            for k in range(KD):
                prepare(k, col("g_mix", k), first=True)
            root(SEQ, KD, D)
            t = stage["conv"]
            for i in range(KD):
                for j in range(3):
                    ahead(t + 3 * i + j)
                high(opB[0][:, i, :], src[:, :])
            gated("conv_out")
            t = stage["qkv"]
            for i in range(3 * KD):
                ahead(t + i)
                if i > 2 * KD:
                    v_out(v_tok[:, :, (i - 1 - 2 * KD) * P:(i - 2 * KD) * P], TB)
            v_out(v_tok[:, :, (KD - 1) * P:KD * P], TB)

            SPANS = ((0, 0, 512), (1, 512, 512), (2, 1024, 256))

            def sb_soft(h):
                act.wait_ge(sb_scored, h + 1)
                if h:
                    act.wait_ge(sb_sp_ready, h)
                for b, c, w in SPANS:
                    lane.did(act.activation(sb_e[:, c:c + w], bank[4 * (h % 2) + b][:, 0:w], ACT.Abs), sb_abs_done)
                lane.sync()
                for b, c, w in SPANS:
                    lane.did(act.activation(sb_e[:, c:c + w], sb_e[:, c:c + w], ACT.Exp, scale=-1.0))
                lane.sync()
                for b, c, w in SPANS:
                    act.activation(sb_e[:, c:c + w], sb_e[:, c:c + w], ACT.Ln, bias=1.0).then_inc(sb_exp_ready, 1)

            def sb_weights(h):
                act.wait_ge(sb_summed, h + 1)
                if h >= 2:
                    act.wait_ge(sb_pv_done, h - 1)
                for b, c, w in SPANS:
                    act.activation(sb_a[h % 2][:, c:c + w], bank[4 * (h % 2) + b][:, 0:w], ACT.Exp).then_inc(sb_a_ready, 1)

            def sb_high(h):
                if h % 2:
                    high(opC[0][:, h // 2, :], src[:, :], sb_o_read, h + 1)

            sb_soft(0)
            for h in range(SB_HEADS):
                if h + 1 < SB_HEADS:
                    sb_soft(h + 1)
                sb_weights(h)
                if h >= 1:
                    sb_high(h - 1)
            sb_high(SB_HEADS - 1)
            gated("sb_out")
            act.wait_ge(mem_in, 16)
            for k in range(KD):
                prepare(k, col("g_mem", k), memx[:, k, :], opM)
            root(MEM, KD, D)
            t = stage["mem_kv"]
            for i in range(2 * KD):
                ahead(t + i)
                if i < KD:
                    n_["sq_in"] += 1
                    act.wait_ge(sq_in, n_["sq_in"])
                    square(xk[:, i, :], i % 2)
                    if i % 2:
                        root(MEM, 2, X_DIM)
                if i > KD:
                    v_out(xv_tok[:, :, (i - 1 - KD) * P:(i - KD) * P], MEM // P)
            v_out(xv_tok[:, :, (KD - 1) * P:KD * P], MEM // P)
            t = stage["xq"]
            for i in range(KD):
                ahead(t + i)
                n_["sq_in"] += 1
                act.wait_ge(sq_in, n_["sq_in"])
                square(xq[:, i, :], i % 2)
                if i % 2:
                    root(SEQ, 2, X_DIM)

            XS = float(X_DIM) ** -0.5

            def x_exp(h):
                act.wait_ge(x_max_ready, h + 1)
                if h >= 2:
                    act.wait_ge(x_turned, 2 * (h - 1))
                o = 32 * (h % 2)
                for qb in range(TB):
                    act.activation(x_p[h % 2][:, qb, :], bank[qb // 2][:, (qb % 2) * MEM:(qb % 2 + 1) * MEM], ACT.Exp,
                                   bias=small[:, o + TB + qb:o + TB + qb + 1], scale=XS,
                                   accum_out=small[:, o + 2 * TB + qb:o + 2 * TB + qb + 1]).then_inc(x_exp_ready, 1)

            x_exp(0)
            for h in range(X_HEADS):
                if h + 1 < X_HEADS:
                    x_exp(h + 1)
                for kb in range(2):
                    act.wait_ge(x_turned, 2 * h + kb + 1)
                    if h:
                        act.wait_ge(x_pv_done, 2 * h)
                    act.activation(x_pT[:, kb, :], bank[2 + kb][:, :], ACT.Copy).then_inc(x_pT_ready, 1)
                for d in range(2):
                    high(opB[0][:, 2 * h + d, :], src[:, :], x_o_read, 2 * h + d + 1)
            gated("x_out", last=True)

            def residual(name, gain=None, width_g=None):
                t = stage[name]
                for i in range(KD):
                    ahead(t + i)
                    if gain is not None:
                        prepare(i, col(*gain[0:1], gain[1] + i))
                if gain is not None:
                    root(SEQ, KD, D)

            residual("w_out", ("g_mlp", 0))
            for half in range(FF1 // P // MLP_HALF):
                t = stage[f"up{half}"]
                for i in range(MLP_HALF):
                    ahead(t + i)
                    high(hid1[0][:, i, :], src[:, :])
                if half == 0:
                    for h in range(A_HEADS):
                        act.wait_ge(strip_flipped, h + 1)
                        act.activation(strip[:, h, :], bank[5 + h % 2][:, :], ACT.Copy).then_inc(strip_turned, 1)
                residual(f"down{half}", ("norm_mix_2", 0) if half else None)
            t = stage["attn_in"]
            for i in range(4 * AW + 2):
                ahead(t + i)
                if i <= 3 * AW:
                    n_["sq_in"] += 1
                    act.wait_ge(sq_in, n_["sq_in"])
                    square(qk2[:, i, :] if i < 3 * AW else src[:, :], 0)
                    root(SEQ, 1, HD)
                if i > 3 * AW + 1:
                    j = i - 1 - (3 * AW + 1)
                    v_out(va_tok[:, :, j * P:(j + 1) * P], TB)
            v_out(vb_tok[:, :, :], TB)

            items = [(h, qb) for h in range(A_HEADS + B_HEADS) for qb in range(TB)]

            def keys_of(h, qb):
                return (0, qb + 1) if h < A_HEADS else (max(0, qb - 1), min(2, qb + 1))

            def at_exp(n):
                h, qb = items[n]
                w = keys_of(h, qb)[1] * P
                o = 32 * (n % 2)
                act.wait_ge(at_max_ready, n + 1)
                act.activation(at_s[n % 2][:, 0:w], at_s[n % 2][:, 0:w], ACT.Exp, bias=small[:, o + 1:o + 2],
                               accum_out=small[:, o + 2:o + 3]).then_inc(at_exp_ready, 1)
                if h >= A_HEADS:
                    act.activation(small[:, o + 3:o + 4], col("sinks_2", h - A_HEADS), ACT.Exp, bias=small[:, o + 1:o + 2]).then_inc(at_exp_ready, 1)

            at_exp(0)
            for n in range(len(items)):
                if n + 1 < len(items):
                    at_exp(n + 1)
                w = keys_of(*items[n])[1] * P
                act.wait_ge(at_turned, n + 1)
                if n >= 2:
                    act.wait_ge(at_pv_done, n - 1)
                act.activation(at_pT[:, n % 2, 0:w], bank[2 + n % 2][:, 0:w], ACT.Copy).then_inc(at_pT_ready, 1)
                if n % 8 == 1 and n > 8:
                    h = (n - 5) // 4
                    high(opB[0][:, h // 2, :], src[:, :], at_o_read, h + 1)
            high(opB[0][:, KD - 1, :], src[:, :], at_o_read, A_HEADS + B_HEADS)
            residual("attn_out", ("norm_ffn_2", 0))

            def ffn(layer, after):
                t = stage[f"ffn_in{layer}"]
                for i in range(KF2):
                    ahead(t + 2 * i)
                    gate()
                    ahead(t + 2 * i + 1)
                    high(hid2[0][:, i, :], src[:, :])
                residual(f"ffn_out{layer}", after)

            ffn(0, ("norm_mix_2", KD))
            S32 = SSM_HEADS
            ahead(stage["dt"])
            act.wait_ge(dt_in, 1)
            lane.did(act.activation(dt_e[0:S32, :], dt_m[0:S32, :], ACT.Abs))
            lane.did(act.activation(small[0:S32, 0:1], col("a_log")[0:S32, :], ACT.Exp))
            lane.sync()
            act.activation(dt_e[0:S32, :], dt_e[0:S32, :], ACT.Exp, scale=-1.0).then_inc(dt_exp, 1)
            act.wait_ge(dt_ln_in, 1)
            act.activation(dt_wT[0:S32, :], dt_d[0:S32, :], ACT.Ln).then_inc(dt_ln, 1)
            act.wait_ge(dt_acs, TB)
            for c in range(TB):
                act.activation(dt_wT[0:S32, c * P:(c + 1) * P], dt_acsT[0:S32, c * P:(c + 1) * P], ACT.Exp,
                               bias=dt_acsT[0:S32, c * P + P - 1:c * P + P], scale=-1.0).then_inc(dt_w, 1)
            xt = [0]

            def x_out_tok(dst):
                n = xt[0]
                xt[0] += 1
                act.wait_ge(xs_turned, n + 1)
                act.activation(dst, bank[5 + n % 2][:, :].rearrange("p (b c) -> p b c", c=P), ACT.Copy).then_inc(x_tok_ready, 1)

            for g in range(SSM_G):
                t = stage[f"ssm_bcx{g}"]
                for j in range(2 + TPG):
                    ahead(t + j)
                    gate()
                    if j == 1:
                        x_out_tok(b_tok[:, :, :])
                    if j >= 3:
                        x_out_tok(x_tok[:, :, (j - 3) * P:(j - 2) * P])
                x_out_tok(x_tok[:, :, (TPG - 1) * P:TPG * P])
                if g == 0:
                    act.wait_ge(dt_turned, 1)
                    act.activation(dt_tok[:, :, :, :].rearrange("p a b c -> p (a b c)"), bank[1][:, 0:3 * TB * S32], ACT.Copy).then_inc(dt_tok_ready, 1)
                    act.wait_ge(dt_elast, 1)
                    act.activation(e_last[:, :, :].rearrange("p b c -> p (b c)"), bank[2][:, 0:TB * S32], ACT.Exp).then_inc(dt_tok_ready, 1)
                for h in range(HPG):
                    n = g * HPG + h
                    act.wait_ge(row_done, n + 1)
                    if n >= 2:
                        act.wait_ge(y_done, n - 1)
                    act.activation(ssm_E[n % 2][:, :], bank[4 if n % 2 else 3][:, :], ACT.Exp).then_inc(dec_exp, 1)
                    act.wait_ge(dec_in, n + 1)
                    act.activation(ssm_S[n % 2][:, :], ssm_S[n % 2][:, :], ACT.Exp).then_inc(dec_exp, 1)
                t = stage[f"ssm_z{g}"]
                for j in range(TPG):
                    ahead(t + j)
                    gate()
                    n_["sq_in"] += 1
                    act.wait_ge(sq_in, n_["sq_in"])
                    square(xs[:, j, :], j)
                root(SEQ, TPG, SSM_IN // SSM_G)
                for j in range(TPG):
                    high(opY[0][:, g * TPG + j, :], src[:, :])
            residual("ssm_out", ("norm_ffn_2", KD))
            ffn(1, None)

        @block.vector
        def _(dve):
            lane = Lane(dve, dve_step)
            did, sync = lane.did, lane.sync
            n_ = {"hi": 0, "sq": 0, "norm": 0, "sig": 0, "v": 0}
            V = nc.vector

            def split(u):
                if u >= NU:
                    return
                _, kt, width = units[u]
                dve.wait_ge(hi_ready, u + 1)
                did(V.tensor_tensor(w_lo[u % SPLIT][:, 0:kt, 0:width], raw[u % RAW][:, 0:kt, 0:width],
                                    w_hi[u % SPLIT][:, 0:kt, 0:width].bitcast(F32), ALU.subtract), lo_ready)

            def ahead(t):
                sync()
                u0, nu, _, _ = tiles[t]
                for u in range(u0, u0 + nu):
                    split(u + 2)

            def arrive(t, n=SEQ):
                dve.wait_ge(unit_used, last_unit(t) + 1)
                return bank[t % 4][0:tiles[t][3], 0:n]

            def low(dst, source, gain=None):
                n_["hi"] += 1
                dve.wait_ge(op_hi_done, n_["hi"])
                sync()
                if gain is None:
                    did(V.tensor_tensor(dst[1], source, dst[0].bitcast(F32), ALU.subtract), op_ready)
                else:
                    did(V.scalar_tensor_tensor(dst[1], source, gain, dst[0].bitcast(F32), ALU.mult, ALU.subtract), op_ready)

            def pair(op, k):
                return op[0][:, k, :], op[1][:, k, :]

            def add_square(m, count, n=SEQ):
                n_["sq"] += 1
                dve.wait_ge(sq_ready, n_["sq"])
                sync()
                s = ss_added if m == count - 1 else sq_used
                if m == 0:
                    did(V.tensor_copy(ss[:, 0:n], sq[0][:, 0:n]), s)
                else:
                    did(V.tensor_tensor(ss[:, 0:n], ss[:, 0:n], sq[m % 2][:, 0:n], ALU.add), s)

            def norm(dst, n, width):
                n_["norm"] += 1
                dve.wait_ge(r0_ready, n_["norm"])
                sync()
                m, r, q = ss[:, 0:n], sq[1][:, 0:n], sq[0][:, 0:n]
                did(V.tensor_scalar(m, bank[4][:, 0:n], 1.0 / width, EPS, ALU.mult, ALU.add))
                did(V.tensor_tensor(q, r, r, ALU.mult))
                sync()
                did(V.tensor_tensor(q, q, m, ALU.mult))
                sync()
                did(V.tensor_scalar(q, q, -0.5, 1.5, ALU.mult, ALU.add))
                sync()
                did(V.tensor_tensor(dst, r, q, ALU.mult), rstd_ready)
                sync()

            def wait_gate():
                n_["sig"] += 1
                dve.wait_ge(sig_ready, n_["sig"])

            R = rstd[:, :]

            def gated(name, first=False, last=False):
                t = stage[name]
                for i in range(KD):
                    ahead(t + 2 * i)
                    did(V.tensor_tensor(tmp[:, :], arrive(t + 2 * i), R, ALU.mult), sig_in)
                    ahead(t + 2 * i + 1)
                    y = arrive(t + 2 * i + 1)
                    wait_gate()
                    if first:
                        did(V.tensor_tensor(merged[:, i, :], sig[:, :], y, ALU.mult))
                        continue
                    did(V.tensor_tensor(tmp2[:, :], sig[:, :], y, ALU.mult))
                    sync()
                    if last:
                        did(V.tensor_tensor(src[:, :], merged[:, i, :], tmp2[:, :], ALU.add), src_ready)
                        low(pair(opC, i), src[:, :])
                    else:
                        did(V.tensor_tensor(merged[:, i, :], merged[:, i, :], tmp2[:, :], ALU.add))
                sync()

            def conv(dst, taps, name, index, stride, bias=None):
                for j in range(taps):
                    s = pad[:, 4 - taps + j:4 - taps + j + SEQ]
                    w = col(name, j * stride + index)
                    sync()
                    if j == 0:
                        if bias is None:
                            did(V.tensor_scalar(dst, s, w, None, ALU.mult))
                        else:
                            did(V.tensor_scalar(dst, s, w, bias, ALU.mult, ALU.add))
                    else:
                        did(V.scalar_tensor_tensor(dst, s, w, dst, ALU.mult, ALU.add), *((sig_in,) if j == taps - 1 and bias is not None else ()))

            def v_in(t, r, n):
                i = n_["v"]
                n_["v"] += 1
                if i >= 2:
                    dve.wait_ge(v_turned, i - 1)
                did(V.tensor_tensor((tmp if i % 2 == 0 else tmp2)[:, 0:n], arrive(t, n), r, ALU.mult), vT_ready)

            did(V.memset(pad[:, 0:3], 0.0))
            dve.wait_ge(params_in, 32)
            split(0)
            split(1)
            did(V.tensor_scalar(col("q_norm_a_2"), col("q_norm_a_2"), HD ** -0.5, None, ALU.mult))
            did(V.tensor_scalar(col("q_norm_b_2"), col("q_norm_b_2"), HD ** -0.5, None, ALU.mult))
            dve.wait_ge(x_in, 16 * (KD // 2))
            for k in range(KD):
                low(pair(opA, k), x[:, k, :], col("g_mix", k))
                add_square(k, KD)
            norm(R, SEQ, D)
            t = stage["conv"]
            for i in range(KD):
                ahead(t + 3 * i)
                did(V.tensor_tensor(tmp2[:, :], arrive(t + 3 * i), R, ALU.mult))
                ahead(t + 3 * i + 1)
                did(V.tensor_tensor(tmp[:, :], arrive(t + 3 * i + 1), R, ALU.mult))
                sync()
                did(V.tensor_tensor(pad[:, 3:3 + SEQ], tmp[:, :], tmp2[:, :], ALU.mult))
                conv(tmp[:, :], 3, "conv_w", i, KD)
                ahead(t + 3 * i + 2)
                did(V.tensor_tensor(tmp2[:, :], arrive(t + 3 * i + 2), R, ALU.mult))
                sync()
                did(V.tensor_tensor(src[:, :], tmp2[:, :], tmp[:, :], ALU.mult), src_ready)
                low(pair(opB, i), src[:, :])
            gated("conv_out", first=True)
            t = stage["qkv"]
            for i in range(3 * KD):
                ahead(t + i)
                if i < KD:
                    did(V.scalar_tensor_tensor(qT[:, i, :], arrive(t + i), SB_DIM ** -0.5, R, ALU.mult, ALU.mult))
                elif i < 2 * KD:
                    did(V.tensor_tensor(kT[:, i - KD, :], arrive(t + i), R, ALU.mult))
                else:
                    v_in(t + i, R, SEQ)
            sync()

            SPANS = ((0, 0, 512), (1, 512, 512), (2, 1024, 256))

            def sb_softplus(h):
                s_ = sb_sp[h % 2]
                if h >= 2:
                    dve.wait_ge(sb_summed, h - 1)
                for i, (b, c, w) in enumerate(SPANS):
                    dve.wait_ge(sb_abs_done, 3 * h + i + 1)
                    did(V.tensor_scalar(s_[:, c:c + w], bank[4 * (h % 2) + b][:, 0:w], 0.0, None, ALU.max))
                sync()
                for i, (b, c, w) in enumerate(SPANS):
                    dve.wait_ge(sb_exp_ready, 3 * h + i + 1)
                    did(V.tensor_tensor(s_[:, c:c + w], s_[:, c:c + w], sb_e[:, c:c + w], ALU.add))
                sync()
                past = const("past")
                did(V.tensor_tensor(s_[:, 0:P], s_[:, 0:P], past, ALU.mult))
                did(V.tensor_tensor(s_[:, 512:512 + P], s_[:, 512:512 + P], past, ALU.mult))
                did(V.tensor_tensor(s_[:, 896:1024], s_[:, 896:1024], past, ALU.mult))
                sync()
                did(V.tensor_tensor(s_[:, 1024:1152], s_[:, 1024:1152], past, ALU.mult), sb_sp_ready)

            def sb_out(h):
                r = HD * (h % 2)
                dve.wait_ge(sb_pv_done, h + 1)
                sync()
                did(V.tensor_copy(src[r:r + HD, :], bank[3 + 4 * (h % 2)][0:HD, :]), sb_o_read)
                if h % 2:
                    low(pair(opC, h // 2), src[:, :])

            sb_softplus(0)
            for h in range(SB_HEADS):
                if h + 1 < SB_HEADS:
                    sb_softplus(h + 1)
                if h >= 1:
                    sb_out(h - 1)
            sb_out(SB_HEADS - 1)
            gated("sb_out")
            dve.wait_ge(mem_in, 16)
            for k in range(KD):
                low(pair(opM, k), memx[:, k, :], col("g_mem", k))
                add_square(k, KD, MEM)
            RM = rstd_m[:, :]
            norm(RM, MEM, D)

            def head_norm(dst, k, n, r, name, ready=None):
                for j in range(2):
                    add_square(j, 2, n)
                norm(sig[:, 0:n], n, X_DIM)
                for j in range(2):
                    did(V.scalar_tensor_tensor(dst[:, k + j, :], dst[:, k + j, :], col(name, j), sig[:, 0:n], ALU.mult, ALU.mult), *((ready,) if ready else ()))

            t = stage["mem_kv"]
            for i in range(2 * KD):
                ahead(t + i)
                if i < KD:
                    did(V.tensor_tensor(xk[:, i, :], arrive(t + i, MEM), RM, ALU.mult), sq_in)
                    if i % 2:
                        head_norm(xk, i - 1, MEM, RM, "k_norm_g")
                else:
                    v_in(t + i, RM, MEM)
            t = stage["xq"]
            for i in range(KD):
                ahead(t + i)
                did(V.tensor_tensor(xq[:, i, :], arrive(t + i), R, ALU.mult), sq_in)
                if i % 2:
                    head_norm(xq, i - 1, SEQ, R, "q_norm_g", xq_ready)
            sync()

            def x_max(h):
                o = 32 * (h % 2)
                dve.wait_ge(x_scored, h + 1)
                for b in range(2):
                    did(V.tensor_reduce(small[:, o + 2 * b:o + 2 * b + 2], bank[b][:, :].rearrange("p (q k) -> p q k", k=MEM), AX.X, ALU.max))
                sync()
                did(V.tensor_scalar(small[:, o + TB:o + 2 * TB], small[:, o:o + TB], -float(X_DIM) ** -0.5, None, ALU.mult), x_max_ready)

            x_max(0)
            for h in range(X_HEADS):
                if h + 1 < X_HEADS:
                    x_max(h + 1)
                o = 32 * (h % 2)
                dve.wait_ge(x_exp_ready, TB * (h + 1))
                did(V.reciprocal(small[:, o + 3 * TB:o + 4 * TB], small[:, o + 2 * TB:o + 3 * TB]))
                sync()
                for qb in range(TB):
                    ins = V.tensor_scalar(x_p[h % 2][:, qb, :], x_p[h % 2][:, qb, :], small[:, o + 3 * TB + qb:o + 3 * TB + qb + 1], None, ALU.mult)
                    if qb == TB - 1:
                        did(ins, x_p_ready)
                    else:
                        did(ins)
                        sync()
                for d in range(2):
                    n = 2 * h + d
                    dve.wait_ge(x_pv_done, n + 1)
                    sync()
                    did(V.tensor_copy(src[:, :], bank[5 + d][:, :]), x_o_read)
                    low(pair(opB, n), src[:, :])
            gated("x_out", last=True)
            dve.sem_inc(strip_zone_free, 1)

            def residual(name, prep=None, result=False):
                t = stage[name]

                def finish(k):
                    low(pair(opA, k), x[:, k, :], col(prep[0], prep[1] + k))
                    add_square(k, KD)

                for i in range(KD):
                    ahead(t + i)
                    did(V.tensor_tensor(x[:, i, :], x[:, i, :], arrive(t + i), ALU.add), *((src_ready,) if prep else (out_ready,) if result else ()))
                    if prep and i:
                        finish(i - 1)
                if prep:
                    finish(KD - 1)
                    norm(R, SEQ, D)

            residual("w_out", ("g_mlp", 0))
            for half in range(FF1 // P // MLP_HALF):
                t = stage[f"up{half}"]
                for i in range(MLP_HALF):
                    ahead(t + i)
                    did(V.tensor_tensor(tmp[:, :], arrive(t + i), R, ALU.mult))
                    sync()
                    did(V.scalar_tensor_tensor(src[:, :], tmp[:, :], 0.0, tmp[:, :], ALU.max, ALU.mult), src_ready)
                    low(pair(hid1, i), src[:, :])
                residual(f"down{half}", ("norm_mix_2", 0) if half else None)
            dve.wait_ge(strip_turned, A_HEADS)
            did(V.memset(strip[0:HD, :, SEQ - HD:SEQ], -BIG))
            t = stage["attn_in"]
            for i in range(4 * AW + 2):
                ahead(t + i)
                if i > 3 * AW:
                    v_in(t + i, R, SEQ)
                    continue
                d = qk2[:, i, :] if i < 3 * AW else src[:, :]
                did(V.tensor_tensor(d, arrive(t + i), R, ALU.mult), sq_in)
                add_square(0, 1)
                norm(sig[:, :], SEQ, HD)
                name = ("q_norm_a_2", "k_norm_a_2", "q_norm_b_2", "k_norm_b_2")[i // AW]
                did(V.scalar_tensor_tensor(d, d, col(name), sig[:, :], ALU.mult, ALU.mult), at_q_ready)
                if i == 3 * AW:
                    sync()
                    for kv in range(B_KV):
                        for half in range(2):
                            did(V.tensor_copy(kb2[half * HD:(half + 1) * HD, kv, :], src[kv * HD:(kv + 1) * HD, :]))
            sync()

            items = [(h, qb) for h in range(A_HEADS + B_HEADS) for qb in range(TB)]

            def keys_of(h, qb):
                return (0, qb + 1) if h < A_HEADS else (max(0, qb - 1), min(2, qb + 1))

            def at_max(n):
                h, qb = items[n]
                w = keys_of(h, qb)[1] * P
                o = 32 * (n % 2)
                s_ = at_s[n % 2][:, 0:w]
                dve.wait_ge(at_scored, n + 1)
                if n >= 2:
                    dve.wait_ge(at_turned, n - 1)
                sync()
                ps = bank[n % 2][:, 0:w]
                if h < A_HEADS:
                    did(V.tensor_tensor(s_, ps, strip[:, h, SEQ - w:SEQ], ALU.add))
                else:
                    dist = con[:, CON["dist_b"] + 2 * P - w:CON["dist_b"] + 2 * P]
                    did(V.scalar_tensor_tensor(s_, dist, 2.0 ** (-8.0 * (h - A_HEADS + 1) / B_HEADS), ps, ALU.mult, ALU.add))
                sync()
                did(V.tensor_reduce(small[:, o:o + 1], s_, AX.X, ALU.max))
                sync()
                if h >= A_HEADS:
                    did(V.tensor_scalar(small[:, o + 1:o + 2], small[:, o:o + 1], col("sinks_2", h - A_HEADS), -1.0, ALU.max, ALU.mult), at_max_ready)
                else:
                    did(V.tensor_scalar(small[:, o + 1:o + 2], small[:, o:o + 1], -1.0, None, ALU.mult), at_max_ready)

            def at_out(h):
                r = HD * (h % 2)
                dve.wait_ge(at_pv_done, TB * (h + 1))
                sync()
                did(V.tensor_copy(src[r:r + HD, :], bank[5 + h % 2][0:HD, :]), at_o_read)
                if h % 2:
                    low(pair(opB, h // 2), src[:, :])

            at_max(0)
            for n, (h, qb) in enumerate(items):
                if n + 1 < len(items):
                    at_max(n + 1)
                o = 32 * (n % 2)
                w = keys_of(h, qb)[1] * P
                b_items = max(0, n + 1 - A_HEADS * TB)
                dve.wait_ge(at_exp_ready, n + 1 + b_items)
                if h >= A_HEADS:
                    did(V.tensor_tensor(small[:, o + 2:o + 3], small[:, o + 2:o + 3], small[:, o + 3:o + 4], ALU.add))
                    sync()
                did(V.reciprocal(small[:, o + 4:o + 5], small[:, o + 2:o + 3]))
                sync()
                did(V.tensor_scalar(at_s[n % 2][:, 0:w], at_s[n % 2][:, 0:w], small[:, o + 4:o + 5], None, ALU.mult), at_p_ready)
                if n % 4 == 1 and n > 4:
                    at_out((n - 5) // 4)
            at_out(A_HEADS + B_HEADS - 1)
            residual("attn_out", ("norm_ffn_2", 0))

            def ffn(layer, after):
                t = stage[f"ffn_in{layer}"]
                for i in range(KF2):
                    ahead(t + 2 * i)
                    did(V.tensor_tensor(pad[:, 3:3 + SEQ], arrive(t + 2 * i), R, ALU.mult))
                    conv(tmp[:, :], 3, "ffn_conv_w_2", layer * 3 * KF2 + i, KF2, col("ffn_conv_b_2", layer * KF2 + i))
                    ahead(t + 2 * i + 1)
                    did(V.tensor_tensor(tmp2[:, :], arrive(t + 2 * i + 1), R, ALU.mult))
                    sync()
                    wait_gate()
                    did(V.tensor_tensor(tmp2[:, :], tmp2[:, :], sig[:, :], ALU.mult))
                    sync()
                    did(V.tensor_tensor(src[:, :], tmp2[:, :], tmp[:, :], ALU.mult), src_ready)
                    low(pair(hid2, i), src[:, :])
                residual(f"ffn_out{layer}", after, result=(layer == 1))

            ffn(0, ("norm_mix_2", KD))
            S32 = SSM_HEADS
            t = stage["dt"]
            ahead(t)
            e, v, u, lnu, dtT = dt_e[0:S32, :], dt_m[0:S32, :], dt_d[0:S32, :], dt_wT[0:S32, :], dt_dtT[0:S32, :]
            did(V.tensor_tensor(v, arrive(t), rstd[0:S32, :], ALU.mult))
            sync()
            did(V.tensor_scalar(v, v, col("dt_bias")[0:S32, :], None, ALU.add), dt_in)
            dve.wait_ge(dt_exp, 1)
            did(V.tensor_scalar(u, e, 1.0, None, ALU.add), dt_ln_in)
            dve.wait_ge(dt_ln, 1)
            sync()
            did(V.tensor_scalar(u, u, -1.0, None, ALU.add))
            sync()
            z = tmp[0:S32, :]
            did(V.tensor_scalar(z, u, 0.0, None, ALU.is_equal))
            sync()
            did(V.tensor_tensor(u, u, z, ALU.add))
            did(V.tensor_tensor(lnu, lnu, z, ALU.add))
            sync()
            did(V.reciprocal(u, u))
            did(V.tensor_tensor(lnu, lnu, e, ALU.mult))
            sync()
            did(V.tensor_tensor(lnu, lnu, u, ALU.mult))
            sync()
            did(V.scalar_tensor_tensor(dtT, v, 0.0, lnu, ALU.max, ALU.add))
            sync()
            did(V.tensor_scalar(u, dtT, small[0:S32, 0:1], -1.0, ALU.mult, ALU.mult))
            sync()
            for c in range(TB):
                cc = slice(c * P, (c + 1) * P)
                did(V.tensor_tensor_scan(dt_acsT[0:S32, cc], const("ones")[0:S32, :], u[:, cc], 0.0, ALU.mult, ALU.add), dt_acs)
            dve.wait_ge(dt_w, TB)
            sync()
            for c in range(TB):
                did(V.tensor_scalar(dt_last[0:S32, c * S32:(c + 1) * S32], ident[0:S32, 0:S32], dt_acsT[0:S32, c * P + P - 1:c * P + P], None, ALU.mult))
            sync()
            did(V.tensor_tensor(dt_wT[0:S32, :], dt_wT[0:S32, :], dtT, ALU.mult), dt_ready)
            for g in range(SSM_G):
                t = stage[f"ssm_bcx{g}"]
                for j in range(2 + TPG):
                    ahead(t + j)
                    ch = (4 * TPG + g, 4 * TPG + SSM_G + g)[j] if j < 2 else g * TPG + j - 2
                    dst = bT[:, :] if j == 0 else cT[:, :] if j == 1 else xs[:, j - 2, :]
                    did(V.tensor_tensor(pad[:, 3:3 + SEQ], arrive(t + j), R, ALU.mult))
                    conv(tmp[:, :], 4, "ssm_conv_w_2", ch, 24, col("ssm_conv_b_2", ch))
                    wait_gate()
                    sync()
                    did(V.tensor_tensor(dst, tmp[:, :], sig[:, :], ALU.mult), xs_ready)
                sync()
                if g == 0:
                    dve.wait_ge(dt_tok_ready, 2)
                dve.wait_ge(cb_done, g + 1)
                did(V.tensor_tensor(cbm[:, :, :], bank[0][:, :].rearrange("p (c l) -> p c l", l=P),
                                    const("causal").rearrange("p (o l) -> p o l", o=1).to_broadcast([P, TB, P]), ALU.mult), cb_ready)
                h0 = g * HPG
                dve.wait_ge(x_tok_ready, 5 * g + 5)
                for c in range(TB - 1):
                    w = dt_tok[:, 2, c, h0:h0 + HPG].rearrange("p (h o) -> p h o", o=1).to_broadcast([P, HPG, SSM_P])
                    sync()
                    did(V.tensor_tensor(xw[:, :].rearrange("p (h d) -> p h d", d=SSM_P), x_tok[:, c, :].rearrange("p (h d) -> p h d", d=SSM_P), w, ALU.mult), xw_ready)
                    sync()
                    dve.wait_ge(upd_done, g * (TB - 1) + c + 1)
                    if c == 0:
                        did(V.tensor_copy(state[:, 0, :], bank[1][:, :]), state_ready)
                    else:
                        d = e_last[:, c, h0:h0 + HPG].rearrange("p (h o) -> p h o", o=1).to_broadcast([P, HPG, SSM_P])
                        did(V.tensor_tensor(tmp[:, :].rearrange("p (h d) -> p h d", d=SSM_P), state[:, c - 1, :].rearrange("p (h d) -> p h d", d=SSM_P), d, ALU.mult))
                        sync()
                        did(V.tensor_tensor(state[:, c, :], tmp[:, :], bank[1 + c % 2][:, :], ALU.add), state_ready)

                def decay_in(h):
                    n = h0 + h
                    dve.wait_ge(dec_exp, 2 * n + 1)
                    sync()
                    for c in range(TB):
                        ins = V.tensor_scalar(ssm_S[n % 2][:, c * P:(c + 1) * P], bank[4 if n % 2 else 3][:, c * P:(c + 1) * P],
                                              dt_tok[:, 0, c, n:n + 1], 0.0, ALU.subtract, ALU.min)
                        did(ins, *((dec_in,) if c == TB - 1 else ()))
                        if c < TB - 1:
                            pass

                def y_out(h):
                    n = h0 + h
                    r, j = SSM_P * (h % 2), h // 2
                    dve.wait_ge(y_done, n + 1)
                    did(V.scalar_tensor_tensor(xs[r:r + SSM_P, j, :], xs[r:r + SSM_P, j, :], par[r:r + SSM_P, PAR["ssm_d_2"] + g * TPG + j:PAR["ssm_d_2"] + g * TPG + j + 1],
                                               bank[5 + n % 2][0:SSM_P, :], ALU.mult, ALU.add), y_read)

                decay_in(0)
                for h in range(HPG):
                    n = h0 + h
                    if h + 1 < HPG:
                        decay_in(h + 1)
                    dve.wait_ge(dec_exp, 2 * (n + 1))
                    if n >= 2:
                        dve.wait_ge(y_done, n - 1)
                    sync()
                    for c in range(TB):
                        cc = slice(c * P, (c + 1) * P)
                        did(V.scalar_tensor_tensor(ssm_G[n % 2][:, cc], ssm_S[n % 2][:, cc], dt_tok[:, 1, c, n:n + 1], cbm[:, c, :], ALU.mult, ALU.mult))
                    sync()
                    did(V.tensor_tensor(ssm_E[n % 2][:, P:SEQ], ssm_E[n % 2][:, P:SEQ], cT[:, P:SEQ], ALU.mult), g_ready)
                    if h >= 1:
                        y_out(h - 1)
                y_out(HPG - 1)
                t = stage[f"ssm_z{g}"]
                for j in range(TPG):
                    ahead(t + j)
                    did(V.tensor_tensor(tmp[:, :], arrive(t + j), R, ALU.mult), sig_in)
                    sync()
                    wait_gate()
                    did(V.tensor_tensor(xs[:, j, :], xs[:, j, :], sig[:, :], ALU.mult))
                    sync()
                    did(V.tensor_tensor(xs[:, j, :], xs[:, j, :], tmp[:, :], ALU.mult), sq_in)
                    add_square(j, TPG)
                norm(sig[:, :], SEQ, SSM_IN // SSM_G)
                for j in range(TPG):
                    sync()
                    did(V.scalar_tensor_tensor(src[:, :], xs[:, j, :], col("ssm_norm_2", g * TPG + j), sig[:, :], ALU.mult, ALU.mult), src_ready)
                    low(pair(opY, g * TPG + j), src[:, :])
            residual("ssm_out", ("norm_ffn_2", KD))
            ffn(1, None)


_WEIGHTS = ["w_in", "w_conv_out", "w_sb_out", "w_mem_kv", "w_x_out", "w_out", "w_up", "w_down",
            "attn_w_in_2", "attn_w_out_2", "ssm_w_in_2", "ssm_w_out_2", "ffn_w_in_2", "ffn_w_out_2"]


def kernel(**inputs):
    import numpy as np
    import concourse.bacc as _bacc
    from concourse.bass_utils import run_bass_kernel_spmd as _run

    a = {k: np.asarray(v) for k, v in inputs.items()}

    def columns(v):
        return v.reshape(-1, P).T

    par = {n: columns(a[n]) for n in ("g_mix", "g_mem", "conv_w", "q_norm_g", "k_norm_g", "g_mlp", "norm_mix_2", "norm_ffn_2",
                                      "ffn_conv_w_2", "ffn_conv_b_2", "ssm_conv_w_2", "ssm_conv_b_2", "ssm_norm_2")}
    par["ssm_d_2"] = columns(np.repeat(a["ssm_d_2"].reshape(-1), SSM_P))
    for n in ("q_norm_a_2", "k_norm_a_2", "q_norm_b_2", "k_norm_b_2"):
        v = a[n].reshape(-1)
        par[n] = np.concatenate([v, v]).reshape(P, 1)
    par["sinks_2"] = np.repeat(a["sinks_2"].reshape(1, -1), P, axis=0)
    par["dt_bias"] = np.tile(a["ssm_dt_bias_2"].reshape(-1), P // SSM_HEADS).reshape(P, 1)
    par["a_log"] = np.tile(a["ssm_a_log_2"].reshape(-1), P // SSM_HEADS).reshape(P, 1)
    table = a["relpos_table_2"].reshape(A_HEADS, -1)
    reach = (table.shape[1] - 1) // 2
    rel = table[:, reach + np.clip(SEQ - 1 - np.arange(STRIP_E), -reach, reach)]

    i, j = np.arange(P)[:, None], np.arange(P)[None, :]
    f = np.float32
    m = np.arange(2 * P)[None, :]
    seen = (m // HD <= i // HD + 2) & (m // HD >= i // HD)
    con = {"ident": i == j, "neg_later": -(i >= j).astype(f), "neg_ones": -np.ones((P, P)), "past": i < j,
           "neg_future": -BIG * (i >= j), "ones": np.ones((P, P)), "head_ones": i // HD == j // HD, "causal": i <= j,
           "dist_b": np.where(seen, -np.abs(i - m + P), -BIG * 256.0), "flip": i + j == P - 1, "eps": np.full((P, 1), EPS)}
    arrays = {
        "xT": np.ascontiguousarray(a["x"].reshape(SEQ, KD, P).transpose(2, 1, 0)),
        "memT": np.ascontiguousarray(a["mem"].reshape(MEM, KD, P).transpose(2, 1, 0)),
        "par": np.ascontiguousarray(np.concatenate([par[n] for n in PAR], axis=1)),
        "con": np.ascontiguousarray(np.concatenate([con[n].astype(f) for n in CON], axis=1)),
        "rel": np.ascontiguousarray(rel),
    }
    for n in _WEIGHTS:
        w = a[n]
        arrays[n] = np.ascontiguousarray(w if n.startswith("ffn") else w.reshape(w.shape[1:]))
    nc = _bacc.Bacc("TRN2", target_bir_lowering=False, num_devices=1, dynamic_dma_scratch_size=2048)
    dram = {n: nc.dram_tensor(n, v.shape, F32, kind="ExternalInput").ap() for n, v in arrays.items()}
    out = nc.dram_tensor("outT", (P, KD, SEQ), F32, kind="ExternalOutput").ap()
    two_block_kernel(nc, dram, out)
    r = _run(nc, [arrays], core_ids=[0])
    return r.results[0]["outT"].transpose(2, 1, 0).reshape(1, SEQ, D)
```

```python
from contextlib import ExitStack

import concourse.bass as bass
from concourse import mybir

F32 = mybir.dt.float32
F32R = mybir.dt.float32r
ALU = mybir.AluOpType
ACT = mybir.ActivationFunctionType
AX = mybir.AxisListType

P = 128
SEQ = 512
D = 1024
MEM = 256
KD = D // P
TB = SEQ // P
EPS = 1e-6
BIG = 1e30

SB_HEADS, SB_DIM = 16, 64
X_HEADS, X_DIM = 4, 256
FF1 = 4096
A_HEADS = B_HEADS = 8
B_KV = 2
HD = 64
SSM_G, SSM_N, SSM_HEADS, SSM_P = 4, 128, 32, 64
SSM_IN = SSM_HEADS * SSM_P
HPG = SSM_HEADS // SSM_G
TPG = HPG * SSM_P // P
FF2 = 2816
KF2 = FF2 // P
UNIT_K = 8
RAW, SPLIT = 3, 3
MLP_HALF = 16

PAR = {}
_at = 0
for _name, _n in (("g_mix", 8), ("g_mem", 8), ("conv_w", 24), ("q_norm_g", 2), ("k_norm_g", 2),
                  ("g_mlp", 8), ("norm_mix_2", 16), ("norm_ffn_2", 16),
                  ("ffn_conv_w_2", 2 * 3 * KF2), ("ffn_conv_b_2", 2 * KF2),
                  ("ssm_conv_w_2", 4 * 24), ("ssm_conv_b_2", 24), ("ssm_norm_2", 16),
                  ("ssm_d_2", 16), ("q_norm_a_2", 1), ("k_norm_a_2", 1), ("q_norm_b_2", 1),
                  ("k_norm_b_2", 1), ("sinks_2", B_HEADS), ("dt_bias", 1), ("a_log", 1)):
    PAR[_name] = _at
    _at += _n
NPAR = _at

CON = {}
_at = 0
for _name, _n in (("ident", P), ("neg_later", P), ("neg_ones", P), ("past", P), ("neg_future", P),
                  ("ones", P), ("head_ones", P), ("causal", P), ("neg_before", P), ("dist_b", 2 * P), ("flip", P), ("eps", 1)):
    CON[_name] = _at
    _at += _n
NCON = _at
STRIP_E = 639


class Lane:

    def __init__(self, eng, step):
        self.eng, self.step, self.count, self.open = eng, step, {}, {}

    def did(self, ins, sem=None):
        s = sem or self.step
        ins.then_inc(s, 1)
        self.count[s.name] = self.count.get(s.name, 0) + 1
        self.open[s.name] = (s, self.count[s.name])

    def sync(self):
        for s, v in self.open.values():
            self.eng.wait_ge(s, v)
        self.open = {}


def two_block_kernel(nc, dram, out):
    ctx = ExitStack()
    with ctx:
        def sem(name):
            return ctx.enter_context(nc.semaphore(name))

        base = (nc.sbuf_base + 31) // 32 * 32
        room = nc.sbuf_usable_end - base
        arena = ctx.enter_context(nc.sbuf_tensor("arena", [P, (nc.sbuf_bytes_remaining - 64) // 4], F32))
        cursor = [base]

        def at(name, offset, shape, dt=F32):
            return nc.alloc_sbuf_tensor_at(name, [P] + list(shape), dt, offset=offset)

        def size(shape):
            n = 4
            for s in shape:
                n *= s
            return (n + 31) // 32 * 32

        def place(name, shape, dt=F32):
            t = at(name, cursor[0], shape, dt)
            cursor[0] += size(shape)
            return t

        par = place("par", [NPAR])
        con = place("con", [NCON])
        raw = [place(f"raw{i}", [UNIT_K, P]) for i in range(RAW)]
        w_hi = [place(f"w_hi{i}", [UNIT_K, P], F32R) for i in range(SPLIT)]
        w_lo = [place(f"w_lo{i}", [UNIT_K, P], F32R) for i in range(SPLIT)]
        x = place("x", [KD, SEQ])
        rstd = place("rstd", [SEQ])
        TILE = 2048
        a_off = cursor[0]
        b_off = a_off + 2 * KD * TILE
        c_off = b_off + 2 * KD * TILE
        d_off = c_off + 2 * KD * TILE
        t_off = d_off + 2 * KD * TILE
        cursor[0] = t_off
        opA = [at("opA_hi", a_off, [KD, SEQ], F32R), at("opA_lo", a_off + KD * TILE, [KD, SEQ], F32R)]
        opB = [at("opB_hi", b_off, [KD, SEQ], F32R), at("opB_lo", b_off + KD * TILE, [KD, SEQ], F32R)]
        opC = [at("opC_hi", c_off, [KD, SEQ], F32R), at("opC_lo", c_off + KD * TILE, [KD, SEQ], F32R)]
        sq = [place(f"sq{i}", [SEQ]) for i in range(2)]
        ss = place("ss", [SEQ])
        src = place("src", [SEQ])
        pad = place("pad", [SEQ + 4])
        tmp = place("tmp", [SEQ])
        tmp2 = place("tmp2", [SEQ])
        sig = place("sig", [SEQ])
        small = place("small", [64])
        dt_acsT = place("dt_acsT", [SEQ])
        dt_last = place("dt_last", [TB * SSM_HEADS])
        dt_tok = place("dt_tok", [3, TB, SSM_HEADS])
        e_last = place("e_last", [TB, SSM_HEADS])
        ident_r = place("ident_r", [P], F32R)
        neg_later_r = place("neg_later_r", [P], F32R)
        neg_ones_r = place("neg_ones_r", [P], F32R)
        neg_future_r = place("neg_future_r", [P], F32R)
        neg_before_r = place("neg_before_r", [P], F32R)
        xw_off = cursor[0]
        xw = place("xw", [TB - 1, TPG * P])
        norm_ln, norm_r, norm_m = (xw[:, i, :] for i in range(3))
        assert cursor[0] <= nc.sbuf_usable_end

        merged = at("merged", d_off + KD * TILE, [KD, SEQ])
        v_tok = at("v_tok", d_off, [TB, D])
        qT = at("qT", c_off, [KD, SEQ])
        kT = at("kT", c_off + KD * TILE, [KD, SEQ])
        SBW = 1280
        sb_e = at("sb_e", b_off, [SBW])
        sb_sp = [at(f"sb_sp{i}", b_off + (1 + i) * 5120, [SBW]) for i in range(2)]
        sb_sp_lo = [at(f"sb_sp_lo{i}", b_off + (1 + i) * 5120, [SBW], F32R) for i in range(2)]
        sb_sp_hi = [at("sb_sp_hi0", b_off + 5 * 5120, [SBW], F32R), at("sb_sp_hi1", xw_off, [SBW], F32R)]
        sb_a = [at(f"sb_a{i}", b_off + (3 + i) * 5120, [SBW]) for i in range(2)]
        opM = [at("opM_hi", b_off, [KD, MEM], F32R), at("opM_lo", b_off + KD * TILE // 2, [KD, MEM], F32R)]
        memx = at("memx", b_off + KD * TILE, [KD, MEM])
        xk = at("xk", d_off, [KD, MEM])
        xv_tok = at("xv_tok", d_off + KD * TILE // 2, [MEM // P, D])
        xq = at("xq", c_off, [KD, SEQ])
        x_p = [at(f"x_p{i}", c_off + KD * TILE + i * 4096, [TB, MEM]) for i in range(2)]
        x_pT = at("x_pT", c_off + KD * TILE + 8192, [MEM // P, SEQ])
        hid1 = [at("hid1_hi", b_off, [MLP_HALF, SEQ], F32R), at("hid1_lo", c_off, [MLP_HALF, SEQ], F32R)]
        qk2 = at("qk2", c_off, [12, SEQ])
        kb2 = at("kb2", c_off + 12 * TILE, [B_KV, SEQ])
        va_tok = at("va_tok", d_off, [TB, A_HEADS * HD])
        vb_tok = at("vb_tok", d_off + TB * TILE, [TB, B_KV * HD])
        strip = at("strip", d_off + 16384, [A_HEADS, SEQ])
        at_s = [at(f"at_s{i}", a_off + i * 5120, [SBW]) for i in range(2)]
        at_pT = [at(f"at_pT{i}", a_off + (2 + i) * 5120, [SBW]) for i in range(2)]
        hid2 = [at("hid2_hi", b_off, [KF2, SEQ], F32R), at("hid2_lo", b_off + KF2 * TILE, [KF2, SEQ], F32R)]
        opY = [at("opY_hi", b_off, [2 * KD, SEQ], F32R), at("opY_lo", c_off, [2 * KD, SEQ], F32R)]
        xs = at("xs", d_off, [TPG, SEQ])
        x_tok = at("x_tok", d_off + 8192, [TB, TPG * P])
        bT = at("bT", d_off + 16384, [SEQ])
        cT = at("cT", d_off + 18432, [SEQ])
        b_tok = at("b_tok", d_off + 20480, [TB, SSM_N])
        state = at("state", d_off + 22528, [TB - 1, TPG * P])
        cbm = at("cbm", d_off + 28672, [TB, P])
        zs = at("zs", b_off + 12 * TILE, [TPG, SEQ])
        z_rstd = at("z_rstd", d_off + 30720, [SEQ])
        dt_dtT = at("dt_dtT", d_off + 22528, [SEQ])
        dt_wT = at("dt_wT", d_off + 24576, [SEQ])
        dt_e = at("dt_e", d_off + 26624, [SEQ])
        dt_d = at("dt_d", d_off + 28672, [SEQ])
        dt_m = at("dt_m", d_off + 30720, [SEQ])
        ssm_S, ssm_E = [tmp, tmp2, sig], [sq[0], sq[1], src]
        rstd_m = at("rstd_m", b_off + 24 * 1024, [MEM])

        def col(name, i=0, n=1):
            return par[:, PAR[name] + i:PAR[name] + i + n]

        def const(name, n=P):
            return con[:, CON[name]:CON[name] + n]

        ident = const("ident")
        bank = [ctx.enter_context(nc.psum_tensor(f"bank{i}", [P, SEQ], F32)) for i in range(8)]

        units, tiles, stage = [], [], {}

        def add_tile(w, c0, k0, kt, width=P):
            first = len(units)
            for k in range(0, kt, UNIT_K):
                n = min(UNIT_K, kt - k)
                rows = w[(k0 + k) * P:(k0 + k + n) * P, c0:c0 + width]
                units.append((rows.rearrange("(k p) c -> p k c", p=P), n, width))
            tiles.append((first, len(units) - first, kt, width))

        def begin(name):
            stage[name] = len(tiles)

        w_in = dram["w_in"]
        begin("conv")
        for i in range(KD):
            for part in (0, 2, 1):
                add_tile(w_in, part * D + i * P, 0, KD)

        def gated(name, gate, w_branch):
            begin(name)
            for i in range(KD):
                add_tile(w_in, (7 + gate) * D + i * P, 0, KD)
                add_tile(w_branch, i * P, 0, KD)

        gated("conv_out", 0, dram["w_conv_out"])
        begin("qkv")
        for part in (3, 4, 5):
            for i in range(KD):
                add_tile(w_in, part * D + i * P, 0, KD)
        gated("sb_out", 1, dram["w_sb_out"])
        begin("mem_kv")
        for i in range(2 * KD):
            add_tile(dram["w_mem_kv"], i * P, 0, KD)
        begin("xq")
        for i in range(KD):
            add_tile(w_in, 6 * D + i * P, 0, KD)
        gated("x_out", 2, dram["w_x_out"])
        begin("w_out")
        for i in range(KD):
            add_tile(dram["w_out"], i * P, 0, KD)
        for half in range(FF1 // P // MLP_HALF):
            begin(f"up{half}")
            for i in range(MLP_HALF):
                add_tile(dram["w_up"], (half * MLP_HALF + i) * P, 0, KD)
            begin(f"down{half}")
            for i in range(KD):
                add_tile(dram["w_down"], i * P, half * MLP_HALF, MLP_HALF)
        begin("attn_in")
        AW = A_HEADS * HD // P
        for c in list(range(0, 2 * AW)) + list(range(3 * AW, 4 * AW)) + [4 * AW] + list(range(2 * AW, 3 * AW)) + [4 * AW + 1]:
            add_tile(dram["attn_w_in_2"], c * P, 0, KD)
        begin("attn_out")
        for i in range(KD):
            add_tile(dram["attn_w_out_2"], i * P, 0, KD)

        def ffn_plan(layer):
            w = dram["ffn_w_in_2"]
            begin(f"ffn_in{layer}")
            for i in range(KF2):
                add_tile(w[layer], i * P, 0, KD)
                add_tile(w[layer], FF2 + i * P, 0, KD)
            begin(f"ffn_out{layer}")
            for i in range(KD):
                add_tile(dram["ffn_w_out_2"][layer], i * P, 0, KF2)

        ffn_plan(0)
        SSM_ORDER = (("z", 0), ("b", 0), ("c", 0), ("x", 0), ("z", 1), ("x", 1), ("z", 2), ("x", 2), ("x", 3), ("z", 3))
        begin("dt")
        ssm_w = dram["ssm_w_in_2"]
        add_tile(ssm_w, 2 * SSM_IN + 2 * SSM_G * SSM_N, 0, KD, SSM_HEADS)
        for g in range(SSM_G):
            begin(f"ssm{g}")
            for kind, i in SSM_ORDER:
                c = {"z": g * TPG + i, "x": SSM_IN // P + g * TPG + i, "b": 2 * SSM_IN // P + g, "c": 2 * SSM_IN // P + SSM_G + g}[kind]
                add_tile(ssm_w, c * P, 0, KD)
        begin("ssm_out")
        for i in range(KD):
            add_tile(dram["ssm_w_out_2"], i * P, 0, 2 * KD)
        ffn_plan(1)
        begin("end")
        NU = len(units)

        def last_unit(t):
            return tiles[t][0] + tiles[t][1] - 1

        params_in = sem("params_in")
        con_r_ready = sem("con_r_ready")
        x_in = sem("x_in")
        mem_in = sem("mem_in")
        strip_in = sem("strip_in")
        strip_zone_free = sem("strip_zone_free")
        strip_flipped, strip_turned = sem("strip_flipped"), sem("strip_turned")
        unit_loaded = [sem(f"unit_loaded{i}") for i in range(RAW)]
        hi_ready = sem("hi_ready")
        lo_ready = sem("lo_ready")
        unit_used = sem("unit_used")
        pe_step, dve_step, act_step = sem("pe_step"), sem("dve_step"), sem("act_step")
        op_hi_done = sem("op_hi_done")
        op_ready = sem("op_ready")
        src_ready = sem("src_ready")
        sq_in, sq_ready, sq_used, ss_added, ss_summed = sem("sq_in"), sem("sq_ready"), sem("sq_used"), sem("ss_added"), sem("ss_summed")
        r0_ready, rstd_ready = sem("r0_ready"), sem("rstd_ready")
        sig_in, sig_ready = sem("sig_in"), sem("sig_ready")
        vT_ready, v_turned, v_tok_ready = sem("vT_ready"), sem("v_turned"), sem("v_tok_ready")
        sb_scored, sb_abs_done, sb_exp_ready, sb_sp_ready = sem("sb_scored"), sem("sb_abs_done"), sem("sb_exp_ready"), sem("sb_sp_ready")
        sb_hi_ready, sb_lo_ready = sem("sb_hi_ready"), sem("sb_lo_ready")
        sb_summed, sb_a_ready, sb_pv_done, sb_o_read = sem("sb_summed"), sem("sb_a_ready"), sem("sb_pv_done"), sem("sb_o_read")
        xk_ready, xq_ready = sem("xk_ready"), sem("xq_ready")
        x_scored, x_max_ready, x_exp_ready, x_p_ready = sem("x_scored"), sem("x_max_ready"), sem("x_exp_ready"), sem("x_p_ready")
        x_turned, x_pT_ready, x_pv_done, x_o_read = sem("x_turned"), sem("x_pT_ready"), sem("x_pv_done"), sem("x_o_read")
        at_q_ready = sem("at_q_ready")
        at_scored, at_biased, at_max_ready, at_exp_ready, at_p_ready = sem("at_scored"), sem("at_biased"), sem("at_max_ready"), sem("at_exp_ready"), sem("at_p_ready")
        at_turned, at_pT_ready, at_pv_done, at_o_read = sem("at_turned"), sem("at_pT_ready"), sem("at_pv_done"), sem("at_o_read")
        dt_in, dt_exp, dt_ln_in, dt_ln, dt_acs, dt_w = sem("dt_in"), sem("dt_exp"), sem("dt_ln_in"), sem("dt_ln"), sem("dt_acs"), sem("dt_w")
        dt_ready, dt_turned = sem("dt_ready"), sem("dt_turned")
        xs_ready, xs_turned, x_tok_ready = sem("xs_ready"), sem("xs_turned"), sem("x_tok_ready")
        cb_done, xw_ready, upd_done, state_ready, cb_ready = sem("cb_done"), sem("xw_ready"), sem("upd_done"), sem("state_ready"), sem("cb_ready")
        row_done, row_masked, e_ready, s_ready, ec_ready, g_ready, y_done, y_read = sem("row_done"), sem("row_masked"), sem("e_ready"), sem("s_ready"), sem("ec_ready"), sem("g_ready"), sem("y_done"), sem("y_read")
        dt_tok_ready, pool_step = sem("dt_tok_ready"), sem("pool_step")
        z_taken = sem("z_taken")
        out_ready, stored = sem("out_ready"), sem("stored")

        SQUARES_BEFORE_ATTN = 4 * KD + 2 * KD
        generation, made = {}, [0]

        def operand(name, n):
            generation[name] = made[0]
            made[0] += n

        for name, n in (("x1", KD), ("conv", KD), ("sb", KD), ("mem", KD), ("xo", KD), ("merged", KD), ("x2", KD),
                        ("hid1_0", MLP_HALF), ("hid1_1", MLP_HALF), ("x3", KD), ("attn", KD), ("x4", KD),
                        ("ffn0", KF2), ("x5", KD), ("ssm", 2 * KD), ("x6", KD), ("ffn1", KF2)):
            operand(name, n)

        A_SCORES = ((3, 0, 4, 0, 0), (2, 0, 3, 1, 0), (0, 0, 1, 1, 384), (1, 0, 2, 2, 0))
        B_SCORES = ((1, 0, 2, 0, 0), (2, 1, 2, 0, 256), (3, 2, 2, 1, 0), (0, 0, 1, 1, 256))
        A_TURNED = ((0, 0, 4, 0, 0), (1, 1, 3, 1, 0), (3, 3, 1, 1, 384), (2, 2, 2, 2, 0))
        B_TURNED = ((0, 0, 2, 0, 0), (1, 1, 2, 0, 256), (2, 2, 2, 1, 0), (3, 3, 1, 1, 256))
        A_SPANS, B_SPANS = ((0, 512), (1, 512), (2, 256)), ((0, 512), (1, 384))

        SB_OFF = (0, 512, 1024, 896)
        SB_BANK = ((0, 0), (1, 0), (2, 0), (1, 384))

        block = ctx.enter_context(nc.Block())

        @block.sync
        def _(sp):
            sp.dma_start(par[:, :], dram["par"]).then_inc(params_in, 16)
            sp.dma_start(con[:, :], dram["con"]).then_inc(params_in, 16)
            for k in range(0, KD, 2):
                sp.dma_start(x[:, k:k + 2, :], dram["xT"][:, k:k + 2, :]).then_inc(x_in, 16)

            for u, (rows, n, width) in enumerate(units):
                if u >= RAW:
                    sp.wait_ge(lo_ready, u - RAW + 1)
                sp.dma_start(raw[u % RAW][:, 0:n, 0:width], rows).then_inc(unit_loaded[u % RAW], 16)
                if u == tiles[stage["sb_out"]][0] + 4:
                    sp.wait_ge(sb_a_ready, 3 * SB_HEADS)
                    sp.wait_ge(sb_pv_done, SB_HEADS)
                    sp.dma_start(memx[:, :, :], dram["memT"]).then_inc(mem_in, 16)
                if u == tiles[stage["up0"]][0] + 4:
                    E = dram["rel"]
                    sp.wait_ge(strip_zone_free, 1)
                    sp.dma_start(strip[:, :, :], bass.AP(E.tensor, 0, [[1, P], [STRIP_E, A_HEADS], [1, SEQ]])).then_inc(strip_in, 16)
            for k in range(KD):
                sp.wait_ge(out_ready, k + 1)
                sp.dma_start(out[:, k, :], x[:, k, :]).then_inc(stored, 16)
            sp.wait_ge(stored, 16 * KD)

        @block.tensor
        def _(pe):
            lane = Lane(pe, pe_step)
            seen = {"op": 0, "sum": 0, "added": 0, "sq": SQUARES_BEFORE_ATTN}

            def tile(t, op, gen, n=SEQ):
                u0, nu, kt, width = tiles[t]
                dst = bank[t % 4][0:width, 0:n]
                for j in range(nu):
                    u = u0 + j
                    pe.wait_ge(lo_ready, u + 1)
                    for k in range(units[u][1]):
                        kk = j * UNIT_K + k
                        need = generation[gen] + kk + 1
                        if need > seen["op"]:
                            pe.wait_ge(op_ready, need)
                            seen["op"] = need
                        wh, wl = w_hi[u % SPLIT][:, k, 0:width], w_lo[u % SPLIT][:, k, 0:width]
                        pe.matmul(dst, wh, op[0][:, kk, 0:n], start=(kk == 0), stop=False)
                        pe.matmul(dst, wh, op[1][:, kk, 0:n], start=False, stop=False)
                        mm = pe.matmul(dst, wl, op[0][:, kk, 0:n], start=False, stop=(kk == kt - 1))
                    mm.then_inc(unit_used, 1)

            def head_norm_sum(k):
                i = seen["sum"]
                seen["sum"] += 1
                pe.wait_ge(sq_ready, seen["sq"] + k + 1)
                pe.wait_ge(rstd_ready, i)
                pe.matmul(bank[4][:, :], const("head_ones"), sq[k % 2][:, :], start=True, stop=True).then_inc(ss_summed, 1)

            def norm_sum(n=SEQ, ones="ones"):
                i = seen["sum"]
                seen["sum"] += 1
                seen["added"] += 1
                pe.wait_ge(ss_added, seen["added"])
                if i:
                    pe.wait_ge(rstd_ready, i)
                pe.matmul(bank[4][:, 0:n], const(ones), ss[:, 0:n], start=True, stop=True).then_inc(ss_summed, 1)

            def turn(srcs, dst, ready, ready_n, free, free_n, done):
                pe.wait_ge(ready, ready_n)
                if free_n > 0:
                    pe.wait_ge(free, free_n)
                for i, s in enumerate(srcs):
                    mm = pe.transpose(dst[:, i * P:(i + 1) * P], s, ident)
                mm.then_inc(done, 1)

            pe.wait_ge(params_in, 32)
            pe.wait_ge(con_r_ready, 5)
            t = stage["conv"]
            for i in range(3 * KD):
                tile(t + i, opA, "x1")
                if i == 0:
                    norm_sum()
            t = stage["conv_out"]
            for i in range(KD):
                tile(t + 2 * i, opA, "x1")
                tile(t + 2 * i + 1, opB, "conv")
            t = stage["qkv"]
            vi = 0

            def turn_v(n, blocks):
                vt = tmp if n % 2 == 0 else tmp2
                turn([vt[:, b * P:(b + 1) * P] for b in range(blocks)], bank[5 + n % 2], vT_ready, n + 1, v_tok_ready, n - 1, v_turned)

            for i in range(3 * KD):
                tile(t + i, opA, "x1")
                if i > 2 * KD:
                    turn_v(vi, TB)
                    vi += 1
            turn_v(vi, TB)
            vi += 1

            def sb_scores(h):
                r, j, s = HD * (h % 2), h // 2, 4 * (h % 2)
                if h >= 2:
                    pe.wait_ge(sb_a_ready, 3 * (h - 1))
                for kb in range(TB):
                    b, c = SB_BANK[kb]
                    mm = pe.matmul(bank[s + b][:, c:c + SEQ - kb * P], kT[r:r + HD, j, kb * P:(kb + 1) * P],
                                   qT[r:r + HD, j, kb * P:SEQ], start=(c == 0), stop=False, skip_group_check=True)
                mm.then_inc(sb_scored, 1)

            def sb_sums(h):
                s = 4 * (h % 2)
                pe.wait_ge(sb_lo_ready, h + 1)
                for kb in range(TB):
                    b, c = SB_BANK[kb]
                    n = SEQ - kb * P
                    dst = bank[s + b]
                    for sp_ in (sb_sp_hi[h % 2], sb_sp_lo[h % 2]):
                        pe.matmul(dst[:, c:c + n], neg_later_r[:, :], sp_[:, SB_OFF[kb]:SB_OFF[kb] + n], start=False, stop=False, skip_group_check=True)
                        for later in range(kb + 1, TB):
                            m = SEQ - later * P
                            pe.matmul(dst[:, c + n - m:c + n], neg_ones_r[:, :], sp_[:, SB_OFF[later]:SB_OFF[later] + m], start=False, stop=False, skip_group_check=True)
                    mm = pe.matmul(dst[:, c:c + P], ident_r[:, :], neg_future_r[:, :], start=False, stop=True, skip_group_check=True)
                mm.then_inc(sb_summed, 1)

            def sb_values(h):
                pe.wait_ge(sb_a_ready, 3 * (h + 1))
                if h >= 2:
                    pe.wait_ge(sb_o_read, h - 1)
                dst = bank[3 + 4 * (h % 2)]
                for kb in range(TB):
                    n = SEQ - kb * P
                    mm = pe.matmul(dst[0:HD, kb * P:SEQ], v_tok[:, kb, h * HD:(h + 1) * HD], sb_a[h % 2][:, SB_OFF[kb]:SB_OFF[kb] + n],
                                   start=(kb == 0), stop=(kb == TB - 1))
                mm.then_inc(sb_pv_done, 1)

            pe.wait_ge(v_tok_ready, vi)
            pe.wait_ge(vT_ready, vi)
            pe.wait_ge(rstd_ready, seen["sum"])
            sb_scores(0)
            for h in range(SB_HEADS):
                if h + 1 < SB_HEADS:
                    sb_scores(h + 1)
                sb_sums(h)
                if h >= 1:
                    sb_values(h - 1)
            sb_values(SB_HEADS - 1)
            pe.wait_ge(sb_o_read, SB_HEADS)
            t = stage["sb_out"]
            for i in range(KD):
                tile(t + 2 * i, opA, "x1")
                tile(t + 2 * i + 1, opC, "sb")
            t = stage["mem_kv"]
            for i in range(2 * KD):
                tile(t + i, opM, "mem", MEM)
                if i == 0 or (i <= KD and i % 2 == 0):
                    norm_sum(MEM)
                if i > KD:
                    turn_v(vi, MEM // P)
                    vi += 1
            turn_v(vi, MEM // P)
            vi += 1
            t = stage["xq"]
            for i in range(KD):
                tile(t + i, opA, "x1")
                if i and i % 2 == 0:
                    norm_sum()
            norm_sum()
            pe.wait_ge(xq_ready, KD)
            pe.wait_ge(v_tok_ready, vi)

            def x_scores(h):
                if h >= 1:
                    pe.wait_ge(x_exp_ready, TB * h)
                for qb in range(TB):
                    for d in range(2):
                        mm = pe.matmul(bank[qb // 2][:, (qb % 2) * MEM:(qb % 2 + 1) * MEM], xq[:, 2 * h + d, qb * P:(qb + 1) * P],
                                       xk[:, 2 * h + d, :], start=(d == 0), stop=(d == 1))
                mm.then_inc(x_scored, 1)

            x_scores(0)
            for h in range(X_HEADS):
                pe.wait_ge(x_p_ready, h + 1)
                if h >= 1:
                    pe.wait_ge(x_pT_ready, 2 * h)
                for kb in range(2):
                    for qb in range(TB):
                        mm = pe.transpose(bank[2 + kb][:, qb * P:(qb + 1) * P], x_p[h % 2][:, qb, kb * P:(kb + 1) * P], ident)
                    mm.then_inc(x_turned, 1)
                if h + 1 < X_HEADS:
                    x_scores(h + 1)
                pe.wait_ge(x_pT_ready, 2 * h + 2)
                for d in range(2):
                    n = 2 * h + d
                    if n >= 2:
                        pe.wait_ge(x_o_read, n - 1)
                    for kb in range(2):
                        mm = pe.matmul(bank[5 + d][:, :], xv_tok[:, kb, n * P:(n + 1) * P], x_pT[:, kb, :], start=(kb == 0), stop=(kb == 1))
                    mm.then_inc(x_pv_done, 1)
            t = stage["x_out"]
            for i in range(KD):
                tile(t + 2 * i, opA, "x1")
                tile(t + 2 * i + 1, opB, "xo")
            t = stage["w_out"]
            for i in range(KD):
                tile(t + i, opC, "merged")
            for half in range(FF1 // P // MLP_HALF):
                t = stage[f"up{half}"]
                for i in range(MLP_HALF):
                    tile(t + i, opA, "x2")
                    if half == 0 and i == 0:
                        norm_sum()
                if half == 0:
                    pe.wait_ge(strip_in, 16)
                    for h in range(A_HEADS):
                        if h >= 2:
                            pe.wait_ge(strip_turned, h - 1)
                        pe.matmul(bank[5 + h % 2][:, :], const("flip"), strip[:, h, :], start=True, stop=True).then_inc(strip_flipped, 1)
                t = stage[f"down{half}"]
                for i in range(KD):
                    tile(t + i, hid1, f"hid1_{half}")
            t = stage["attn_in"]
            order = [0] * (3 * AW + 1) + [1] * (AW + 1)
            for i, is_v in enumerate(order):
                tile(t + i, opA, "x3")
                if i == 0:
                    norm_sum()
                if 1 <= i <= 3 * AW + 1:
                    head_norm_sum(i - 1)
                if i > 3 * AW + 1:
                    turn_v(vi, TB)
                    vi += 1
            turn_v(vi, TB)
            vi += 1
            pe.wait_ge(at_q_ready, 3 * AW + 1)
            pe.wait_ge(v_tok_ready, vi)
            pe.wait_ge(vT_ready, vi)
            pe.wait_ge(rstd_ready, seen["sum"])

            AH = A_HEADS + B_HEADS

            def at_scores(h):
                r = HD * (h % 2)
                if h < A_HEADS:
                    q, k = qk2[r:r + HD, h // 2, :], qk2[r:r + HD, AW + h // 2, :]
                else:
                    q, k = qk2[r:r + HD, 2 * AW + (h - A_HEADS) // 2, :], kb2[r:r + HD, (h - A_HEADS) // (B_HEADS // B_KV), :]
                if h:
                    pe.wait_ge(at_biased, h)
                for qb, k0, nk, b, c in A_SCORES if h < A_HEADS else B_SCORES:
                    mm = pe.matmul(bank[b][:, c:c + nk * P], q[:, qb * P:(qb + 1) * P], k[:, k0 * P:(k0 + nk) * P], start=True, stop=True)
                mm.then_inc(at_scored, 1)

            def at_turn(h):
                pe.wait_ge(at_p_ready, h + 1)
                if h:
                    pe.wait_ge(at_pT_ready, h)
                for qb, k0, nk, b, c in A_SCORES if h < A_HEADS else B_SCORES:
                    for i in range(nk):
                        tb, tc = next((tb, tc + (qb - q0) * P) for kb, q0, _, tb, tc in (A_TURNED if h < A_HEADS else B_TURNED) if kb == k0 + i)
                        o = b * SEQ + c + i * P
                        mm = pe.transpose(bank[3 + tb][:, tc:tc + P], at_s[h % 2][:, o:o + P], ident)
                mm.then_inc(at_turned, 1)

            def at_values(h):
                pe.wait_ge(at_pT_ready, h + 1)
                if h >= 2:
                    pe.wait_ge(at_o_read, h - 1)
                for kb, q0, nq, b, c in sorted(A_TURNED if h < A_HEADS else B_TURNED):
                    if h < A_HEADS:
                        v = va_tok[:, kb, h * HD:(h + 1) * HD]
                    else:
                        g = (h - A_HEADS) // (B_HEADS // B_KV)
                        v = vb_tok[:, kb, g * HD:(g + 1) * HD]
                    mm = pe.matmul(bank[6 + h % 2][0:HD, q0 * P:(q0 + nq) * P], v, at_pT[h % 2][:, b * SEQ + c:b * SEQ + c + nq * P],
                                   start=(kb == 0), stop=(kb == TB - 1), skip_group_check=True)
                mm.then_inc(at_pv_done, 1)

            at_scores(0)
            at_scores(1)
            for h in range(AH):
                at_turn(h)
                if h + 2 < AH:
                    at_scores(h + 2)
                at_values(h)
            t = stage["attn_out"]
            for i in range(KD):
                tile(t + i, opB, "attn")

            def ffn(layer, gen_in, gen_mid):
                t = stage[f"ffn_in{layer}"]
                for i in range(2 * KF2):
                    tile(t + i, opA, gen_in)
                    if i == 0:
                        norm_sum()
                t = stage[f"ffn_out{layer}"]
                for i in range(KD):
                    tile(t + i, hid2, gen_mid)

            ffn(0, "x4", "ffn0")
            tile(stage["dt"], opA, "x5")
            norm_sum()
            for g in range(SSM_G):
                t = stage[f"ssm{g}"]
                bank_x = g * 5

                def turn_x(j):
                    n = bank_x + j
                    s = bT if j == 0 else xs[:, j - 1, :]
                    pe.wait_ge(xs_ready, g * 6 + (1 if j == 0 else j + 2))
                    if n >= 2:
                        pe.wait_ge(x_tok_ready, n - 1)
                    for c in range(TB):
                        mm = pe.transpose(bank[5 + n % 2][:, c * P:(c + 1) * P], s[:, c * P:(c + 1) * P], ident)
                    mm.then_inc(xs_turned, 1)

                for j in range(len(SSM_ORDER)):
                    tile(t + j, opA, "x5")
                    if j == 1 and g:
                        norm_sum()
                    if j == 2:
                        turn_x(0)
                        if g == 0:
                            pe.wait_ge(dt_ready, 1)
                            for c in range(TB):
                                for k, row in enumerate((dt_acsT, dt_dtT, dt_wT)):
                                    o = (k * TB + c) * SSM_HEADS
                                    pe.transpose(bank[7][:, o:o + SSM_HEADS], row[0:SSM_HEADS, c * P:(c + 1) * P], ident[0:SSM_HEADS, 0:SSM_HEADS])
                            pe.matmul(bank[7][:, 3 * TB * SSM_HEADS:], const("ones")[0:SSM_HEADS, :], dt_last[0:SSM_HEADS, :], start=True, stop=True).then_inc(dt_turned, 1)
                    if j == 4:
                        pe.wait_ge(xs_ready, g * 6 + 2)
                        if g == 0:
                            pe.wait_ge(dt_tok_ready, 3)
                        for c in range(TB):
                            mm = pe.matmul(bank[7][:, c * P:(c + 1) * P], bT[:, c * P:(c + 1) * P], cT[:, c * P:(c + 1) * P], start=True, stop=True)
                        mm.then_inc(cb_done, 1)
                        turn_x(1)
                    if j in (6, 8):
                        turn_x(j // 2 - 1)
                turn_x(TPG)

                def head_row(h):
                    n = g * HPG + h
                    if n >= 2:
                        pe.wait_ge(s_ready, n - 1)
                    sel = ident[0:SSM_HEADS, n:n + 1].to_broadcast([SSM_HEADS, P])
                    pe.matmul(bank[4 - n % 2][:, :], sel, dt_acsT[0:SSM_HEADS, :], start=True, stop=False, skip_group_check=True).then_inc(row_done, 1)

                def head_mask(h):
                    n = g * HPG + h
                    pe.wait_ge(e_ready, n + 1)
                    mask = neg_before_r[:, :].rearrange("p (o l) -> p o l", o=1).to_broadcast([P, TB, P])
                    pe.matmul(bank[4 - n % 2][:, :], ident_r[:, :], mask, start=False, stop=True, skip_group_check=True).then_inc(row_masked, 1)

                def head_out(h):
                    n = g * HPG + h
                    pe.wait_ge(g_ready, n + 1)
                    pe.wait_ge(ec_ready, n + 1)
                    if n >= 2:
                        pe.wait_ge(y_read, n - 1)
                    for c in range(TB):
                        dst = bank[5 + n % 2][0:SSM_P, c * P:(c + 1) * P]
                        mm = pe.matmul(dst, x_tok[:, c, h * SSM_P:(h + 1) * SSM_P], ssm_S[n % 3][:, c * P:(c + 1) * P], start=True, stop=(c == 0))
                        if c:
                            mm = pe.matmul(dst, state[:, c - 1, h * SSM_P:(h + 1) * SSM_P], ssm_E[n % 3][:, c * P:(c + 1) * P], start=False, stop=True)
                    mm.then_inc(y_done, 1)

                pe.wait_ge(rstd_ready, seen["sum"])
                head_row(0)
                pe.wait_ge(z_taken, TPG * (g + 1))
                head_row(1)
                pe.wait_ge(x_tok_ready, bank_x + 5)
                pe.wait_ge(cb_ready, g + 1)
                pe.wait_ge(xw_ready, (g + 1) * TPG)
                for c in range(TB - 1):
                    pe.matmul(bank[5 + c][:, :], b_tok[:, c, :], xw[:, c, :], start=True, stop=True).then_inc(upd_done, 1)
                head_mask(0)
                head_mask(1)
                pe.wait_ge(state_ready, (g + 1) * (TB - 1))
                for h in range(HPG):
                    if h + 2 < HPG:
                        head_row(h + 2)
                    head_out(h)
                    if h + 2 < HPG:
                        head_mask(h + 2)
            norm_sum()
            t = stage["ssm_out"]
            for i in range(KD):
                tile(t + i, opY, "ssm")
            ffn(1, "x6", "ffn1")

        @block.scalar
        def _(act):
            lane = Lane(act, act_step)
            n_ = {"src": 0, "sq": 0, "used": 0, "norm": 0, "sig": 0, "v": 0, "sq_in": 0, "hi": 0}
            act.preload_act_table_set("natural_log_exp_and_others")

            def split(u):
                if u >= NU:
                    return
                _, kt, width = units[u]
                act.wait_ge(unit_loaded[u % RAW], 16 * (u // RAW + 1))
                if u >= SPLIT:
                    act.wait_ge(unit_used, u - SPLIT + 1)
                act.activation(w_hi[u % SPLIT][:, 0:kt, 0:width], raw[u % RAW][:, 0:kt, 0:width], ACT.Copy).then_inc(hi_ready, 1)

            def ahead(t):
                u0, nu, _, _ = tiles[t]
                for u in range(u0, u0 + nu):
                    split(u + 2)

            def high(dst, source, ready=None, ready_n=None):
                if ready is None:
                    n_["src"] += 1
                    act.wait_ge(src_ready, n_["src"])
                else:
                    act.wait_ge(ready, ready_n)
                act.activation(dst, source, ACT.Copy).then_inc(op_hi_done, 1)

            def square(source, m):
                if m == 0 and n_["norm"]:
                    act.wait_ge(rstd_ready, n_["norm"])
                if m >= 2:
                    act.wait_ge(sq_used, n_["used"] + m - 1)
                n = source.shape[-1]
                act.activation(sq[m % 2][:, 0:n], source, ACT.Square).then_inc(sq_ready, 1)

            def root(n, count, width):
                n_["norm"] += 1
                n_["used"] += count - 1
                act.wait_ge(ss_summed, n_["norm"])
                eps = con[:, CON["eps"]:CON["eps"] + 1]
                lane.did(act.activation(norm_ln[:, 0:n], bank[4][:, 0:n], ACT.Ln, bias=eps, scale=1.0 / width))
                lane.did(act.activation(norm_m[:, 0:n], bank[4][:, 0:n], ACT.Identity, bias=eps, scale=1.0 / width))
                lane.sync()
                act.activation(norm_r[:, 0:n], norm_ln[:, 0:n], ACT.Exp, scale=-0.5).then_inc(r0_ready, 1)

            def prepare(k, gain, source=None, dst=opA, first=False):
                if source is None:
                    if not first:
                        n_["src"] += 1
                        act.wait_ge(src_ready, n_["src"])
                    source = x[:, k, :]
                act.activation(dst[0][:, k, :], source, ACT.Copy, scale=gain).then_inc(op_hi_done, 1)
                square(source, k)

            def gate():
                n_["sig"] += 1
                act.wait_ge(sig_in, n_["sig"])
                act.activation(sig[:, :], tmp[:, :], ACT.Sigmoid).then_inc(sig_ready, 1)

            def gated(name, last=False):
                t = stage[name]
                for i in range(KD):
                    ahead(t + 2 * i)
                    gate()
                    ahead(t + 2 * i + 1)
                    if last:
                        high(opC[0][:, i, :], src[:, :])
                act.preload_act_table_set("natural_log_exp_and_others")

            def v_out(dst, blocks):
                n = n_["v"]
                n_["v"] += 1
                act.wait_ge(v_turned, n + 1)
                act.activation(dst, bank[5 + n % 2][:, 0:blocks * P].rearrange("p (b c) -> p b c", c=P), ACT.Copy).then_inc(v_tok_ready, 1)

            act.wait_ge(params_in, 32)
            split(0)
            split(1)
            for dst, name in ((ident_r, "ident"), (neg_later_r, "neg_later"), (neg_ones_r, "neg_ones"), (neg_future_r, "neg_future"), (neg_before_r, "neg_before")):
                act.activation(dst[:, :], const(name), ACT.Copy).then_inc(con_r_ready, 1)
            act.wait_ge(x_in, 16 * (KD // 2))
            for k in range(KD):
                prepare(k, col("g_mix", k), first=True)
            root(SEQ, KD, D)
            t = stage["conv"]
            for i in range(KD):
                for j in range(3):
                    ahead(t + 3 * i + j)
                high(opB[0][:, i, :], src[:, :])
            gated("conv_out")
            t = stage["qkv"]
            for i in range(3 * KD):
                ahead(t + i)
                if i > 2 * KD:
                    v_out(v_tok[:, :, (i - 1 - 2 * KD) * P:(i - 2 * KD) * P], TB)
            v_out(v_tok[:, :, (KD - 1) * P:KD * P], TB)

            SPANS = ((0, 0, 512), (1, 512, 512), (2, 1024, 256))

            def sb_soft(h):
                act.wait_ge(sb_scored, h + 1)
                if h:
                    act.wait_ge(sb_sp_ready, h)
                for b, c, w in SPANS:
                    lane.did(act.activation(sb_e[:, c:c + w], bank[4 * (h % 2) + b][:, 0:w], ACT.Abs), sb_abs_done)
                lane.sync()
                for b, c, w in SPANS:
                    lane.did(act.activation(sb_e[:, c:c + w], sb_e[:, c:c + w], ACT.Exp, scale=-1.0))
                lane.sync()
                for b, c, w in SPANS:
                    act.activation(sb_e[:, c:c + w], sb_e[:, c:c + w], ACT.Ln, bias=1.0).then_inc(sb_exp_ready, 1)

            def sb_weights(h):
                act.wait_ge(sb_summed, h + 1)
                if h >= 2:
                    act.wait_ge(sb_pv_done, h - 1)
                for b, c, w in SPANS:
                    act.activation(sb_a[h % 2][:, c:c + w], bank[4 * (h % 2) + b][:, 0:w], ACT.Exp).then_inc(sb_a_ready, 1)

            def sb_high(h):
                if h % 2:
                    high(opC[0][:, h // 2, :], src[:, :], sb_o_read, h + 1)

            def sb_sp_high(h):
                act.wait_ge(sb_sp_ready, h + 1)
                act.activation(sb_sp_hi[h % 2][:, :], sb_sp[h % 2][:, :], ACT.Copy).then_inc(sb_hi_ready, 1)

            sb_soft(0)
            sb_sp_high(0)
            for h in range(SB_HEADS):
                if h + 1 < SB_HEADS:
                    sb_soft(h + 1)
                sb_weights(h)
                if h >= 1:
                    sb_high(h - 1)
                if h + 1 < SB_HEADS:
                    sb_sp_high(h + 1)
            sb_high(SB_HEADS - 1)
            gated("sb_out")
            act.wait_ge(mem_in, 16)
            for k in range(KD):
                prepare(k, col("g_mem", k), memx[:, k, :], opM)
            root(MEM, KD, D)
            t = stage["mem_kv"]
            for i in range(2 * KD):
                ahead(t + i)
                if i < KD:
                    n_["sq_in"] += 1
                    act.wait_ge(sq_in, n_["sq_in"])
                    square(xk[:, i, :], i % 2)
                    if i % 2:
                        root(MEM, 2, X_DIM)
                if i > KD:
                    v_out(xv_tok[:, :, (i - 1 - KD) * P:(i - KD) * P], MEM // P)
            v_out(xv_tok[:, :, (KD - 1) * P:KD * P], MEM // P)
            t = stage["xq"]
            for i in range(KD):
                ahead(t + i)
                n_["sq_in"] += 1
                act.wait_ge(sq_in, n_["sq_in"])
                square(xq[:, i, :], i % 2)
                if i % 2:
                    root(SEQ, 2, X_DIM)

            XS = float(X_DIM) ** -0.5

            def x_exp(h):
                act.wait_ge(x_max_ready, h + 1)
                if h >= 2:
                    act.wait_ge(x_turned, 2 * (h - 1))
                o = 32 * (h % 2)
                for qb in range(TB):
                    act.activation(x_p[h % 2][:, qb, :], bank[qb // 2][:, (qb % 2) * MEM:(qb % 2 + 1) * MEM], ACT.Exp,
                                   bias=small[:, o + TB + qb:o + TB + qb + 1], scale=XS,
                                   accum_out=small[:, o + 2 * TB + qb:o + 2 * TB + qb + 1]).then_inc(x_exp_ready, 1)

            x_exp(0)
            for h in range(X_HEADS):
                for kb in range(2):
                    act.wait_ge(x_turned, 2 * h + kb + 1)
                    if h:
                        act.wait_ge(x_pv_done, 2 * h)
                    act.activation(x_pT[:, kb, :], bank[2 + kb][:, :], ACT.Copy).then_inc(x_pT_ready, 1)
                if h + 1 < X_HEADS:
                    x_exp(h + 1)
                for d in range(2):
                    high(opB[0][:, 2 * h + d, :], src[:, :], x_o_read, 2 * h + d + 1)
            gated("x_out", last=True)

            def residual(name, gain=None, width_g=None):
                t = stage[name]
                for i in range(KD):
                    ahead(t + i)
                    if gain is not None:
                        prepare(i, col(*gain[0:1], gain[1] + i))
                if gain is not None:
                    root(SEQ, KD, D)

            residual("w_out", ("g_mlp", 0))
            for half in range(FF1 // P // MLP_HALF):
                t = stage[f"up{half}"]
                for i in range(MLP_HALF):
                    ahead(t + i)
                    high(hid1[0][:, i, :], src[:, :])
                if half == 0:
                    for h in range(A_HEADS):
                        act.wait_ge(strip_flipped, h + 1)
                        act.activation(strip[:, h, :], bank[5 + h % 2][:, :], ACT.Copy).then_inc(strip_turned, 1)
                residual(f"down{half}", ("norm_mix_2", 0) if half else None)
            t = stage["attn_in"]
            for i in range(4 * AW + 2):
                ahead(t + i)
                if i <= 3 * AW:
                    n_["sq_in"] += 1
                    act.wait_ge(sq_in, n_["sq_in"])
                    if i >= 2:
                        act.wait_ge(ss_summed, n_["norm"])
                    act.activation(sq[i % 2][:, :], qk2[:, i, :] if i < 3 * AW else src[:, :], ACT.Square).then_inc(sq_ready, 1)
                if 1 <= i <= 3 * AW + 1:
                    root(SEQ, 1, HD)
                if i > 3 * AW + 1:
                    j = i - 1 - (3 * AW + 1)
                    v_out(va_tok[:, :, j * P:(j + 1) * P], TB)
            v_out(vb_tok[:, :, :], TB)

            AH = A_HEADS + B_HEADS

            def at_exp(h):
                act.wait_ge(at_max_ready, h + 1)
                o = 32 * (h % 2)
                for qb, _, nk, b, c in A_SCORES if h < A_HEADS else B_SCORES:
                    s_ = at_s[h % 2][:, b * SEQ + c:b * SEQ + c + nk * P]
                    act.activation(s_, s_, ACT.Exp, bias=small[:, o + TB + qb:o + TB + qb + 1],
                                   accum_out=small[:, o + 2 * TB + qb:o + 2 * TB + qb + 1]).then_inc(at_exp_ready, 1)
                if h >= A_HEADS:
                    act.activation(small[:, o + 3 * TB:o + 4 * TB], small[:, o + TB:o + 2 * TB], ACT.Exp, bias=col("sinks_2", h - A_HEADS)).then_inc(at_exp_ready, 1)

            at_exp(0)
            at_exp(1)
            for h in range(AH):
                act.wait_ge(at_turned, h + 1)
                if h >= 2:
                    act.wait_ge(at_pv_done, h - 1)
                spans = A_SPANS if h < A_HEADS else B_SPANS
                for b, n in spans:
                    ins = act.activation(at_pT[h % 2][:, b * SEQ:b * SEQ + n], bank[3 + b][:, 0:n], ACT.Copy)
                    if b == len(spans) - 1:
                        ins.then_inc(at_pT_ready, 1)
                    else:
                        lane.did(ins)
                        if b == len(spans) - 2:
                            lane.sync()
                if h and h % 2 == 0:
                    high(opB[0][:, (h - 1) // 2, :], src[:, :], at_o_read, h)
                if h + 2 < AH:
                    at_exp(h + 2)
            high(opB[0][:, KD - 1, :], src[:, :], at_o_read, AH)
            residual("attn_out", ("norm_ffn_2", 0))

            def ffn(layer, after):
                t = stage[f"ffn_in{layer}"]
                for i in range(KF2):
                    ahead(t + 2 * i)
                    gate()
                    ahead(t + 2 * i + 1)
                    high(hid2[0][:, i, :], src[:, :])
                act.preload_act_table_set("natural_log_exp_and_others")
                residual(f"ffn_out{layer}", after)

            ffn(0, ("norm_mix_2", KD))
            S32 = SSM_HEADS
            ahead(stage["dt"])
            act.wait_ge(dt_in, 1)
            lane.did(act.activation(dt_e[0:S32, :], dt_m[0:S32, :], ACT.Abs))
            lane.did(act.activation(small[0:S32, 0:1], col("a_log")[0:S32, :], ACT.Exp))
            lane.sync()
            act.activation(dt_e[0:S32, :], dt_e[0:S32, :], ACT.Exp, scale=-1.0).then_inc(dt_exp, 1)
            act.wait_ge(dt_ln_in, 1)
            act.activation(dt_wT[0:S32, :], dt_d[0:S32, :], ACT.Ln).then_inc(dt_ln, 1)
            act.wait_ge(dt_acs, TB)
            for c in range(TB):
                act.activation(dt_wT[0:S32, c * P:(c + 1) * P], dt_acsT[0:S32, c * P:(c + 1) * P], ACT.Exp,
                               bias=dt_acsT[0:S32, c * P + P - 1:c * P + P], scale=-1.0).then_inc(dt_w, 1)
            xt = [0]

            def x_out_tok(dst):
                n = xt[0]
                xt[0] += 1
                act.wait_ge(xs_turned, n + 1)
                act.activation(dst, bank[5 + n % 2][:, :].rearrange("p (b c) -> p b c", c=P), ACT.Copy).then_inc(x_tok_ready, 1)

            for g in range(SSM_G):
                t = stage[f"ssm{g}"]
                for j, (kind, i) in enumerate(SSM_ORDER):
                    ahead(t + j)
                    if kind == "x" and g:
                        high(opY[0][:, (g - 1) * TPG + i, :], src[:, :])
                    gate()
                    if j == 1 and g:
                        act.preload_act_table_set("natural_log_exp_and_others")
                        root(SEQ, TPG, SSM_IN // SSM_G)
                    if j == 2:
                        x_out_tok(b_tok[:, :, :])
                        if g == 0:
                            act.wait_ge(dt_turned, 1)
                            n = TB * S32
                            act.activation(dt_tok[:, 0, :, :].rearrange("p b c -> p (b c)"), bank[7][:, 0:n], ACT.Copy, scale=-1.0).then_inc(dt_tok_ready, 1)
                            act.activation(dt_tok[:, 1:3, :, :].rearrange("p a b c -> p (a b c)"), bank[7][:, n:3 * n], ACT.Copy).then_inc(dt_tok_ready, 1)
                            act.activation(e_last[:, :, :].rearrange("p b c -> p (b c)"), bank[7][:, 3 * n:], ACT.Exp).then_inc(dt_tok_ready, 1)
                    if j in (4, 6, 8):
                        x_out_tok(x_tok[:, :, (j // 2 - 2) * P:(j // 2 - 1) * P])
                act.preload_act_table_set("natural_log_exp_and_others")
                x_out_tok(x_tok[:, :, (TPG - 1) * P:TPG * P])

                def decay(h):
                    n = g * HPG + h
                    row = bank[4 - n % 2]
                    act.wait_ge(row_done, n + 1)
                    if n >= 3:
                        act.wait_ge(y_done, n - 2)
                    act.activation(ssm_E[n % 3][:, :], row[:, :], ACT.Exp).then_inc(e_ready, 1)
                    act.wait_ge(row_masked, n + 1)
                    for c in range(TB):
                        cc = slice(c * P, (c + 1) * P)
                        ins = act.activation(ssm_S[n % 3][:, cc], row[:, cc], ACT.Exp, bias=dt_tok[:, 0, c, n:n + 1])
                        if c == TB - 1:
                            ins.then_inc(s_ready, 1)
                        else:
                            lane.did(ins)
                            if c == TB - 2:
                                lane.sync()

                for h in range(HPG):
                    decay(h)
                n_["sq_in"] += TPG
                act.wait_ge(sq_in, n_["sq_in"])
                for j in range(TPG):
                    square(xs[:, j, :], j)
            root(SEQ, TPG, SSM_IN // SSM_G)
            for j in range(TPG):
                high(opY[0][:, (SSM_G - 1) * TPG + j, :], src[:, :])
            residual("ssm_out", ("norm_ffn_2", KD))
            ffn(1, None)

        @block.vector
        def _(dve):
            lane = Lane(dve, dve_step)
            did, sync = lane.did, lane.sync
            n_ = {"hi": 0, "sq": 0, "norm": 0, "sig": 0, "v": 0}
            V = nc.vector

            def split(u):
                if u >= NU:
                    return
                _, kt, width = units[u]
                dve.wait_ge(hi_ready, u + 1)
                did(V.tensor_tensor(w_lo[u % SPLIT][:, 0:kt, 0:width], raw[u % RAW][:, 0:kt, 0:width],
                                    w_hi[u % SPLIT][:, 0:kt, 0:width].bitcast(F32), ALU.subtract), lo_ready)

            def ahead(t):
                sync()
                u0, nu, _, _ = tiles[t]
                for u in range(u0, u0 + nu):
                    split(u + 2)

            def arrive(t, n=SEQ):
                dve.wait_ge(unit_used, last_unit(t) + 1)
                return bank[t % 4][0:tiles[t][3], 0:n]

            def low(dst, source, gain=None):
                n_["hi"] += 1
                dve.wait_ge(op_hi_done, n_["hi"])
                sync()
                if gain is None:
                    did(V.tensor_tensor(dst[1], source, dst[0].bitcast(F32), ALU.subtract), op_ready)
                else:
                    did(V.scalar_tensor_tensor(dst[1], source, gain, dst[0].bitcast(F32), ALU.mult, ALU.subtract), op_ready)

            def pair(op, k):
                return op[0][:, k, :], op[1][:, k, :]

            def add_square(m, count, n=SEQ):
                n_["sq"] += 1
                dve.wait_ge(sq_ready, n_["sq"])
                sync()
                s = ss_added if m == count - 1 else sq_used
                if m == 0:
                    did(V.tensor_copy(ss[:, 0:n], sq[0][:, 0:n]), s)
                else:
                    did(V.tensor_tensor(ss[:, 0:n], ss[:, 0:n], sq[m % 2][:, 0:n], ALU.add), s)

            def norm(dst, n, width):
                n_["norm"] += 1
                dve.wait_ge(r0_ready, n_["norm"])
                sync()
                m, r = norm_m[:, 0:n], norm_r[:, 0:n]
                did(V.tensor_tensor(m, m, r, ALU.mult))
                sync()
                did(V.scalar_tensor_tensor(m, m, -0.5, r, ALU.mult, ALU.mult))
                sync()
                did(V.scalar_tensor_tensor(dst, m, 1.5, r, ALU.add, ALU.mult), rstd_ready)
                sync()

            def wait_gate():
                n_["sig"] += 1
                dve.wait_ge(sig_ready, n_["sig"])

            R = rstd[:, :]

            def gated(name, first=False, last=False):
                t = stage[name]
                for i in range(KD):
                    ahead(t + 2 * i)
                    did(V.tensor_tensor(tmp[:, :], arrive(t + 2 * i), R, ALU.mult), sig_in)
                    ahead(t + 2 * i + 1)
                    y = arrive(t + 2 * i + 1)
                    wait_gate()
                    if first:
                        did(V.tensor_tensor(merged[:, i, :], sig[:, :], y, ALU.mult))
                        continue
                    did(V.tensor_tensor(tmp2[:, :], sig[:, :], y, ALU.mult))
                    sync()
                    if last:
                        did(V.tensor_tensor(src[:, :], merged[:, i, :], tmp2[:, :], ALU.add), src_ready)
                        low(pair(opC, i), src[:, :])
                    else:
                        did(V.tensor_tensor(merged[:, i, :], merged[:, i, :], tmp2[:, :], ALU.add))
                sync()

            def conv(dst, taps, name, index, stride, bias=None):
                for j in range(taps):
                    s = pad[:, 4 - taps + j:4 - taps + j + SEQ]
                    w = col(name, j * stride + index)
                    sync()
                    if j == 0:
                        if bias is None:
                            did(V.tensor_scalar(dst, s, w, None, ALU.mult))
                        else:
                            did(V.tensor_scalar(dst, s, w, bias, ALU.mult, ALU.add))
                    else:
                        did(V.scalar_tensor_tensor(dst, s, w, dst, ALU.mult, ALU.add), *((sig_in,) if j == taps - 1 and bias is not None else ()))

            def v_in(t, r, n):
                i = n_["v"]
                n_["v"] += 1
                if i >= 2:
                    dve.wait_ge(v_turned, i - 1)
                did(V.tensor_tensor((tmp if i % 2 == 0 else tmp2)[:, 0:n], arrive(t, n), r, ALU.mult), vT_ready)

            did(V.memset(pad[:, 0:3], 0.0))
            dve.wait_ge(params_in, 32)
            split(0)
            split(1)
            did(V.tensor_scalar(col("q_norm_a_2"), col("q_norm_a_2"), HD ** -0.5, None, ALU.mult))
            did(V.tensor_scalar(col("q_norm_b_2"), col("q_norm_b_2"), HD ** -0.5, None, ALU.mult))
            dve.wait_ge(x_in, 16 * (KD // 2))
            for k in range(KD):
                low(pair(opA, k), x[:, k, :], col("g_mix", k))
                add_square(k, KD)
            norm(R, SEQ, D)
            t = stage["conv"]
            for i in range(KD):
                ahead(t + 3 * i)
                did(V.tensor_tensor(tmp2[:, :], arrive(t + 3 * i), R, ALU.mult))
                ahead(t + 3 * i + 1)
                did(V.tensor_tensor(tmp[:, :], arrive(t + 3 * i + 1), R, ALU.mult))
                sync()
                did(V.tensor_tensor(pad[:, 3:3 + SEQ], tmp[:, :], tmp2[:, :], ALU.mult))
                conv(tmp[:, :], 3, "conv_w", i, KD)
                ahead(t + 3 * i + 2)
                did(V.tensor_tensor(tmp2[:, :], arrive(t + 3 * i + 2), R, ALU.mult))
                sync()
                did(V.tensor_tensor(src[:, :], tmp2[:, :], tmp[:, :], ALU.mult), src_ready)
                low(pair(opB, i), src[:, :])
            gated("conv_out", first=True)
            t = stage["qkv"]
            for i in range(3 * KD):
                ahead(t + i)
                if i < KD:
                    did(V.scalar_tensor_tensor(qT[:, i, :], arrive(t + i), SB_DIM ** -0.5, R, ALU.mult, ALU.mult))
                elif i < 2 * KD:
                    did(V.tensor_tensor(kT[:, i - KD, :], arrive(t + i), R, ALU.mult))
                else:
                    v_in(t + i, R, SEQ)
            sync()

            SPANS = ((0, 0, 512), (1, 512, 512), (2, 1024, 256))

            def sb_softplus(h):
                s_ = sb_sp[h % 2]
                if h >= 2:
                    dve.wait_ge(sb_summed, h - 1)
                for i, (b, c, w) in enumerate(SPANS):
                    dve.wait_ge(sb_exp_ready, 3 * h + i + 1)
                    did(V.scalar_tensor_tensor(s_[:, c:c + w], bank[4 * (h % 2) + b][:, 0:w], 0.0, sb_e[:, c:c + w], ALU.max, ALU.add))
                sync()
                past = const("past").rearrange("p (o k) -> p o k", o=1).to_broadcast([P, 2, P])
                first = s_[:, 0:1024].rearrange("p (b k) -> p b k", k=512)[:, :, 0:P]
                rest = s_[:, 896:1152].rearrange("p (b k) -> p b k", k=P)
                did(V.tensor_tensor(first, first, past, ALU.mult))
                sync()
                did(V.tensor_tensor(rest, rest, past, ALU.mult), sb_sp_ready)

            def sb_low(h):
                dve.wait_ge(sb_hi_ready, h + 1)
                sync()
                did(V.tensor_tensor(sb_sp_lo[h % 2][:, :], sb_sp[h % 2][:, :], sb_sp_hi[h % 2][:, :].bitcast(F32), ALU.subtract), sb_lo_ready)

            def sb_out(h):
                r = HD * (h % 2)
                dve.wait_ge(sb_pv_done, h + 1)
                sync()
                did(V.tensor_copy(src[r:r + HD, :], bank[3 + 4 * (h % 2)][0:HD, :]), sb_o_read)
                if h % 2:
                    low(pair(opC, h // 2), src[:, :])

            sb_softplus(0)
            sb_low(0)
            for h in range(SB_HEADS):
                if h + 1 < SB_HEADS:
                    sb_softplus(h + 1)
                if h >= 1:
                    sb_out(h - 1)
                if h + 1 < SB_HEADS:
                    sb_low(h + 1)
            sb_out(SB_HEADS - 1)
            gated("sb_out")
            dve.wait_ge(mem_in, 16)
            for k in range(KD):
                low(pair(opM, k), memx[:, k, :], col("g_mem", k))
                add_square(k, KD, MEM)
            RM = rstd_m[:, :]
            norm(RM, MEM, D)

            def head_norm(dst, k, n, r, name, ready=None):
                for j in range(2):
                    add_square(j, 2, n)
                norm(sig[:, 0:n], n, X_DIM)
                for j in range(2):
                    did(V.scalar_tensor_tensor(dst[:, k + j, :], dst[:, k + j, :], col(name, j), sig[:, 0:n], ALU.mult, ALU.mult), *((ready,) if ready else ()))

            t = stage["mem_kv"]
            for i in range(2 * KD):
                ahead(t + i)
                if i < KD:
                    did(V.tensor_tensor(xk[:, i, :], arrive(t + i, MEM), RM, ALU.mult), sq_in)
                    if i % 2:
                        head_norm(xk, i - 1, MEM, RM, "k_norm_g")
                else:
                    v_in(t + i, RM, MEM)
            t = stage["xq"]
            for i in range(KD):
                ahead(t + i)
                did(V.tensor_tensor(xq[:, i, :], arrive(t + i), R, ALU.mult), sq_in)
                if i % 2:
                    head_norm(xq, i - 1, SEQ, R, "q_norm_g", xq_ready)
            sync()

            def x_max(h):
                o = 32 * (h % 2)
                dve.wait_ge(x_scored, h + 1)
                for b in range(2):
                    did(V.tensor_reduce(small[:, o + 2 * b:o + 2 * b + 2], bank[b][:, :].rearrange("p (q k) -> p q k", k=MEM), AX.X, ALU.max))
                sync()
                did(V.tensor_scalar(small[:, o + TB:o + 2 * TB], small[:, o:o + TB], -float(X_DIM) ** -0.5, None, ALU.mult), x_max_ready)

            def x_share(h):
                o = 32 * (h % 2)
                dve.wait_ge(x_exp_ready, TB * (h + 1))
                did(V.reciprocal(small[:, o + 3 * TB:o + 4 * TB], small[:, o + 2 * TB:o + 3 * TB]))
                sync()
                for qb in range(TB):
                    ins = V.tensor_scalar(x_p[h % 2][:, qb, :], x_p[h % 2][:, qb, :], small[:, o + 3 * TB + qb:o + 3 * TB + qb + 1], None, ALU.mult)
                    if qb == TB - 1:
                        sync()
                        did(ins, x_p_ready)
                    else:
                        did(ins)

            x_max(0)
            x_share(0)
            for h in range(X_HEADS):
                if h + 1 < X_HEADS:
                    x_max(h + 1)
                    x_share(h + 1)
                for d in range(2):
                    n = 2 * h + d
                    dve.wait_ge(x_pv_done, n + 1)
                    sync()
                    did(V.tensor_copy(src[:, :], bank[5 + d][:, :]), x_o_read)
                    low(pair(opB, n), src[:, :])
            gated("x_out", last=True)
            dve.sem_inc(strip_zone_free, 1)

            def residual(name, prep=None, result=False):
                t = stage[name]

                def finish(k):
                    low(pair(opA, k), x[:, k, :], col(prep[0], prep[1] + k))
                    add_square(k, KD)

                for i in range(KD):
                    ahead(t + i)
                    did(V.tensor_tensor(x[:, i, :], x[:, i, :], arrive(t + i), ALU.add), *((src_ready,) if prep else (out_ready,) if result else ()))
                    if prep and i:
                        finish(i - 1)
                if prep:
                    finish(KD - 1)
                    norm(R, SEQ, D)

            residual("w_out", ("g_mlp", 0))
            for half in range(FF1 // P // MLP_HALF):
                t = stage[f"up{half}"]
                for i in range(MLP_HALF):
                    ahead(t + i)
                    did(V.tensor_tensor(tmp[:, :], arrive(t + i), R, ALU.mult))
                    sync()
                    did(V.scalar_tensor_tensor(src[:, :], tmp[:, :], 0.0, tmp[:, :], ALU.max, ALU.mult), src_ready)
                    low(pair(hid1, i), src[:, :])
                residual(f"down{half}", ("norm_mix_2", 0) if half else None)
            dve.wait_ge(strip_turned, A_HEADS)
            did(V.memset(strip[0:HD, :, SEQ - HD:SEQ], -BIG))
            t = stage["attn_in"]
            for i in range(4 * AW + 2):
                ahead(t + i)
                if i > 3 * AW:
                    v_in(t + i, R, SEQ)
                else:
                    did(V.tensor_tensor(qk2[:, i, :] if i < 3 * AW else src[:, :], arrive(t + i), R, ALU.mult), sq_in)
                    n_["sq"] += 1
                if 1 <= i <= 3 * AW + 1:
                    d = qk2[:, i - 1, :] if i - 1 < 3 * AW else src[:, :]
                    norm(sig[:, :], SEQ, HD)
                    name = ("q_norm_a_2", "k_norm_a_2", "q_norm_b_2", "k_norm_b_2")[(i - 1) // AW]
                    did(V.scalar_tensor_tensor(d, d, col(name), sig[:, :], ALU.mult, ALU.mult), at_q_ready)
                if i == 3 * AW + 1:
                    sync()
                    for kv in range(B_KV):
                        for half in range(2):
                            did(V.tensor_copy(kb2[half * HD:(half + 1) * HD, kv, :], src[kv * HD:(kv + 1) * HD, :]))
            sync()

            AH = A_HEADS + B_HEADS

            def at_max(h):
                o = 32 * (h % 2)
                s_ = at_s[h % 2]
                dve.wait_ge(at_scored, h + 1)
                if h >= 2:
                    dve.wait_ge(at_turned, h - 1)
                sync()
                rows = A_SCORES if h < A_HEADS else B_SCORES
                for qb, _, nk, b, c in rows:
                    w = nk * P
                    part, ps = s_[:, b * SEQ + c:b * SEQ + c + w], bank[b][:, c:c + w]
                    if h < A_HEADS:
                        ins = V.tensor_tensor(part, ps, strip[:, h, SEQ - w:SEQ], ALU.add)
                    else:
                        dist = con[:, CON["dist_b"] + 2 * P - w:CON["dist_b"] + 2 * P]
                        ins = V.scalar_tensor_tensor(part, dist, 2.0 ** (-8.0 * (h - A_HEADS + 1) / B_HEADS), ps, ALU.mult, ALU.add)
                    if qb == rows[-1][0]:
                        sync()
                        did(ins, at_biased)
                    else:
                        did(ins)
                sync()
                for qb, _, nk, b, c in rows:
                    did(V.tensor_reduce(small[:, o + qb:o + qb + 1], s_[:, b * SEQ + c:b * SEQ + c + nk * P], AX.X, ALU.max))
                sync()
                if h >= A_HEADS:
                    did(V.tensor_scalar(small[:, o + TB:o + 2 * TB], small[:, o:o + TB], col("sinks_2", h - A_HEADS), -1.0, ALU.max, ALU.mult), at_max_ready)
                else:
                    did(V.tensor_scalar(small[:, o + TB:o + 2 * TB], small[:, o:o + TB], -1.0, None, ALU.mult), at_max_ready)

            def at_out(h):
                r = HD * (h % 2)
                dve.wait_ge(at_pv_done, h + 1)
                sync()
                did(V.tensor_copy(src[r:r + HD, :], bank[6 + h % 2][0:HD, :]), at_o_read)
                if h % 2:
                    low(pair(opB, h // 2), src[:, :])

            def at_share(h):
                o = 32 * (h % 2)
                dve.wait_ge(at_exp_ready, TB * (h + 1) + max(0, h + 1 - A_HEADS))
                total, share = small[:, o + 2 * TB:o + 3 * TB], small[:, o:o + TB]
                if h >= A_HEADS:
                    did(V.tensor_tensor(total, total, small[:, o + 3 * TB:o + 4 * TB], ALU.add))
                    sync()
                did(V.reciprocal(share, total))
                sync()
                rows = A_SCORES if h < A_HEADS else B_SCORES
                for qb, _, nk, b, c in rows:
                    s_ = at_s[h % 2][:, b * SEQ + c:b * SEQ + c + nk * P]
                    ins = V.tensor_scalar(s_, s_, small[:, o + qb:o + qb + 1], None, ALU.mult)
                    if qb == rows[-1][0]:
                        sync()
                        did(ins, at_p_ready)
                    else:
                        did(ins)

            at_max(0)
            at_max(1)
            at_share(0)
            for h in range(AH):
                if h + 1 < AH:
                    at_share(h + 1)
                if h + 2 < AH:
                    at_max(h + 2)
                at_out(h)
            residual("attn_out", ("norm_ffn_2", 0))

            def ffn(layer, after):
                t = stage[f"ffn_in{layer}"]
                for i in range(KF2):
                    ahead(t + 2 * i)
                    did(V.tensor_tensor(pad[:, 3:3 + SEQ], arrive(t + 2 * i), R, ALU.mult))
                    conv(tmp[:, :], 3, "ffn_conv_w_2", layer * 3 * KF2 + i, KF2, col("ffn_conv_b_2", layer * KF2 + i))
                    ahead(t + 2 * i + 1)
                    did(V.tensor_tensor(tmp2[:, :], arrive(t + 2 * i + 1), R, ALU.mult))
                    sync()
                    wait_gate()
                    did(V.tensor_tensor(tmp2[:, :], tmp2[:, :], sig[:, :], ALU.mult))
                    sync()
                    did(V.tensor_tensor(src[:, :], tmp2[:, :], tmp[:, :], ALU.mult), src_ready)
                    low(pair(hid2, i), src[:, :])
                residual(f"ffn_out{layer}", after, result=(layer == 1))

            ffn(0, ("norm_mix_2", KD))
            S32 = SSM_HEADS
            t = stage["dt"]
            ahead(t)
            e, v, u, lnu, dtT = dt_e[0:S32, :], dt_m[0:S32, :], dt_d[0:S32, :], dt_wT[0:S32, :], dt_dtT[0:S32, :]
            did(V.tensor_tensor(v, arrive(t), rstd[0:S32, :], ALU.mult))
            sync()
            did(V.tensor_scalar(v, v, col("dt_bias")[0:S32, :], None, ALU.add), dt_in)
            dve.wait_ge(dt_exp, 1)
            did(V.tensor_scalar(u, e, 1.0, None, ALU.add), dt_ln_in)
            dve.wait_ge(dt_ln, 1)
            sync()
            did(V.tensor_scalar(u, u, -1.0, None, ALU.add))
            sync()
            z = tmp[0:S32, :]
            did(V.tensor_scalar(z, u, 0.0, None, ALU.is_equal))
            sync()
            did(V.tensor_tensor(u, u, z, ALU.add))
            did(V.tensor_tensor(lnu, lnu, z, ALU.add))
            sync()
            did(V.reciprocal(u, u))
            did(V.tensor_tensor(lnu, lnu, e, ALU.mult))
            sync()
            did(V.tensor_tensor(lnu, lnu, u, ALU.mult))
            sync()
            did(V.scalar_tensor_tensor(dtT, v, 0.0, lnu, ALU.max, ALU.add))
            sync()
            did(V.tensor_scalar(u, dtT, small[0:S32, 0:1], -1.0, ALU.mult, ALU.mult))
            sync()
            for c in range(TB):
                cc = slice(c * P, (c + 1) * P)
                did(V.tensor_tensor_scan(dt_acsT[0:S32, cc], const("ones")[0:S32, :], u[:, cc], 0.0, ALU.mult, ALU.add), dt_acs)
            dve.wait_ge(dt_w, TB)
            sync()
            for c in range(TB):
                if c == TB - 1:
                    sync()
                did(V.tensor_scalar(dt_last[0:S32, c * S32:(c + 1) * S32], ident[0:S32, 0:S32], dt_acsT[0:S32, c * P + P - 1:c * P + P], None, ALU.mult),
                    *((dt_ready,) if c == TB - 1 else ()))

            def y_operand(g, j):
                sync()
                did(V.scalar_tensor_tensor(src[:, :], xs[:, j, :], col("ssm_norm_2", g * TPG + j), z_rstd[:, :], ALU.mult, ALU.mult), src_ready)
                low(pair(opY, g * TPG + j), src[:, :])

            for g in range(SSM_G):
                t = stage[f"ssm{g}"]
                for j, (kind, i) in enumerate(SSM_ORDER):
                    ahead(t + j)
                    if kind == "z":
                        did(V.tensor_tensor(tmp[:, :], arrive(t + j), R, ALU.mult), sig_in)
                        sync()
                        wait_gate()
                        did(V.tensor_tensor(zs[:, i, :], tmp[:, :], sig[:, :], ALU.mult), z_taken)
                        continue
                    if kind == "x" and g:
                        y_operand(g - 1, i)
                    ch = {"b": 4 * TPG + g, "c": 4 * TPG + SSM_G + g, "x": g * TPG + i}[kind]
                    dst = {"b": bT[:, :], "c": cT[:, :], "x": xs[:, i, :]}[kind]
                    did(V.tensor_tensor(pad[:, 3:3 + SEQ], arrive(t + j), R, ALU.mult))
                    conv(tmp[:, :], 4, "ssm_conv_w_2", ch, 24, col("ssm_conv_b_2", ch))
                    wait_gate()
                    sync()
                    did(V.tensor_tensor(dst, tmp[:, :], sig[:, :], ALU.mult), xs_ready)
                    if j == 2 and g:
                        norm(z_rstd[:, :], SEQ, SSM_IN // SSM_G)
                    if j == 5:
                        dve.wait_ge(cb_done, g + 1)
                        did(V.tensor_tensor(cbm[:, :, :], bank[7][:, :].rearrange("p (c l) -> p c l", l=P),
                                            const("causal").rearrange("p (o l) -> p o l", o=1).to_broadcast([P, TB, P]), ALU.mult), cb_ready)
                sync()
                h0 = g * HPG
                for c in range(TB - 1):
                    dve.wait_ge(upd_done, g * (TB - 1) + c + 1)
                    if c == 0:
                        did(V.tensor_copy(state[:, 0, :], bank[5][:, :]), state_ready)
                    else:
                        d = e_last[:, c, h0:h0 + HPG].rearrange("p (h o) -> p h o", o=1).to_broadcast([P, HPG, SSM_P])
                        s_ = state[:, c, :]
                        if c == 1:
                            dve.wait_ge(dt_tok_ready, 3)
                        sync()
                        did(V.tensor_tensor(s_.rearrange("p (h d) -> p h d", d=SSM_P), state[:, c - 1, :].rearrange("p (h d) -> p h d", d=SSM_P), d, ALU.mult))
                        sync()
                        did(V.tensor_tensor(s_, s_, bank[5 + c][:, :], ALU.add), state_ready)

                def weigh(h):
                    n = h0 + h
                    dve.wait_ge(s_ready, n + 1)
                    S = ssm_S[n % 3][:, :]
                    did(V.tensor_tensor(S, S, cbm[:, :, :].rearrange("p c l -> p (c l)"), ALU.mult), g_ready)

                def y_out(h):
                    n = h0 + h
                    r, j = SSM_P * (h % 2), h // 2
                    dve.wait_ge(y_done, n + 1)
                    did(V.scalar_tensor_tensor(xs[r:r + SSM_P, j, :], xs[r:r + SSM_P, j, :], par[r:r + SSM_P, PAR["ssm_d_2"] + g * TPG + j:PAR["ssm_d_2"] + g * TPG + j + 1],
                                               bank[5 + n % 2][0:SSM_P, :], ALU.mult, ALU.add), y_read)

                weigh(0)
                for h in range(HPG):
                    if h + 1 < HPG:
                        weigh(h + 1)
                    y_out(h)
                    if h % 2:
                        sync()
                        did(V.tensor_tensor(xs[:, h // 2, :], xs[:, h // 2, :], zs[:, h // 2, :], ALU.mult), sq_in)
                for j in range(TPG):
                    add_square(j, TPG)
            norm(z_rstd[:, :], SEQ, SSM_IN // SSM_G)
            for j in range(TPG):
                y_operand(SSM_G - 1, j)
            residual("ssm_out", ("norm_ffn_2", KD))
            ffn(1, None)

        @block.gpsimd
        def _(pool):
            lane = Lane(pool, pool_step)
            did, sync = lane.did, lane.sync
            G = nc.gpsimd
            for g in range(SSM_G):
                h0 = g * HPG
                for j in range(TPG):
                    pool.wait_ge(x_tok_ready, 5 * g + 2 + j)
                    if g == 0 and j == 0:
                        pool.wait_ge(dt_tok_ready, 3)
                    sync()

                    def heads(v, n):
                        return v[:, 0:n, j * P:(j + 1) * P].rearrange("p c (h d) -> p c h d", d=SSM_P)

                    def per_head(k, n):
                        w = dt_tok[:, k, 0:n, h0 + 2 * j:h0 + 2 * j + 2].rearrange("p c (h o) -> p c h o", o=1)
                        return w.to_broadcast([P, n, 2, SSM_P])

                    did(G.tensor_tensor(heads(x_tok, TB), heads(x_tok, TB), per_head(1, TB), ALU.mult))
                    sync()
                    did(G.tensor_tensor(heads(xw, TB - 1), heads(x_tok, TB - 1), per_head(2, TB - 1), ALU.mult), xw_ready)
                pool.wait_ge(xs_ready, 6 * g + 2)
                for h in range(HPG):
                    n = h0 + h
                    E = ssm_E[n % 3][:, P:SEQ]
                    pool.wait_ge(e_ready, n + 1)
                    did(G.tensor_tensor(E, E, cT[:, P:SEQ], ALU.mult), ec_ready)
                sync()


_WEIGHTS = ["w_in", "w_conv_out", "w_sb_out", "w_mem_kv", "w_x_out", "w_out", "w_up", "w_down",
            "attn_w_in_2", "attn_w_out_2", "ssm_w_in_2", "ssm_w_out_2", "ffn_w_in_2", "ffn_w_out_2"]


def kernel(**inputs):
    import numpy as np
    import concourse.bacc as _bacc
    from concourse.bass_utils import run_bass_kernel_spmd as _run

    a = {k: np.asarray(v) for k, v in inputs.items()}

    def columns(v):
        return v.reshape(-1, P).T

    par = {n: columns(a[n]) for n in ("g_mix", "g_mem", "conv_w", "q_norm_g", "k_norm_g", "g_mlp", "norm_mix_2", "norm_ffn_2",
                                      "ffn_conv_w_2", "ffn_conv_b_2", "ssm_conv_w_2", "ssm_conv_b_2", "ssm_norm_2")}
    par["ssm_d_2"] = columns(np.repeat(a["ssm_d_2"].reshape(-1), SSM_P))
    for n in ("q_norm_a_2", "k_norm_a_2", "q_norm_b_2", "k_norm_b_2"):
        v = a[n].reshape(-1)
        par[n] = np.concatenate([v, v]).reshape(P, 1)
    par["sinks_2"] = np.repeat(a["sinks_2"].reshape(1, -1), P, axis=0)
    par["dt_bias"] = np.tile(a["ssm_dt_bias_2"].reshape(-1), P // SSM_HEADS).reshape(P, 1)
    par["a_log"] = np.tile(a["ssm_a_log_2"].reshape(-1), P // SSM_HEADS).reshape(P, 1)
    table = a["relpos_table_2"].reshape(A_HEADS, -1)
    reach = (table.shape[1] - 1) // 2
    rel = table[:, reach + np.clip(SEQ - 1 - np.arange(STRIP_E), -reach, reach)]

    i, j = np.arange(P)[:, None], np.arange(P)[None, :]
    f = np.float32
    m = np.arange(2 * P)[None, :]
    seen = (m // HD <= i // HD + 2) & (m // HD >= i // HD)
    con = {"ident": i == j, "neg_later": -(i >= j).astype(f), "neg_ones": -np.ones((P, P)), "past": i < j,
           "neg_future": -BIG * (i >= j), "ones": np.ones((P, P)), "head_ones": i // HD == j // HD, "causal": i <= j, "neg_before": -BIG * (i > j),
           "dist_b": np.where(seen, -np.abs(i - m + P), -BIG * 256.0), "flip": i + j == P - 1, "eps": np.full((P, 1), EPS)}
    arrays = {
        "xT": np.ascontiguousarray(a["x"].reshape(SEQ, KD, P).transpose(2, 1, 0)),
        "memT": np.ascontiguousarray(a["mem"].reshape(MEM, KD, P).transpose(2, 1, 0)),
        "par": np.ascontiguousarray(np.concatenate([par[n] for n in PAR], axis=1)),
        "con": np.ascontiguousarray(np.concatenate([con[n].astype(f) for n in CON], axis=1)),
        "rel": np.ascontiguousarray(rel),
    }
    for n in _WEIGHTS:
        w = a[n]
        arrays[n] = np.ascontiguousarray(w if n.startswith("ffn") else w.reshape(w.shape[1:]))
    nc = _bacc.Bacc("TRN2", target_bir_lowering=False, num_devices=1, dynamic_dma_scratch_size=2048)
    dram = {n: nc.dram_tensor(n, v.shape, F32, kind="ExternalInput").ap() for n, v in arrays.items()}
    out = nc.dram_tensor("outT", (P, KD, SEQ), F32, kind="ExternalOutput").ap()
    two_block_kernel(nc, dram, out)
    r = _run(nc, [arrays], core_ids=[0])
    return r.results[0]["outT"].transpose(2, 1, 0).reshape(1, SEQ, D)
```

```python
from contextlib import ExitStack

import concourse.bass as bass
from concourse import mybir

F32 = mybir.dt.float32
F32R = mybir.dt.float32r
ALU = mybir.AluOpType
ACT = mybir.ActivationFunctionType
AX = mybir.AxisListType

P = 128
SEQ = 512
D = 1024
MEM = 256
KD = D // P
TB = SEQ // P
EPS = 1e-6
BIG = 1e30

SB_HEADS, SB_DIM = 16, 64
X_HEADS, X_DIM = 4, 256
FF1 = 4096
A_HEADS = B_HEADS = 8
B_KV = 2
HD = 64
SSM_G, SSM_N, SSM_HEADS, SSM_P = 4, 128, 32, 64
SSM_IN = SSM_HEADS * SSM_P
HPG = SSM_HEADS // SSM_G
TPG = HPG * SSM_P // P
FF2 = 2816
KF2 = FF2 // P
UNIT_K = 8
RAW, SPLIT = 3, 3
MLP_HALF = 16

PAR = {}
_at = 0
for _name, _n in (("g_mix", 8), ("g_mem", 8), ("conv_w", 24), ("q_norm_g", 2), ("k_norm_g", 2),
                  ("g_mlp", 8), ("norm_mix_2", 16), ("norm_ffn_2", 16),
                  ("ffn_conv_w_2", 2 * 3 * KF2), ("ffn_conv_b_2", 2 * KF2),
                  ("ssm_conv_w_2", 4 * 24), ("ssm_conv_b_2", 24), ("ssm_norm_2", 16),
                  ("ssm_d_2", 16), ("q_norm_a_2", 1), ("k_norm_a_2", 1), ("q_norm_b_2", 1),
                  ("k_norm_b_2", 1), ("sinks_2", B_HEADS), ("dt_bias", 1), ("a_log", 1)):
    PAR[_name] = _at
    _at += _n
NPAR = _at

CON = {}
_at = 0
for _name, _n in (("ident", P), ("neg_later", P), ("neg_ones", P), ("past", P), ("neg_future", P),
                  ("ones", P), ("head_ones", P), ("causal", P), ("neg_before", P), ("dist_b", 2 * P), ("flip", P), ("eps", 1)):
    CON[_name] = _at
    _at += _n
NCON = _at
STRIP_E = 639


class Lane:

    def __init__(self, eng, step):
        self.eng, self.step, self.count, self.open = eng, step, {}, {}

    def did(self, ins, sem=None):
        s = sem or self.step
        ins.then_inc(s, 1)
        self.count[s.name] = self.count.get(s.name, 0) + 1
        self.open[s.name] = (s, self.count[s.name])

    def sync(self):
        for s, v in self.open.values():
            self.eng.wait_ge(s, v)
        self.open = {}


def two_block_kernel(nc, dram, out):
    ctx = ExitStack()
    with ctx:
        def sem(name):
            return ctx.enter_context(nc.semaphore(name))

        base = (nc.sbuf_base + 31) // 32 * 32
        arena = ctx.enter_context(nc.sbuf_tensor("arena", [P, (nc.sbuf_bytes_remaining - 64) // 4], F32))
        cursor = [base]

        def at(name, offset, shape, dt=F32):
            return nc.alloc_sbuf_tensor_at(name, [P] + list(shape), dt, offset=offset)

        def size(shape):
            n = 4
            for s in shape:
                n *= s
            return (n + 31) // 32 * 32

        def place(name, shape, dt=F32):
            t = at(name, cursor[0], shape, dt)
            cursor[0] += size(shape)
            return t

        par = place("par", [NPAR])
        con = place("con", [NCON])
        raw = [place(f"raw{i}", [UNIT_K, P]) for i in range(RAW)]
        w_hi = [place(f"w_hi{i}", [UNIT_K, P], F32R) for i in range(SPLIT)]
        w_lo = [place(f"w_lo{i}", [UNIT_K, P], F32R) for i in range(SPLIT)]
        x = place("x", [KD, SEQ])
        rstd = place("rstd", [SEQ])
        TILE = 2048
        a_off = cursor[0]
        b_off = a_off + 2 * KD * TILE
        c_off = b_off + 2 * KD * TILE
        d_off = c_off + 2 * KD * TILE
        t_off = d_off + 2 * KD * TILE
        cursor[0] = t_off
        opA = [at("opA_hi", a_off, [KD, SEQ], F32R), at("opA_lo", a_off + KD * TILE, [KD, SEQ], F32R)]
        opB = [at("opB_hi", b_off, [KD, SEQ], F32R), at("opB_lo", b_off + KD * TILE, [KD, SEQ], F32R)]
        opC = [at("opC_hi", c_off, [KD, SEQ], F32R), at("opC_lo", c_off + KD * TILE, [KD, SEQ], F32R)]
        sq = [place(f"sq{i}", [SEQ]) for i in range(2)]
        ss = place("ss", [SEQ])
        src = place("src", [SEQ])
        pad = place("pad", [SEQ + 4])
        tmp = place("tmp", [SEQ])
        tmp2 = place("tmp2", [SEQ])
        sig = place("sig", [SEQ])
        small = place("small", [64])
        dt_acs_lo = at("dt_acs_lo", cursor[0], [SEQ], F32R)
        dt_acsT = place("dt_acsT", [SEQ])
        dt_last = place("dt_last", [TB * SSM_HEADS])
        dt_tok = place("dt_tok", [3, TB, SSM_HEADS])
        e_last = place("e_last", [TB, SSM_HEADS])
        ident_r = place("ident_r", [P], F32R)
        neg_later_r = place("neg_later_r", [P], F32R)
        neg_ones_r = place("neg_ones_r", [P], F32R)
        neg_future_r = place("neg_future_r", [P], F32R)
        neg_before_r = place("neg_before_r", [P], F32R)
        xw_off = cursor[0]
        xw = place("xw", [TB - 1, TPG * P])
        dt_acs_hi = place("dt_acs_hi", [SEQ], F32R)
        norm_ln, norm_r, norm_m = (xw[:, i, :] for i in range(3))
        assert cursor[0] <= nc.sbuf_usable_end

        merged = at("merged", d_off + KD * TILE, [KD, SEQ])
        v_tok = at("v_tok", d_off, [TB, D])
        qT = at("qT", c_off, [KD, SEQ])
        kT = at("kT", c_off + KD * TILE, [KD, SEQ])
        SBW = 1280
        sb_e = at("sb_e", b_off, [SBW])
        sb_sp = [at(f"sb_sp{i}", b_off + (1 + i) * 5120, [SBW]) for i in range(2)]
        sb_sp_lo = [at(f"sb_sp_lo{i}", b_off + (1 + i) * 5120, [SBW], F32R) for i in range(2)]
        sb_sp_hi = [at("sb_sp_hi0", b_off + 5 * 5120, [SBW], F32R), at("sb_sp_hi1", xw_off, [SBW], F32R)]
        sb_a = [at(f"sb_a{i}", b_off + (3 + i) * 5120, [SBW]) for i in range(2)]
        opM = [at("opM_hi", b_off, [KD, MEM], F32R), at("opM_lo", b_off + KD * TILE // 2, [KD, MEM], F32R)]
        memx = at("memx", b_off + KD * TILE, [KD, MEM])
        xk = at("xk", d_off, [KD, MEM])
        xv_tok = at("xv_tok", d_off + KD * TILE // 2, [MEM // P, D])
        xq = at("xq", c_off, [KD, SEQ])
        x_p = [at(f"x_p{i}", c_off + KD * TILE + i * 4096, [TB, MEM]) for i in range(2)]
        x_pT = at("x_pT", c_off + KD * TILE + 8192, [MEM // P, SEQ])
        hid1 = [at("hid1_hi", b_off, [MLP_HALF, SEQ], F32R), at("hid1_lo", c_off, [MLP_HALF, SEQ], F32R)]
        qk2 = at("qk2", c_off, [12, SEQ])
        kb2 = at("kb2", c_off + 12 * TILE, [B_KV, SEQ])
        va_tok = at("va_tok", d_off, [TB, A_HEADS * HD])
        vb_tok = at("vb_tok", d_off + TB * TILE, [TB, B_KV * HD])
        strip = at("strip", d_off + 16384, [A_HEADS, SEQ])
        at_s = [at(f"at_s{i}", a_off + i * 5120, [SBW]) for i in range(3)]
        at_pT = [at(f"at_pT{i}", a_off + (3 + i) * 5120, [SBW]) for i in range(2)]
        hid2 = [at("hid2_hi", b_off, [KF2, SEQ], F32R), at("hid2_lo", b_off + KF2 * TILE, [KF2, SEQ], F32R)]
        opY = [at("opY_hi", b_off, [2 * KD, SEQ], F32R), at("opY_lo", c_off, [2 * KD, SEQ], F32R)]
        xs = at("xs", d_off, [TPG, SEQ])
        x_tok = at("x_tok", d_off + 8192, [TB, TPG * P])
        bT = at("bT", d_off + 16384, [SEQ])
        cT = at("cT", d_off + 18432, [SEQ])
        b_tok = at("b_tok", d_off + 20480, [TB, SSM_N])
        state = at("state", d_off + 22528, [TB - 1, TPG * P])
        cbm = at("cbm", d_off + 28672, [TB, P])
        zs = at("zs", b_off + 12 * TILE, [TPG, SEQ])
        z_rstd = at("z_rstd", d_off + 30720, [SEQ])
        dt_dtT = at("dt_dtT", d_off + 22528, [SEQ])
        dt_wT = at("dt_wT", d_off + 24576, [SEQ])
        dt_e = at("dt_e", d_off + 26624, [SEQ])
        dt_d = at("dt_d", d_off + 28672, [SEQ])
        dt_m = at("dt_m", d_off + 30720, [SEQ])
        ssm_S, ssm_E = [tmp, tmp2, sig], [sq[0], sq[1], src]
        rstd_m = at("rstd_m", b_off + 24 * 1024, [MEM])

        def col(name, i=0, n=1):
            return par[:, PAR[name] + i:PAR[name] + i + n]

        def const(name, n=P):
            return con[:, CON[name]:CON[name] + n]

        ident = const("ident")
        bank = [ctx.enter_context(nc.psum_tensor(f"bank{i}", [P, SEQ], F32)) for i in range(8)]

        units, tiles, stage = [], [], {}

        def add_tile(w, c0, k0, kt, width=P):
            first = len(units)
            for k in range(0, kt, UNIT_K):
                n = min(UNIT_K, kt - k)
                rows = w[(k0 + k) * P:(k0 + k + n) * P, c0:c0 + width]
                units.append((rows.rearrange("(k p) c -> p k c", p=P), n, width))
            tiles.append((first, len(units) - first, kt, width))

        def begin(name):
            stage[name] = len(tiles)

        w_in = dram["w_in"]
        begin("conv")
        for i in range(KD):
            for part in (0, 2, 1):
                add_tile(w_in, part * D + i * P, 0, KD)

        def gated(name, gate, w_branch):
            begin(name)
            for i in range(KD):
                add_tile(w_in, (7 + gate) * D + i * P, 0, KD)
                add_tile(w_branch, i * P, 0, KD)

        gated("conv_out", 0, dram["w_conv_out"])
        begin("qkv")
        for part in (3, 4, 5):
            for i in range(KD):
                add_tile(w_in, part * D + i * P, 0, KD)
        gated("sb_out", 1, dram["w_sb_out"])
        begin("mem_kv")
        for i in range(2 * KD):
            add_tile(dram["w_mem_kv"], i * P, 0, KD)
        begin("xq")
        for i in range(KD):
            add_tile(w_in, 6 * D + i * P, 0, KD)
        gated("x_out", 2, dram["w_x_out"])
        begin("w_out")
        for i in range(KD):
            add_tile(dram["w_out"], i * P, 0, KD)
        for half in range(FF1 // P // MLP_HALF):
            begin(f"up{half}")
            for i in range(MLP_HALF):
                add_tile(dram["w_up"], (half * MLP_HALF + i) * P, 0, KD)
            begin(f"down{half}")
            for i in range(KD):
                add_tile(dram["w_down"], i * P, half * MLP_HALF, MLP_HALF)
        begin("attn_in")
        AW = A_HEADS * HD // P
        for c in list(range(0, 2 * AW)) + list(range(3 * AW, 4 * AW)) + [4 * AW] + list(range(2 * AW, 3 * AW)) + [4 * AW + 1]:
            add_tile(dram["attn_w_in_2"], c * P, 0, KD)
        begin("attn_out")
        for i in range(KD):
            add_tile(dram["attn_w_out_2"], i * P, 0, KD)

        def ffn_plan(layer):
            w = dram["ffn_w_in_2"]
            begin(f"ffn_in{layer}")
            for i in range(KF2):
                add_tile(w[layer], i * P, 0, KD)
                add_tile(w[layer], FF2 + i * P, 0, KD)
            begin(f"ffn_out{layer}")
            for i in range(KD):
                add_tile(dram["ffn_w_out_2"][layer], i * P, 0, KF2)

        ffn_plan(0)
        SSM_ORDER = (("z", 0), ("b", 0), ("c", 0), ("x", 0), ("x", 1), ("x", 2), ("x", 3), ("z", 1), ("z", 2), ("z", 3))
        SSM_TURN = {3: 0, 5: 1, 6: 2, 7: 3, 8: 4}
        GT = len(SSM_ORDER)
        begin("dt")
        ssm_w = dram["ssm_w_in_2"]
        add_tile(ssm_w, 2 * SSM_IN + 2 * SSM_G * SSM_N, 0, KD, SSM_HEADS)
        for g in range(SSM_G):
            begin(f"ssm{g}")
            for kind, i in SSM_ORDER:
                c = {"z": g * TPG + i, "x": SSM_IN // P + g * TPG + i, "b": 2 * SSM_IN // P + g, "c": 2 * SSM_IN // P + SSM_G + g}[kind]
                add_tile(ssm_w, c * P, 0, KD)
        begin("ssm_out")
        for i in range(KD):
            add_tile(dram["ssm_w_out_2"], i * P, 0, 2 * KD)
        ffn_plan(1)
        begin("end")
        NU = len(units)

        def last_unit(t):
            return tiles[t][0] + tiles[t][1] - 1

        params_in = sem("params_in")
        con_in = sem("con_in")
        con_r_ready = sem("con_r_ready")
        x_in = [sem(f"x_in{i}") for i in range(KD // 2)]
        mem_in = sem("mem_in")
        strip_in = sem("strip_in")
        strip_zone_free = sem("strip_zone_free")
        strip_flipped, strip_turned = sem("strip_flipped"), sem("strip_turned")
        unit_loaded = [sem(f"unit_loaded{i}") for i in range(RAW)]
        hi_ready = sem("hi_ready")
        lo_ready = sem("lo_ready")
        unit_used = sem("unit_used")
        pe_step, dve_step, act_step = sem("pe_step"), sem("dve_step"), sem("act_step")
        op_hi_done = sem("op_hi_done")
        op_ready = sem("op_ready")
        src_ready = sem("src_ready")
        sq_in, sq_ready, sq_used, ss_added, ss_summed = sem("sq_in"), sem("sq_ready"), sem("sq_used"), sem("ss_added"), sem("ss_summed")
        r0_ready, rstd_ready = sem("r0_ready"), sem("rstd_ready")
        sig_in, sig_ready = sem("sig_in"), sem("sig_ready")
        vT_ready, v_turned, v_tok_ready = sem("vT_ready"), sem("v_turned"), sem("v_tok_ready")
        sb_scored, sb_abs_done, sb_exp_ready, sb_sp_ready = sem("sb_scored"), sem("sb_abs_done"), sem("sb_exp_ready"), sem("sb_sp_ready")
        sb_hi_ready, sb_lo_ready = sem("sb_hi_ready"), sem("sb_lo_ready")
        sb_summed, sb_a_ready, sb_pv_done, sb_o_read = sem("sb_summed"), sem("sb_a_ready"), sem("sb_pv_done"), sem("sb_o_read")
        xq_ready = sem("xq_ready")
        x_scored, x_max_ready, x_exp_ready, x_p_ready = sem("x_scored"), sem("x_max_ready"), sem("x_exp_ready"), sem("x_p_ready")
        x_turned, x_pT_ready, x_pv_done, x_o_read = sem("x_turned"), sem("x_pT_ready"), sem("x_pv_done"), sem("x_o_read")
        at_q_ready = sem("at_q_ready")
        at_scored, at_biased, at_max_ready, at_exp_ready, at_p_ready = sem("at_scored"), sem("at_biased"), sem("at_max_ready"), sem("at_exp_ready"), sem("at_p_ready")
        at_turned, at_pT_ready, at_pv_done, at_o_read = sem("at_turned"), sem("at_pT_ready"), sem("at_pv_done"), sem("at_o_read")
        dt_in, dt_exp, dt_ln_in, dt_ln, dt_acs, dt_w = sem("dt_in"), sem("dt_exp"), sem("dt_ln_in"), sem("dt_ln"), sem("dt_acs"), sem("dt_w")
        dt_ready, dt_turned = sem("dt_ready"), sem("dt_turned")
        xs_turned, x_tok_ready = sem("xs_turned"), sem("x_tok_ready")
        cb_done, xw_ready, upd_done, state_ready, cb_ready = sem("cb_done"), sem("xw_ready"), sem("upd_done"), sem("state_ready"), sem("cb_ready")
        row_done, row_masked, e_ready, s_ready, ec_ready, g_ready, y_done, y_read = sem("row_done"), sem("row_masked"), sem("e_ready"), sem("s_ready"), sem("ec_ready"), sem("g_ready"), sem("y_done"), sem("y_read")
        dt_acs_high, dt_acs_split = sem("dt_acs_high"), sem("dt_acs_split")
        dt_tok_ready, pool_step = sem("dt_tok_ready"), sem("pool_step")
        to_gate, gate_ready, gated_ready = sem("to_gate"), sem("gate_ready"), sem("gated_ready")
        out_ready, stored = sem("out_ready"), sem("stored")

        SQUARES_BEFORE_ATTN = 4 * KD + 2 * KD
        generation, made = {}, [0]

        def operand(name, n):
            generation[name] = made[0]
            made[0] += n

        for name, n in (("x1", KD), ("conv", KD), ("sb", KD), ("mem", KD), ("xo", KD), ("merged", KD), ("x2", KD),
                        ("hid1_0", MLP_HALF), ("hid1_1", MLP_HALF), ("x3", KD), ("attn", KD), ("x4", KD),
                        ("ffn0", KF2), ("x5", KD), ("ssm", 2 * KD), ("x6", KD), ("ffn1", KF2)):
            operand(name, n)

        A_SCORES = ((3, 0, 4, 0, 0), (2, 0, 3, 1, 0), (0, 0, 1, 1, 384), (1, 0, 2, 2, 0))
        B_SCORES = ((1, 0, 2, 0, 0), (2, 1, 2, 0, 256), (3, 2, 2, 1, 0), (0, 0, 1, 1, 256))
        A_TURNED = ((0, 0, 4, 0, 0), (1, 1, 3, 1, 0), (3, 3, 1, 1, 384), (2, 2, 2, 2, 0))
        B_TURNED = ((0, 0, 2, 0, 0), (1, 1, 2, 0, 256), (2, 2, 2, 1, 0), (3, 3, 1, 1, 256))
        A_SPANS, B_SPANS = ((0, 512), (1, 512), (2, 256)), ((0, 512), (1, 384))

        SB_OFF = (0, 512, 1024, 896)
        SB_BANK = ((0, 0), (1, 0), (2, 0), (1, 384))

        block = ctx.enter_context(nc.Block())

        @block.sync
        def _(sp):
            def load(u):
                rows, n, width = units[u]
                sp.dma_start(raw[u % RAW][:, 0:n, 0:width], rows).then_inc(unit_loaded[u % RAW], 16)

            sp.dma_start(par[:, :], dram["par"]).then_inc(params_in, 16)
            load(0)
            for k in range(0, KD, 2):
                sp.dma_start(x[:, k:k + 2, :], dram["xT"][:, k:k + 2, :]).then_inc(x_in[k // 2], 16)

            load(1)
            sp.dma_start(con[:, :], dram["con"]).then_inc(con_in, 16)
            load(2)
            for u in range(RAW, NU):
                sp.wait_ge(lo_ready, u - RAW + 1)
                load(u)
                if u == tiles[stage["sb_out"]][0] + 4:
                    sp.wait_ge(sb_a_ready, 3 * SB_HEADS)
                    sp.wait_ge(sb_pv_done, SB_HEADS)
                    sp.dma_start(memx[:, :, :], dram["memT"]).then_inc(mem_in, 16)
                if u == tiles[stage["up0"]][0] + 4:
                    E = dram["rel"]
                    sp.wait_ge(strip_zone_free, 1)
                    sp.dma_start(strip[:, :, :], bass.AP(E.tensor, 0, [[1, P], [STRIP_E, A_HEADS], [1, SEQ]])).then_inc(strip_in, 16)
            for k in range(KD):
                sp.wait_ge(out_ready, k + 1)
                sp.dma_start(out[:, k, :], x[:, k, :]).then_inc(stored, 16)
            sp.wait_ge(stored, 16 * KD)

        @block.tensor
        def _(pe):
            lane = Lane(pe, pe_step)
            seen = {"op": 0, "sum": 0, "added": 0, "sq": SQUARES_BEFORE_ATTN}

            def tile(t, op, gen, n=SEQ):
                u0, nu, kt, width = tiles[t]
                dst = bank[t % 4][0:width, 0:n]
                for j in range(nu):
                    u = u0 + j
                    pe.wait_ge(lo_ready, u + 1)
                    for k in range(units[u][1]):
                        kk = j * UNIT_K + k
                        need = generation[gen] + kk + 1
                        if need > seen["op"]:
                            pe.wait_ge(op_ready, need)
                            seen["op"] = need
                        wh, wl = w_hi[u % SPLIT][:, k, 0:width], w_lo[u % SPLIT][:, k, 0:width]
                        pe.matmul(dst, wh, op[0][:, kk, 0:n], start=(kk == 0), stop=False)
                        pe.matmul(dst, wh, op[1][:, kk, 0:n], start=False, stop=False)
                        mm = pe.matmul(dst, wl, op[0][:, kk, 0:n], start=False, stop=(kk == kt - 1))
                    mm.then_inc(unit_used, 1)

            def head_norm_sum(k):
                i = seen["sum"]
                seen["sum"] += 1
                pe.wait_ge(sq_ready, seen["sq"] + k + 1)
                pe.wait_ge(r0_ready, i)
                pe.matmul(bank[4][:, :], const("head_ones"), sq[k % 2][:, :], start=True, stop=True).then_inc(ss_summed, 1)

            def norm_sum(n=SEQ, ones="ones"):
                i = seen["sum"]
                seen["sum"] += 1
                seen["added"] += 1
                pe.wait_ge(ss_added, seen["added"])
                if i:
                    pe.wait_ge(r0_ready, i)
                pe.matmul(bank[4][:, 0:n], const(ones), ss[:, 0:n], start=True, stop=True).then_inc(ss_summed, 1)

            def turn(srcs, dst, ready, ready_n, free, free_n, done):
                pe.wait_ge(ready, ready_n)
                if free_n > 0:
                    pe.wait_ge(free, free_n)
                for i, s in enumerate(srcs):
                    mm = pe.transpose(dst[:, i * P:(i + 1) * P], s, ident)
                mm.then_inc(done, 1)

            t = stage["conv"]
            for i in range(3 * KD):
                tile(t + i, opA, "x1")
                if i == 0:
                    pe.wait_ge(con_in, 16)
                    pe.wait_ge(con_r_ready, 5)
                    norm_sum()
            t = stage["conv_out"]
            for i in range(KD):
                tile(t + 2 * i, opA, "x1")
                tile(t + 2 * i + 1, opB, "conv")
            t = stage["qkv"]
            vi = 0

            def turn_v(n, blocks):
                vt = tmp if n % 2 == 0 else tmp2
                turn([vt[:, b * P:(b + 1) * P] for b in range(blocks)], bank[5 + n % 2], vT_ready, n + 1, v_tok_ready, n - 1, v_turned)

            for i in range(3 * KD):
                tile(t + i, opA, "x1")
                if i > 2 * KD:
                    turn_v(vi, TB)
                    vi += 1
            turn_v(vi, TB)
            vi += 1

            def sb_scores(h):
                r, j, s = HD * (h % 2), h // 2, 4 * (h % 2)
                if h >= 2:
                    pe.wait_ge(sb_a_ready, 3 * (h - 1))
                for kb in range(TB):
                    b, c = SB_BANK[kb]
                    mm = pe.matmul(bank[s + b][:, c:c + SEQ - kb * P], kT[r:r + HD, j, kb * P:(kb + 1) * P],
                                   qT[r:r + HD, j, kb * P:SEQ], start=(c == 0), stop=False, skip_group_check=True)
                mm.then_inc(sb_scored, 1)

            def sb_sums(h):
                s = 4 * (h % 2)
                for span, blocks in enumerate(((0,), (1,), (2, 3))):
                    pe.wait_ge(sb_lo_ready, 3 * h + span + 1)
                    for kb in blocks:
                        b, c = SB_BANK[kb]
                        pe.matmul(bank[s + b][:, c:c + P], ident_r[:, :], neg_future_r[:, :], start=False, stop=False, skip_group_check=True)
                    for sp_ in (sb_sp_hi[h % 2], sb_sp_lo[h % 2]):
                        for kb in blocks:
                            n = SEQ - kb * P
                            part = sp_[:, SB_OFF[kb]:SB_OFF[kb] + n]
                            for to in range(kb + 1):
                                b, c = SB_BANK[to]
                                c += (kb - to) * P
                                ones = neg_later_r if to == kb else neg_ones_r
                                mm = pe.matmul(bank[s + b][:, c:c + n], ones[:, :], part, start=False, stop=(span == 2), skip_group_check=True)
                mm.then_inc(sb_summed, 1)

            def sb_values(h):
                pe.wait_ge(sb_a_ready, 3 * (h + 1))
                if h >= 2:
                    pe.wait_ge(sb_o_read, h - 1)
                dst = bank[3 + 4 * (h % 2)]
                for kb in range(TB):
                    n = SEQ - kb * P
                    mm = pe.matmul(dst[0:HD, kb * P:SEQ], v_tok[:, kb, h * HD:(h + 1) * HD], sb_a[h % 2][:, SB_OFF[kb]:SB_OFF[kb] + n],
                                   start=(kb == 0), stop=(kb == TB - 1))
                mm.then_inc(sb_pv_done, 1)

            pe.wait_ge(v_tok_ready, vi)
            pe.wait_ge(vT_ready, vi)
            pe.wait_ge(r0_ready, seen["sum"])
            sb_scores(0)
            for h in range(SB_HEADS):
                if h + 1 < SB_HEADS:
                    sb_scores(h + 1)
                sb_sums(h)
                if h >= 1:
                    sb_values(h - 1)
            sb_values(SB_HEADS - 1)
            pe.wait_ge(sb_o_read, SB_HEADS)
            t = stage["sb_out"]
            for i in range(KD):
                tile(t + 2 * i, opA, "x1")
                tile(t + 2 * i + 1, opC, "sb")
            t = stage["mem_kv"]
            for i in range(2 * KD):
                tile(t + i, opM, "mem", MEM)
                if i == 0 or (i <= KD and i % 2 == 0):
                    norm_sum(MEM)
                if i > KD:
                    turn_v(vi, MEM // P)
                    vi += 1
            turn_v(vi, MEM // P)
            vi += 1
            def x_scores(h):
                pe.wait_ge(xq_ready, 2 * h + 2)
                if h >= 1:
                    pe.wait_ge(x_exp_ready, TB * h)
                for qb in range(TB):
                    for d in range(2):
                        mm = pe.matmul(bank[5 + qb // 2][:, (qb % 2) * MEM:(qb % 2 + 1) * MEM], xq[:, 2 * h + d, qb * P:(qb + 1) * P],
                                       xk[:, 2 * h + d, :], start=(d == 0), stop=(d == 1))
                mm.then_inc(x_scored, 1)

            t = stage["xq"]
            for i in range(KD):
                tile(t + i, opA, "x1")
                if i and i % 2 == 0:
                    norm_sum()
                if i == 5:
                    pe.wait_ge(v_tok_ready, vi)
                    x_scores(0)
            norm_sum()
            pe.wait_ge(sq_in, 2 * KD)
            for h in range(X_HEADS):
                pe.wait_ge(x_p_ready, h + 1)
                if h >= 1:
                    pe.wait_ge(x_pT_ready, 2 * h)
                for kb in range(2):
                    for qb in range(TB):
                        mm = pe.transpose(bank[2 + kb][:, qb * P:(qb + 1) * P], x_p[h % 2][:, qb, kb * P:(kb + 1) * P], ident)
                    mm.then_inc(x_turned, 1)
                if h + 1 < X_HEADS:
                    x_scores(h + 1)
                pe.wait_ge(x_pT_ready, 2 * h + 2)
                for d in range(2):
                    n = 2 * h + d
                    if n >= 2:
                        pe.wait_ge(x_o_read, n - 1)
                    for kb in range(2):
                        mm = pe.matmul(bank[d][:, :], xv_tok[:, kb, n * P:(n + 1) * P], x_pT[:, kb, :], start=(kb == 0), stop=(kb == 1))
                    mm.then_inc(x_pv_done, 1)
            pe.wait_ge(x_o_read, KD)
            t = stage["x_out"]
            for i in range(KD):
                tile(t + 2 * i, opA, "x1")
                tile(t + 2 * i + 1, opB, "xo")
            t = stage["w_out"]
            for i in range(KD):
                tile(t + i, opC, "merged")
            for half in range(FF1 // P // MLP_HALF):
                t = stage[f"up{half}"]
                for i in range(MLP_HALF):
                    tile(t + i, opA, "x2")
                    if half == 0 and i == 0:
                        norm_sum()
                if half == 0:
                    pe.wait_ge(strip_in, 16)
                    for h in range(A_HEADS):
                        if h >= 2:
                            pe.wait_ge(strip_turned, h - 1)
                        pe.matmul(bank[5 + h % 2][:, :], const("flip"), strip[:, h, :], start=True, stop=True).then_inc(strip_flipped, 1)
                t = stage[f"down{half}"]
                for i in range(KD):
                    tile(t + i, hid1, f"hid1_{half}")
            t = stage["attn_in"]
            order = [0] * (3 * AW + 1) + [1] * (AW + 1)
            for i, is_v in enumerate(order):
                tile(t + i, opA, "x3")
                if i == 0:
                    norm_sum()
                if 1 <= i <= 3 * AW + 1:
                    head_norm_sum(i - 1)
                if i > 3 * AW + 1:
                    turn_v(vi, TB)
                    vi += 1
            turn_v(vi, TB)
            vi += 1
            pe.wait_ge(at_q_ready, 3 * AW + 1)
            pe.wait_ge(v_tok_ready, vi)
            pe.wait_ge(vT_ready, vi)
            pe.wait_ge(r0_ready, seen["sum"])

            AH = A_HEADS + B_HEADS

            def at_scores(h):
                r = HD * (h % 2)
                if h < A_HEADS:
                    q, k = qk2[r:r + HD, h // 2, :], qk2[r:r + HD, AW + h // 2, :]
                else:
                    q, k = qk2[r:r + HD, 2 * AW + (h - A_HEADS) // 2, :], kb2[r:r + HD, (h - A_HEADS) // (B_HEADS // B_KV), :]
                if h:
                    pe.wait_ge(at_biased, h)
                for qb, k0, nk, b, c in A_SCORES if h < A_HEADS else B_SCORES:
                    mm = pe.matmul(bank[b][:, c:c + nk * P], q[:, qb * P:(qb + 1) * P], k[:, k0 * P:(k0 + nk) * P], start=True, stop=True)
                mm.then_inc(at_scored, 1)

            def at_turn(h):
                if h:
                    pe.wait_ge(at_pT_ready, h)
                for n, (qb, k0, nk, b, c) in enumerate(A_SCORES if h < A_HEADS else B_SCORES):
                    pe.wait_ge(at_p_ready, TB * h + n + 1)
                    for i in range(nk):
                        tb, tc = next((tb, tc + (qb - q0) * P) for kb, q0, _, tb, tc in (A_TURNED if h < A_HEADS else B_TURNED) if kb == k0 + i)
                        o = b * SEQ + c + i * P
                        mm = pe.transpose(bank[3 + tb][:, tc:tc + P], at_s[h % 3][:, o:o + P], ident)
                mm.then_inc(at_turned, 1)

            def at_values(h):
                pe.wait_ge(at_pT_ready, h + 1)
                if h >= 2:
                    pe.wait_ge(at_o_read, h - 1)
                for kb, q0, nq, b, c in sorted(A_TURNED if h < A_HEADS else B_TURNED):
                    if h < A_HEADS:
                        v = va_tok[:, kb, h * HD:(h + 1) * HD]
                    else:
                        g = (h - A_HEADS) // (B_HEADS // B_KV)
                        v = vb_tok[:, kb, g * HD:(g + 1) * HD]
                    mm = pe.matmul(bank[6 + h % 2][0:HD, q0 * P:(q0 + nq) * P], v, at_pT[h % 2][:, b * SEQ + c:b * SEQ + c + nq * P],
                                   start=(kb == 0), stop=(kb == TB - 1), skip_group_check=True)
                mm.then_inc(at_pv_done, 1)

            at_scores(0)
            at_scores(1)
            for h in range(AH):
                if h + 2 < AH:
                    at_scores(h + 2)
                at_turn(h)
                if h:
                    at_values(h - 1)
            at_values(AH - 1)
            t = stage["attn_out"]
            for i in range(KD):
                tile(t + i, opB, "attn")

            def ffn(layer, gen_in, gen_mid):
                t = stage[f"ffn_in{layer}"]
                for i in range(2 * KF2):
                    tile(t + i, opA, gen_in)
                    if i == 0:
                        norm_sum()
                t = stage[f"ffn_out{layer}"]
                for i in range(KD):
                    tile(t + i, hid2, gen_mid)

            ffn(0, "x4", "ffn0")
            tile(stage["dt"], opA, "x5")
            norm_sum()
            for g in range(SSM_G):
                t = stage[f"ssm{g}"]
                bank_x = g * 5

                def turn_x(j):
                    n = bank_x + j
                    s = bT if j == 0 else xs[:, j - 1, :]
                    pe.wait_ge(gated_ready, GT * g + 1 + SSM_ORDER.index(("b", 0) if j == 0 else ("x", j - 1)))
                    if n >= 2:
                        pe.wait_ge(x_tok_ready, n - 1)
                    for c in range(TB):
                        mm = pe.transpose(bank[5 + n % 2][:, c * P:(c + 1) * P], s[:, c * P:(c + 1) * P], ident)
                    mm.then_inc(xs_turned, 1)

                for j in range(len(SSM_ORDER)):
                    tile(t + j, opA, "x5")
                    if j == 1 and g:
                        norm_sum()
                    if j in SSM_TURN:
                        turn_x(SSM_TURN[j])
                    if j == 3 and g == 0:
                        pe.wait_ge(dt_ready, 1)
                        for c in range(TB):
                            for k, row in enumerate((dt_acsT, dt_dtT, dt_wT)):
                                o = (k * TB + c) * SSM_HEADS
                                pe.transpose(bank[7][:, o:o + SSM_HEADS], row[0:SSM_HEADS, c * P:(c + 1) * P], ident[0:SSM_HEADS, 0:SSM_HEADS])
                        pe.matmul(bank[7][:, 3 * TB * SSM_HEADS:], const("ones")[0:SSM_HEADS, :], dt_last[0:SSM_HEADS, :], start=True, stop=True).then_inc(dt_turned, 1)
                    if j == 5:
                        pe.wait_ge(gated_ready, GT * g + 3)
                        if g == 0:
                            pe.wait_ge(dt_tok_ready, 3)
                        for c in range(TB):
                            mm = pe.matmul(bank[7][:, c * P:(c + 1) * P], bT[:, c * P:(c + 1) * P], cT[:, c * P:(c + 1) * P], start=True, stop=True)
                        mm.then_inc(cb_done, 1)

                def head_row(h):
                    n = g * HPG + h
                    if n >= 2:
                        pe.wait_ge(s_ready, n - 1)
                    sel = ident_r[0:SSM_HEADS, n:n + 1].to_broadcast([SSM_HEADS, P])
                    pe.matmul(bank[4 - n % 2][:, :], sel, dt_acs_hi[0:SSM_HEADS, :], start=True, stop=False, skip_group_check=True)
                    pe.matmul(bank[4 - n % 2][:, :], sel, dt_acs_lo[0:SSM_HEADS, :], start=False, stop=False, skip_group_check=True).then_inc(row_done, 1)

                def head_mask(h):
                    n = g * HPG + h
                    pe.wait_ge(e_ready, n + 1)
                    mask = neg_before_r[:, :].rearrange("p (o l) -> p o l", o=1).to_broadcast([P, TB, P])
                    pe.matmul(bank[4 - n % 2][:, :], ident_r[:, :], mask, start=False, stop=True, skip_group_check=True).then_inc(row_masked, 1)

                def head_out(h):
                    n = g * HPG + h
                    pe.wait_ge(g_ready, n + 1)
                    pe.wait_ge(ec_ready, n + 1)
                    if n >= 2:
                        pe.wait_ge(y_read, n - 1)
                    for c in range(TB):
                        dst = bank[5 + n % 2][0:SSM_P, c * P:(c + 1) * P]
                        mm = pe.matmul(dst, x_tok[:, c, h * SSM_P:(h + 1) * SSM_P], ssm_S[n % 3][:, c * P:(c + 1) * P], start=True, stop=(c == 0))
                        if c:
                            mm = pe.matmul(dst, state[:, c - 1, h * SSM_P:(h + 1) * SSM_P], ssm_E[n % 3][:, c * P:(c + 1) * P], start=False, stop=True)
                    mm.then_inc(y_done, 1)

                pe.wait_ge(r0_ready, seen["sum"])
                if g == 0:
                    pe.wait_ge(dt_acs_split, 1)
                head_row(0)
                pe.wait_ge(to_gate, GT * (g + 1))
                head_row(1)
                pe.wait_ge(x_tok_ready, bank_x + 5)
                pe.wait_ge(cb_ready, g + 1)
                pe.wait_ge(xw_ready, (g + 1) * TPG)
                for c in range(TB - 1):
                    pe.matmul(bank[5 + c][:, :], b_tok[:, c, :], xw[:, c, :], start=True, stop=True).then_inc(upd_done, 1)
                head_mask(0)
                head_mask(1)
                pe.wait_ge(state_ready, (g + 1) * (TB - 1))
                for h in range(HPG):
                    if h + 2 < HPG:
                        head_row(h + 2)
                    head_out(h)
                    if h + 2 < HPG:
                        head_mask(h + 2)
            norm_sum()
            t = stage["ssm_out"]
            for i in range(KD):
                tile(t + i, opY, "ssm")
            ffn(1, "x6", "ffn1")

        @block.scalar
        def _(act):
            lane = Lane(act, act_step)
            n_ = {"src": 0, "sq": 0, "used": 0, "norm": 0, "sig": 0, "v": 0, "sq_in": 0, "hi": 0, "groups": 0}
            act.preload_act_table_set("natural_log_exp_and_others")

            def split(u):
                if u >= NU:
                    return
                _, kt, width = units[u]
                act.wait_ge(unit_loaded[u % RAW], 16 * (u // RAW + 1))
                if u >= SPLIT:
                    act.wait_ge(unit_used, u - SPLIT + 1)
                act.activation(w_hi[u % SPLIT][:, 0:kt, 0:width], raw[u % RAW][:, 0:kt, 0:width], ACT.Copy).then_inc(hi_ready, 1)

            hurried = set()

            def hurry(t):
                ahead(t)
                hurried.add(t)

            def ahead(t):
                if t in hurried:
                    return
                u0, nu, _, _ = tiles[t]
                for u in range(u0, u0 + nu):
                    split(u + 3)

            def high(dst, source, ready=None, ready_n=None):
                if ready is None:
                    n_["src"] += 1
                    act.wait_ge(src_ready, n_["src"])
                else:
                    act.wait_ge(ready, ready_n)
                act.activation(dst, source, ACT.Copy).then_inc(op_hi_done, 1)

            def square(source, m):
                if m == 0:
                    if n_["groups"]:
                        act.wait_ge(ss_added, n_["groups"])
                    n_["groups"] += 1
                if m >= 2:
                    act.wait_ge(sq_used, n_["used"] + m - 1)
                n = source.shape[-1]
                act.activation(sq[m % 2][:, 0:n], source, ACT.Square).then_inc(sq_ready, 1)

            def root(n, count, width):
                n_["norm"] += 1
                n_["used"] += count - 1
                act.wait_ge(ss_summed, n_["norm"])
                if n_["norm"] > 1:
                    act.wait_ge(rstd_ready, n_["norm"] - 1)
                eps = con[:, CON["eps"]:CON["eps"] + 1]
                lane.did(act.activation(norm_ln[:, 0:n], bank[4][:, 0:n], ACT.Ln, bias=eps, scale=1.0 / width))
                lane.did(act.activation(norm_m[:, 0:n], bank[4][:, 0:n], ACT.Identity, bias=eps, scale=1.0 / width))
                lane.sync()
                act.activation(norm_r[:, 0:n], norm_ln[:, 0:n], ACT.Exp, scale=-0.5).then_inc(r0_ready, 1)

            def prepare(k, gain, source=None, dst=opA, first=False):
                if source is None:
                    if not first:
                        n_["src"] += 1
                        act.wait_ge(src_ready, n_["src"])
                    source = x[:, k, :]
                act.activation(dst[0][:, k, :], source, ACT.Copy, scale=gain).then_inc(op_hi_done, 1)
                square(source, k)

            def gate():
                n_["sig"] += 1
                act.wait_ge(sig_in, n_["sig"])
                act.activation(sig[:, :], tmp[:, :], ACT.Sigmoid).then_inc(sig_ready, 1)

            def gated(name, last=False, also=None):
                t = stage[name]
                for i in range(KD):
                    ahead(t + 2 * i)
                    gate()
                    ahead(t + 2 * i + 1)
                    if last:
                        high(opC[0][:, i, :], src[:, :])
                    if also is not None:
                        also(i)
                act.preload_act_table_set("natural_log_exp_and_others")

            def v_out(dst, blocks):
                n = n_["v"]
                n_["v"] += 1
                act.wait_ge(v_turned, n + 1)
                act.activation(dst, bank[5 + n % 2][:, 0:blocks * P].rearrange("p (b c) -> p b c", c=P), ACT.Copy).then_inc(v_tok_ready, 1)

            act.wait_ge(params_in, 16)
            split(0)
            for k in range(KD):
                act.wait_ge(x_in[k // 2], 16)
                prepare(k, col("g_mix", k), first=True)
                if k == 3:
                    split(1)
            split(2)
            act.wait_ge(con_in, 16)
            for dst, name in ((ident_r, "ident"), (neg_later_r, "neg_later"), (neg_ones_r, "neg_ones"), (neg_future_r, "neg_future"), (neg_before_r, "neg_before")):
                act.activation(dst[:, :], const(name), ACT.Copy).then_inc(con_r_ready, 1)
            root(SEQ, KD, D)
            t = stage["conv"]
            for i in range(KD):
                for j in range(3):
                    ahead(t + 3 * i + j)
                high(opB[0][:, i, :], src[:, :])
            gated("conv_out")
            t = stage["qkv"]
            for i in range(3 * KD):
                ahead(t + i)
                if i > 2 * KD:
                    v_out(v_tok[:, :, (i - 1 - 2 * KD) * P:(i - 2 * KD) * P], TB)
            v_out(v_tok[:, :, (KD - 1) * P:KD * P], TB)

            SPANS = ((0, 0, 512), (1, 512, 512), (2, 1024, 256))

            def sb_soft(h):
                act.wait_ge(sb_scored, h + 1)
                if h:
                    act.wait_ge(sb_sp_ready, 3 * h)
                for b, c, w in SPANS:
                    lane.did(act.activation(sb_e[:, c:c + w], bank[4 * (h % 2) + b][:, 0:w], ACT.Abs), sb_abs_done)
                lane.sync()
                for b, c, w in SPANS:
                    lane.did(act.activation(sb_e[:, c:c + w], sb_e[:, c:c + w], ACT.Exp, scale=-1.0))
                if h >= 3:
                    sb_high(h - 3)
                lane.sync()
                for b, c, w in SPANS:
                    act.activation(sb_e[:, c:c + w], sb_e[:, c:c + w], ACT.Ln, bias=1.0).then_inc(sb_exp_ready, 1)

            def sb_weights(h):
                act.wait_ge(sb_summed, h + 1)
                if h >= 2:
                    act.wait_ge(sb_pv_done, h - 1)
                for b, c, w in SPANS:
                    act.activation(sb_a[h % 2][:, c:c + w], bank[4 * (h % 2) + b][:, 0:w], ACT.Exp).then_inc(sb_a_ready, 1)

            def sb_high(h):
                if h % 2:
                    high(opC[0][:, h // 2, :], src[:, :], sb_o_read, h + 1)

            def sb_sp_high(h):
                for i, (b, c, w) in enumerate(SPANS):
                    act.wait_ge(sb_sp_ready, 3 * h + i + 1)
                    act.activation(sb_sp_hi[h % 2][:, c:c + w], sb_sp[h % 2][:, c:c + w], ACT.Copy).then_inc(sb_hi_ready, 1)

            sb_soft(0)
            sb_sp_high(0)
            for h in range(SB_HEADS):
                if h + 1 < SB_HEADS:
                    sb_soft(h + 1)
                sb_weights(h)
                if h + 1 < SB_HEADS:
                    sb_sp_high(h + 1)
            for h in range(SB_HEADS - 3, SB_HEADS):
                sb_high(h)
            def mem_operand(i):
                if i == KD // 2:
                    act.wait_ge(mem_in, 16)
                for k in range(2 * i - KD, 2 * i - KD + 2):
                    if k >= 0:
                        prepare(k, col("g_mem", k), memx[:, k, :], opM)

            gated("sb_out", also=mem_operand)
            root(MEM, KD, D)
            t = stage["mem_kv"]
            for i in range(2 * KD):
                if i and i % 2 == 0 and i <= KD:
                    root(MEM, 2, X_DIM)
                ahead(t + i)
                if i < KD:
                    n_["sq_in"] += 1
                    act.wait_ge(sq_in, n_["sq_in"])
                    square(xk[:, i, :], i % 2)
                if i > KD:
                    v_out(xv_tok[:, :, (i - 1 - KD) * P:(i - KD) * P], MEM // P)
            v_out(xv_tok[:, :, (KD - 1) * P:KD * P], MEM // P)

            XS = float(X_DIM) ** -0.5

            def x_exp(h):
                act.wait_ge(x_max_ready, h + 1)
                if h >= 2:
                    act.wait_ge(x_turned, 2 * (h - 1))
                o = 32 * (h % 2)
                for qb in range(TB):
                    act.activation(x_p[h % 2][:, qb, :], bank[5 + qb // 2][:, (qb % 2) * MEM:(qb % 2 + 1) * MEM], ACT.Exp,
                                   bias=small[:, o + TB + qb:o + TB + qb + 1], scale=XS,
                                   accum_out=small[:, o + 2 * TB + qb:o + 2 * TB + qb + 1]).then_inc(x_exp_ready, 1)

            t = stage["xq"]
            for i in range(KD):
                if i and i % 2 == 0:
                    root(SEQ, 2, X_DIM)
                ahead(t + i)
                n_["sq_in"] += 1
                act.wait_ge(sq_in, n_["sq_in"])
                square(xq[:, i, :], i % 2)
                if i == 6:
                    x_exp(0)
            root(SEQ, 2, X_DIM)
            for h in range(X_HEADS):
                for kb in range(2):
                    act.wait_ge(x_turned, 2 * h + kb + 1)
                    if h:
                        act.wait_ge(x_pv_done, 2 * h)
                    act.activation(x_pT[:, kb, :], bank[2 + kb][:, :], ACT.Copy).then_inc(x_pT_ready, 1)
                if h + 1 < X_HEADS:
                    x_exp(h + 1)
                for d in range(2):
                    high(opB[0][:, 2 * h + d, :], src[:, :], x_o_read, 2 * h + d + 1)
            gated("x_out", last=True)

            def residual(name, gain=None, width_g=None):
                t = stage[name]
                for i in range(KD):
                    ahead(t + i)
                    if gain is not None:
                        prepare(i, col(*gain[0:1], gain[1] + i))
                if gain is not None:
                    root(SEQ, KD, D)

            residual("w_out", ("g_mlp", 0))
            for half in range(FF1 // P // MLP_HALF):
                t = stage[f"up{half}"]
                for i in range(MLP_HALF):
                    ahead(t + i)
                    high(hid1[0][:, i, :], src[:, :])
                if half == 0:
                    for h in range(A_HEADS):
                        act.wait_ge(strip_flipped, h + 1)
                        act.activation(strip[:, h, :], bank[5 + h % 2][:, :], ACT.Copy).then_inc(strip_turned, 1)
                residual(f"down{half}", ("norm_mix_2", 0) if half else None)
            t = stage["attn_in"]
            for i in range(4 * AW + 2):
                if 1 <= i <= 3 * AW + 1:
                    root(SEQ, 1, HD)
                ahead(t + i)
                if i <= 3 * AW:
                    n_["sq_in"] += 1
                    act.wait_ge(sq_in, n_["sq_in"])
                    if i >= 2:
                        act.wait_ge(ss_summed, n_["norm"])
                    act.activation(sq[i % 2][:, :], qk2[:, i, :] if i < 3 * AW else src[:, :], ACT.Square).then_inc(sq_ready, 1)
                if i > 3 * AW + 1:
                    j = i - 1 - (3 * AW + 1)
                    v_out(va_tok[:, :, j * P:(j + 1) * P], TB)
            v_out(vb_tok[:, :, :], TB)

            AH = A_HEADS + B_HEADS

            def at_exp(h):
                act.wait_ge(at_max_ready, h + 1)
                o = 32 * (h % 2)
                if h >= A_HEADS:
                    act.activation(small[:, o + 3 * TB:o + 4 * TB], small[:, o + TB:o + 2 * TB], ACT.Exp, bias=col("sinks_2", h - A_HEADS)).then_inc(at_exp_ready, 1)
                for qb, _, nk, b, c in A_SCORES if h < A_HEADS else B_SCORES:
                    s_ = at_s[h % 3][:, b * SEQ + c:b * SEQ + c + nk * P]
                    act.activation(s_, s_, ACT.Exp, bias=small[:, o + TB + qb:o + TB + qb + 1],
                                   accum_out=small[:, o + 2 * TB + qb:o + 2 * TB + qb + 1]).then_inc(at_exp_ready, 1)

            at_exp(0)
            for h in range(AH):
                if h + 1 < AH:
                    at_exp(h + 1)
                act.wait_ge(at_turned, h + 1)
                if h >= 2:
                    act.wait_ge(at_pv_done, h - 1)
                spans = A_SPANS if h < A_HEADS else B_SPANS
                for b, n in spans:
                    ins = act.activation(at_pT[h % 2][:, b * SEQ:b * SEQ + n], bank[3 + b][:, 0:n], ACT.Copy)
                    if b == len(spans) - 1:
                        ins.then_inc(at_pT_ready, 1)
                    else:
                        lane.did(ins)
                        if b == len(spans) - 2:
                            lane.sync()
                if h and h % 2 == 0:
                    high(opB[0][:, (h - 1) // 2, :], src[:, :], at_o_read, h)
            high(opB[0][:, KD - 1, :], src[:, :], at_o_read, AH)
            residual("attn_out", ("norm_ffn_2", 0))

            def ffn(layer, after):
                t = stage[f"ffn_in{layer}"]
                for i in range(KF2):
                    ahead(t + 2 * i)
                    gate()
                    ahead(t + 2 * i + 1)
                    high(hid2[0][:, i, :], src[:, :])
                act.preload_act_table_set("natural_log_exp_and_others")
                residual(f"ffn_out{layer}", after)

            ffn(0, ("norm_mix_2", KD))
            S32 = SSM_HEADS
            ahead(stage["dt"])
            act.wait_ge(dt_in, 1)
            lane.did(act.activation(dt_e[0:S32, :], dt_m[0:S32, :], ACT.Abs))
            lane.did(act.activation(small[0:S32, 0:1], col("a_log")[0:S32, :], ACT.Exp))
            lane.sync()
            act.activation(dt_e[0:S32, :], dt_e[0:S32, :], ACT.Exp, scale=-1.0).then_inc(dt_exp, 1)
            act.wait_ge(dt_ln_in, 1)
            act.activation(dt_wT[0:S32, :], dt_d[0:S32, :], ACT.Ln).then_inc(dt_ln, 1)
            hurry(stage["ssm0"])
            act.wait_ge(dt_acs, TB)
            for c in range(TB):
                act.activation(dt_wT[0:S32, c * P:(c + 1) * P], dt_acsT[0:S32, c * P:(c + 1) * P], ACT.Exp,
                               bias=dt_acsT[0:S32, c * P + P - 1:c * P + P], scale=-1.0).then_inc(dt_w, 1)
            act.activation(dt_acs_hi[0:S32, :], dt_acsT[0:S32, :], ACT.Copy).then_inc(dt_acs_high, 1)
            xt = [0]

            def x_out_tok(dst):
                n = xt[0]
                xt[0] += 1
                act.wait_ge(xs_turned, n + 1)
                act.activation(dst, bank[5 + n % 2][:, :].rearrange("p (b c) -> p b c", c=P), ACT.Copy).then_inc(x_tok_ready, 1)

            for g in range(SSM_G):
                t = stage[f"ssm{g}"]
                for j, (kind, i) in enumerate(SSM_ORDER):
                    ahead(t + j)
                    if kind == "x" and g:
                        high(opY[0][:, (g - 1) * TPG + i, :], src[:, :])
                    n = GT * g + j
                    act.wait_ge(to_gate, n + 1)
                    if n:
                        act.wait_ge(gated_ready, n)
                    act.activation(sig[:, :], (tmp, tmp2)[n % 2][:, :], ACT.Sigmoid).then_inc(gate_ready, 1)
                    if j == 1 and g:
                        act.preload_act_table_set("natural_log_exp_and_others")
                        root(SEQ, TPG, SSM_IN // SSM_G)
                    if j in SSM_TURN:
                        i = SSM_TURN[j]
                        x_out_tok(x_tok[:, :, (i - 1) * P:i * P] if i else b_tok[:, :, :])
                    if j == 3 and g == 0:
                        act.wait_ge(dt_turned, 1)
                        n = TB * S32
                        act.activation(dt_tok[:, 0, :, :].rearrange("p b c -> p (b c)"), bank[7][:, 0:n], ACT.Copy, scale=-1.0).then_inc(dt_tok_ready, 1)
                        act.activation(dt_tok[:, 1:3, :, :].rearrange("p a b c -> p (a b c)"), bank[7][:, n:3 * n], ACT.Copy).then_inc(dt_tok_ready, 1)
                        act.activation(e_last[:, :, :].rearrange("p b c -> p (b c)"), bank[7][:, 3 * n:], ACT.Exp).then_inc(dt_tok_ready, 1)
                act.preload_act_table_set("natural_log_exp_and_others")

                def decay(h):
                    n = g * HPG + h
                    row = bank[4 - n % 2]
                    act.wait_ge(row_done, n + 1)
                    if n >= 3:
                        act.wait_ge(y_done, n - 2)
                    act.activation(ssm_E[n % 3][:, :], row[:, :], ACT.Exp).then_inc(e_ready, 1)
                    act.wait_ge(row_masked, n + 1)
                    for c in range(TB):
                        cc = slice(c * P, (c + 1) * P)
                        ins = act.activation(ssm_S[n % 3][:, cc], row[:, cc], ACT.Exp, bias=dt_tok[:, 0, c, n:n + 1])
                        if c == TB - 1:
                            ins.then_inc(s_ready, 1)
                        else:
                            lane.did(ins)
                            if c == TB - 2:
                                lane.sync()

                act.wait_ge(gated_ready, GT * (g + 1))
                for h in range(HPG):
                    decay(h)
                n_["sq_in"] += TPG
                act.wait_ge(sq_in, n_["sq_in"])
                for j in range(TPG):
                    square(xs[:, j, :], j)
            root(SEQ, TPG, SSM_IN // SSM_G)
            for j in range(TPG):
                high(opY[0][:, (SSM_G - 1) * TPG + j, :], src[:, :])
            residual("ssm_out", ("norm_ffn_2", KD))
            ffn(1, None)

        @block.vector
        def _(dve):
            lane = Lane(dve, dve_step)
            did, sync = lane.did, lane.sync
            n_ = {"hi": 0, "sq": 0, "norm": 0, "sig": 0, "v": 0}
            V = nc.vector

            def split(u):
                if u >= NU:
                    return
                _, kt, width = units[u]
                dve.wait_ge(hi_ready, u + 1)
                did(V.tensor_tensor(w_lo[u % SPLIT][:, 0:kt, 0:width], raw[u % RAW][:, 0:kt, 0:width],
                                    w_hi[u % SPLIT][:, 0:kt, 0:width].bitcast(F32), ALU.subtract), lo_ready)

            hurried = set()

            def hurry(t):
                ahead(t)
                hurried.add(t)

            def ahead(t):
                if t in hurried:
                    return
                sync()
                u0, nu, _, _ = tiles[t]
                for u in range(u0, u0 + nu):
                    split(u + 2)

            def arrive(t, n=SEQ):
                dve.wait_ge(unit_used, last_unit(t) + 1)
                return bank[t % 4][0:tiles[t][3], 0:n]

            def low(dst, source, gain=None):
                n_["hi"] += 1
                dve.wait_ge(op_hi_done, n_["hi"])
                sync()
                if gain is None:
                    did(V.tensor_tensor(dst[1], source, dst[0].bitcast(F32), ALU.subtract), op_ready)
                else:
                    did(V.scalar_tensor_tensor(dst[1], source, gain, dst[0].bitcast(F32), ALU.mult, ALU.subtract), op_ready)

            def pair(op, k):
                return op[0][:, k, :], op[1][:, k, :]

            def add_square(m, count, n=SEQ):
                n_["sq"] += 1
                dve.wait_ge(sq_ready, n_["sq"])
                sync()
                s = ss_added if m == count - 1 else sq_used
                if m == 0:
                    did(V.tensor_copy(ss[:, 0:n], sq[0][:, 0:n]), s)
                else:
                    did(V.tensor_tensor(ss[:, 0:n], ss[:, 0:n], sq[m % 2][:, 0:n], ALU.add), s)

            def norm(dst, n, width):
                n_["norm"] += 1
                dve.wait_ge(r0_ready, n_["norm"])
                sync()
                m, r = norm_m[:, 0:n], norm_r[:, 0:n]
                did(V.tensor_tensor(m, m, r, ALU.mult))
                sync()
                did(V.scalar_tensor_tensor(m, m, -0.5, r, ALU.mult, ALU.mult))
                sync()
                did(V.scalar_tensor_tensor(dst, m, 1.5, r, ALU.add, ALU.mult), rstd_ready)
                sync()

            def wait_gate():
                n_["sig"] += 1
                dve.wait_ge(sig_ready, n_["sig"])

            R = rstd[:, :]

            def gated(name, first=False, last=False, also=None):
                t = stage[name]
                for i in range(KD):
                    ahead(t + 2 * i)
                    did(V.tensor_tensor(tmp[:, :], arrive(t + 2 * i), R, ALU.mult), sig_in)
                    ahead(t + 2 * i + 1)
                    y = arrive(t + 2 * i + 1)
                    wait_gate()
                    if first:
                        did(V.tensor_tensor(merged[:, i, :], sig[:, :], y, ALU.mult))
                        continue
                    did(V.tensor_tensor(tmp2[:, :], sig[:, :], y, ALU.mult))
                    sync()
                    if last:
                        did(V.tensor_tensor(src[:, :], merged[:, i, :], tmp2[:, :], ALU.add), src_ready)
                        low(pair(opC, i), src[:, :])
                    else:
                        did(V.tensor_tensor(merged[:, i, :], merged[:, i, :], tmp2[:, :], ALU.add))
                    if also is not None:
                        also(i)
                sync()

            def conv(dst, taps, name, index, stride, bias=None, ready=sig_in):
                for j in range(taps):
                    s = pad[:, 4 - taps + j:4 - taps + j + SEQ]
                    w = col(name, j * stride + index)
                    sync()
                    if j == 0:
                        if bias is None:
                            did(V.tensor_scalar(dst, s, w, None, ALU.mult))
                        else:
                            did(V.tensor_scalar(dst, s, w, bias, ALU.mult, ALU.add))
                    else:
                        did(V.scalar_tensor_tensor(dst, s, w, dst, ALU.mult, ALU.add), *((ready,) if j == taps - 1 and bias is not None else ()))

            def v_in(t, r, n):
                i = n_["v"]
                n_["v"] += 1
                if i >= 2:
                    dve.wait_ge(v_turned, i - 1)
                did(V.tensor_tensor((tmp if i % 2 == 0 else tmp2)[:, 0:n], arrive(t, n), r, ALU.mult), vT_ready)

            did(V.memset(pad[:, 0:3], 0.0))
            dve.wait_ge(params_in, 16)
            split(0)
            for k in range(KD):
                dve.wait_ge(x_in[k // 2], 16)
                low(pair(opA, k), x[:, k, :], col("g_mix", k))
                add_square(k, KD)
                if k == 3:
                    split(1)
            dve.wait_ge(con_in, 16)
            did(V.tensor_scalar(col("q_norm_a_2"), col("q_norm_a_2"), HD ** -0.5, None, ALU.mult))
            did(V.tensor_scalar(col("q_norm_b_2"), col("q_norm_b_2"), HD ** -0.5, None, ALU.mult))
            norm(R, SEQ, D)
            t = stage["conv"]
            for i in range(KD):
                ahead(t + 3 * i)
                did(V.tensor_tensor(tmp2[:, :], arrive(t + 3 * i), R, ALU.mult))
                ahead(t + 3 * i + 1)
                did(V.tensor_tensor(tmp[:, :], arrive(t + 3 * i + 1), R, ALU.mult))
                sync()
                did(V.tensor_tensor(pad[:, 3:3 + SEQ], tmp[:, :], tmp2[:, :], ALU.mult))
                conv(tmp[:, :], 3, "conv_w", i, KD)
                ahead(t + 3 * i + 2)
                did(V.tensor_tensor(tmp2[:, :], arrive(t + 3 * i + 2), R, ALU.mult))
                sync()
                did(V.tensor_tensor(src[:, :], tmp2[:, :], tmp[:, :], ALU.mult), src_ready)
                low(pair(opB, i), src[:, :])
            gated("conv_out", first=True)
            t = stage["qkv"]
            for i in range(3 * KD):
                ahead(t + i)
                if i < KD:
                    did(V.scalar_tensor_tensor(qT[:, i, :], arrive(t + i), SB_DIM ** -0.5, R, ALU.mult, ALU.mult))
                elif i < 2 * KD:
                    did(V.tensor_tensor(kT[:, i - KD, :], arrive(t + i), R, ALU.mult))
                else:
                    v_in(t + i, R, SEQ)
            sync()

            SPANS = ((0, 0, 512), (1, 512, 512), (2, 1024, 256))

            def sb_softplus(h):
                s_ = sb_sp[h % 2]
                if h >= 2:
                    dve.wait_ge(sb_summed, h - 1)
                past = const("past")
                for i, (b, c, w) in enumerate(SPANS):
                    dve.wait_ge(sb_exp_ready, 3 * h + i + 1)
                    did(V.scalar_tensor_tensor(s_[:, c:c + w], bank[4 * (h % 2) + b][:, 0:w], 0.0, sb_e[:, c:c + w], ALU.max, ALU.add))
                    sync()
                    if i == 1:
                        own = s_[:, c:c + w].rearrange("p (b k) -> p b k", k=P)[:, 0:TB:TB - 1, :]
                        did(V.tensor_tensor(own, own, past.rearrange("p (o k) -> p o k", o=1).to_broadcast([P, 2, P]), ALU.mult), sb_sp_ready)
                    else:
                        did(V.tensor_tensor(s_[:, c:c + P], s_[:, c:c + P], past, ALU.mult), sb_sp_ready)

            def sb_low(h):
                for i, (b, c, w) in enumerate(SPANS):
                    dve.wait_ge(sb_hi_ready, 3 * h + i + 1)
                    if i == 0:
                        sync()
                    did(V.tensor_tensor(sb_sp_lo[h % 2][:, c:c + w], sb_sp[h % 2][:, c:c + w], sb_sp_hi[h % 2][:, c:c + w].bitcast(F32), ALU.subtract), sb_lo_ready)

            def sb_out(h):
                r = HD * (h % 2)
                dve.wait_ge(sb_pv_done, h + 1)
                sync()
                did(V.tensor_copy(src[r:r + HD, :], bank[3 + 4 * (h % 2)][0:HD, :]), sb_o_read)
                if h % 2:
                    low(pair(opC, h // 2), src[:, :])

            sb_softplus(0)
            sb_low(0)
            for h in range(SB_HEADS):
                if h + 1 < SB_HEADS:
                    sb_softplus(h + 1)
                    sb_low(h + 1)
                if h >= 1:
                    sb_out(h - 1)
            sb_out(SB_HEADS - 1)
            def mem_operand(i):
                if i == KD // 2:
                    dve.wait_ge(mem_in, 16)
                for k in range(2 * i - KD, 2 * i - KD + 2):
                    if k >= 0:
                        low(pair(opM, k), memx[:, k, :], col("g_mem", k))
                        add_square(k, KD, MEM)

            gated("sb_out", also=mem_operand)
            RM = rstd_m[:, :]
            hurry(stage["mem_kv"])
            norm(RM, MEM, D)

            def head_norm(dst, k, n, r, name, ready=None):
                norm(sig[:, 0:n], n, X_DIM)
                for j in range(2):
                    did(V.scalar_tensor_tensor(dst[:, k + j, :], dst[:, k + j, :], col(name, j), sig[:, 0:n], ALU.mult, ALU.mult), *((ready,) if ready else ()))

            t = stage["mem_kv"]
            for i in range(2 * KD):
                ahead(t + i)
                if i < KD:
                    did(V.tensor_tensor(xk[:, i, :], arrive(t + i, MEM), RM, ALU.mult), sq_in)
                else:
                    v_in(t + i, RM, MEM)
                if i and i % 2 == 0 and i <= KD:
                    head_norm(xk, i - 2, MEM, RM, "k_norm_g")
                if i < KD and i % 2:
                    for j in range(2):
                        add_square(j, 2, MEM)

            def x_max(h):
                o = 32 * (h % 2)
                dve.wait_ge(x_scored, h + 1)
                for b in range(2):
                    did(V.tensor_reduce(small[:, o + 2 * b:o + 2 * b + 2], bank[5 + b][:, :].rearrange("p (q k) -> p q k", k=MEM), AX.X, ALU.max))
                sync()
                did(V.tensor_scalar(small[:, o + TB:o + 2 * TB], small[:, o:o + TB], -float(X_DIM) ** -0.5, None, ALU.mult), x_max_ready)

            def x_share(h):
                o = 32 * (h % 2)
                dve.wait_ge(x_exp_ready, TB * (h + 1))
                did(V.reciprocal(small[:, o + 3 * TB:o + 4 * TB], small[:, o + 2 * TB:o + 3 * TB]))
                sync()
                for qb in range(TB):
                    ins = V.tensor_scalar(x_p[h % 2][:, qb, :], x_p[h % 2][:, qb, :], small[:, o + 3 * TB + qb:o + 3 * TB + qb + 1], None, ALU.mult)
                    if qb == TB - 1:
                        sync()
                        did(ins, x_p_ready)
                    else:
                        did(ins)

            t = stage["xq"]
            for i in range(KD):
                ahead(t + i)
                did(V.tensor_tensor(xq[:, i, :], arrive(t + i), R, ALU.mult), sq_in)
                if i and i % 2 == 0:
                    head_norm(xq, i - 2, SEQ, R, "q_norm_g", xq_ready)
                if i % 2:
                    for j in range(2):
                        add_square(j, 2)
                if i == 6:
                    x_max(0)
                if i == 7:
                    x_share(0)
            head_norm(xq, KD - 2, SEQ, R, "q_norm_g", xq_ready)
            sync()
            for h in range(X_HEADS):
                if h + 1 < X_HEADS:
                    x_max(h + 1)
                    x_share(h + 1)
                for d in range(2):
                    n = 2 * h + d
                    dve.wait_ge(x_pv_done, n + 1)
                    sync()
                    did(V.tensor_copy(src[:, :], bank[d][:, :]), x_o_read)
                    low(pair(opB, n), src[:, :])
            gated("x_out", last=True)
            dve.sem_inc(strip_zone_free, 1)

            def residual(name, prep=None, result=False):
                t = stage[name]

                def finish(k):
                    low(pair(opA, k), x[:, k, :], col(prep[0], prep[1] + k))
                    add_square(k, KD)

                for i in range(KD):
                    ahead(t + i)
                    did(V.tensor_tensor(x[:, i, :], x[:, i, :], arrive(t + i), ALU.add), *((src_ready,) if prep else (out_ready,) if result else ()))
                    if prep and i:
                        finish(i - 1)
                if prep:
                    finish(KD - 1)
                    hurry(t + KD)
                    norm(R, SEQ, D)

            residual("w_out", ("g_mlp", 0))
            for half in range(FF1 // P // MLP_HALF):
                t = stage[f"up{half}"]
                for i in range(MLP_HALF):
                    ahead(t + i)
                    did(V.tensor_tensor(tmp[:, :], arrive(t + i), R, ALU.mult))
                    sync()
                    did(V.scalar_tensor_tensor(src[:, :], tmp[:, :], 0.0, tmp[:, :], ALU.max, ALU.mult), src_ready)
                    low(pair(hid1, i), src[:, :])
                if half:
                    dve.wait_ge(strip_turned, A_HEADS)
                    did(V.memset(strip[0:HD, :, SEQ - HD:SEQ], -BIG))
                residual(f"down{half}", ("norm_mix_2", 0) if half else None)
            t = stage["attn_in"]
            for i in range(4 * AW + 2):
                ahead(t + i)
                if i > 3 * AW:
                    v_in(t + i, R, SEQ)
                else:
                    did(V.tensor_tensor(qk2[:, i, :] if i < 3 * AW else src[:, :], arrive(t + i), R, ALU.mult), sq_in)
                    n_["sq"] += 1
                if 1 <= i <= 3 * AW + 1:
                    d = qk2[:, i - 1, :] if i - 1 < 3 * AW else src[:, :]
                    norm(sig[:, :], SEQ, HD)
                    name = ("q_norm_a_2", "k_norm_a_2", "q_norm_b_2", "k_norm_b_2")[(i - 1) // AW]
                    did(V.scalar_tensor_tensor(d, d, col(name), sig[:, :], ALU.mult, ALU.mult), at_q_ready)
                if i == 3 * AW + 1:
                    sync()
                    for kv in range(B_KV):
                        for half in range(2):
                            did(V.tensor_copy(kb2[half * HD:(half + 1) * HD, kv, :], src[kv * HD:(kv + 1) * HD, :]))
            sync()

            AH = A_HEADS + B_HEADS

            def at_max(h):
                o = 32 * (h % 2)
                s_ = at_s[h % 3]
                dve.wait_ge(at_scored, h + 1)
                if h >= 3:
                    dve.wait_ge(at_turned, h - 2)
                sync()
                rows = A_SCORES if h < A_HEADS else B_SCORES
                for qb, _, nk, b, c in rows:
                    w = nk * P
                    part, ps = s_[:, b * SEQ + c:b * SEQ + c + w], bank[b][:, c:c + w]
                    if h < A_HEADS:
                        ins = V.tensor_tensor(part, ps, strip[:, h, SEQ - w:SEQ], ALU.add)
                    else:
                        dist = con[:, CON["dist_b"] + 2 * P - w:CON["dist_b"] + 2 * P]
                        ins = V.scalar_tensor_tensor(part, dist, 2.0 ** (-8.0 * (h - A_HEADS + 1) / B_HEADS), ps, ALU.mult, ALU.add)
                    if qb == rows[-1][0]:
                        sync()
                        did(ins, at_biased)
                    else:
                        did(ins)
                sync()
                for qb, _, nk, b, c in rows:
                    did(V.tensor_reduce(small[:, o + qb:o + qb + 1], s_[:, b * SEQ + c:b * SEQ + c + nk * P], AX.X, ALU.max))
                sync()
                if h >= A_HEADS:
                    did(V.tensor_scalar(small[:, o + TB:o + 2 * TB], small[:, o:o + TB], col("sinks_2", h - A_HEADS), -1.0, ALU.max, ALU.mult), at_max_ready)
                else:
                    did(V.tensor_scalar(small[:, o + TB:o + 2 * TB], small[:, o:o + TB], -1.0, None, ALU.mult), at_max_ready)

            def at_out(h):
                r = HD * (h % 2)
                dve.wait_ge(at_pv_done, h + 1)
                sync()
                did(V.tensor_copy(src[r:r + HD, :], bank[6 + h % 2][0:HD, :]), at_o_read)
                if h % 2:
                    low(pair(opB, h // 2), src[:, :])

            def at_share(h):
                o = 32 * (h % 2)
                rows = A_SCORES if h < A_HEADS else B_SCORES
                dve.wait_ge(at_exp_ready, TB * (h + 1) + max(0, h + 1 - A_HEADS))
                total, share = small[:, o + 2 * TB:o + 3 * TB], small[:, o:o + TB]
                if h >= A_HEADS:
                    did(V.tensor_tensor(total, total, small[:, o + 3 * TB:o + 4 * TB], ALU.add))
                    sync()
                did(V.reciprocal(share, total))
                sync()
                for qb, _, nk, b, c in rows:
                    s_ = at_s[h % 3][:, b * SEQ + c:b * SEQ + c + nk * P]
                    did(V.tensor_scalar(s_, s_, small[:, o + qb:o + qb + 1], None, ALU.mult), at_p_ready)

            at_max(0)
            at_max(1)
            for h in range(AH):
                at_share(h)
                if h + 2 < AH:
                    at_max(h + 2)
                if h:
                    at_out(h - 1)
            at_out(AH - 1)
            residual("attn_out", ("norm_ffn_2", 0))

            def ffn(layer, after):
                t = stage[f"ffn_in{layer}"]
                for i in range(KF2):
                    ahead(t + 2 * i)
                    did(V.tensor_tensor(pad[:, 3:3 + SEQ], arrive(t + 2 * i), R, ALU.mult))
                    conv(tmp[:, :], 3, "ffn_conv_w_2", layer * 3 * KF2 + i, KF2, col("ffn_conv_b_2", layer * KF2 + i))
                    ahead(t + 2 * i + 1)
                    did(V.tensor_tensor(tmp2[:, :], arrive(t + 2 * i + 1), R, ALU.mult))
                    sync()
                    wait_gate()
                    did(V.tensor_tensor(tmp2[:, :], tmp2[:, :], sig[:, :], ALU.mult))
                    sync()
                    did(V.tensor_tensor(src[:, :], tmp2[:, :], tmp[:, :], ALU.mult), src_ready)
                    low(pair(hid2, i), src[:, :])
                residual(f"ffn_out{layer}", after, result=(layer == 1))

            ffn(0, ("norm_mix_2", KD))
            S32 = SSM_HEADS
            t = stage["dt"]
            ahead(t)
            e, v, u, lnu, dtT = dt_e[0:S32, :], dt_m[0:S32, :], dt_d[0:S32, :], dt_wT[0:S32, :], dt_dtT[0:S32, :]
            did(V.tensor_tensor(v, arrive(t), rstd[0:S32, :], ALU.mult))
            sync()
            did(V.tensor_scalar(v, v, col("dt_bias")[0:S32, :], None, ALU.add), dt_in)
            hurry(stage["ssm0"])
            dve.wait_ge(dt_exp, 1)
            did(V.tensor_scalar(u, e, 1.0, None, ALU.add), dt_ln_in)
            dve.wait_ge(dt_ln, 1)
            sync()
            did(V.tensor_scalar(u, u, -1.0, None, ALU.add))
            sync()
            z = tmp[0:S32, :]
            did(V.tensor_scalar(z, u, 0.0, None, ALU.is_equal))
            sync()
            did(V.tensor_tensor(u, u, z, ALU.add))
            did(V.tensor_tensor(lnu, lnu, z, ALU.add))
            sync()
            hurry(stage["ssm0"] + 1)
            did(V.reciprocal(u, u))
            did(V.tensor_tensor(lnu, lnu, e, ALU.mult))
            sync()
            did(V.tensor_tensor(lnu, lnu, u, ALU.mult))
            sync()
            did(V.scalar_tensor_tensor(dtT, v, 0.0, lnu, ALU.max, ALU.add))
            sync()
            did(V.tensor_scalar(u, dtT, small[0:S32, 0:1], -1.0, ALU.mult, ALU.mult))
            sync()
            for c in range(TB):
                cc = slice(c * P, (c + 1) * P)
                did(V.tensor_tensor_scan(dt_acsT[0:S32, cc], const("ones")[0:S32, :], u[:, cc], 0.0, ALU.mult, ALU.add), dt_acs)
            dve.wait_ge(dt_w, TB)
            sync()
            for c in range(TB):
                if c == TB - 1:
                    sync()
                did(V.tensor_scalar(dt_last[0:S32, c * S32:(c + 1) * S32], ident[0:S32, 0:S32], dt_acsT[0:S32, c * P + P - 1:c * P + P], None, ALU.mult),
                    *((dt_ready,) if c == TB - 1 else ()))

            def y_operand(g, j):
                sync()
                did(V.scalar_tensor_tensor(src[:, :], xs[:, j, :], col("ssm_norm_2", g * TPG + j), z_rstd[:, :], ALU.mult, ALU.mult), src_ready)
                low(pair(opY, g * TPG + j), src[:, :])

            for g in range(SSM_G):
                t = stage[f"ssm{g}"]
                for j, (kind, i) in enumerate(SSM_ORDER):
                    ahead(t + j)
                    n = GT * g + j
                    into = (tmp, tmp2)[n % 2][:, :]
                    if n >= 2:
                        dve.wait_ge(gated_ready, n - 1)
                    sync()
                    if kind == "z":
                        did(V.tensor_tensor(into, arrive(t + j), R, ALU.mult), to_gate)
                        continue
                    if kind == "x" and g:
                        y_operand(g - 1, i)
                    ch = {"b": 4 * TPG + g, "c": 4 * TPG + SSM_G + g, "x": g * TPG + i}[kind]
                    did(V.tensor_tensor(pad[:, 3:3 + SEQ], arrive(t + j), R, ALU.mult))
                    conv(into, 4, "ssm_conv_w_2", ch, 24, col("ssm_conv_b_2", ch), to_gate)
                    if j == 2 and g:
                        norm(z_rstd[:, :], SEQ, SSM_IN // SSM_G)
                    if j == 6:
                        if g == 0:
                            dve.wait_ge(dt_acs_high, 1)
                            dve.wait_ge(dt_turned, 1)
                            did(V.tensor_tensor(dt_acs_lo[0:S32, :], dt_acsT[0:S32, :], dt_acs_hi[0:S32, :].bitcast(F32), ALU.subtract), dt_acs_split)
                        dve.wait_ge(cb_done, g + 1)
                        did(V.tensor_tensor(cbm[:, :, :], bank[7][:, :].rearrange("p (c l) -> p c l", l=P),
                                            const("causal").rearrange("p (o l) -> p o l", o=1).to_broadcast([P, TB, P]), ALU.mult), cb_ready)
                sync()
                if g + 1 < SSM_G:
                    hurry(stage[f"ssm{g + 1}"])
                h0 = g * HPG
                for c in range(TB - 1):
                    dve.wait_ge(upd_done, g * (TB - 1) + c + 1)
                    if c == 0:
                        did(V.tensor_copy(state[:, 0, :], bank[5][:, :]), state_ready)
                    else:
                        d = e_last[:, c, h0:h0 + HPG].rearrange("p (h o) -> p h o", o=1).to_broadcast([P, HPG, SSM_P])
                        s_ = state[:, c, :]
                        if c == 1:
                            dve.wait_ge(dt_tok_ready, 3)
                        sync()
                        did(V.tensor_tensor(s_.rearrange("p (h d) -> p h d", d=SSM_P), state[:, c - 1, :].rearrange("p (h d) -> p h d", d=SSM_P), d, ALU.mult))
                        sync()
                        did(V.tensor_tensor(s_, s_, bank[5 + c][:, :], ALU.add), state_ready)

                dve.wait_ge(gated_ready, GT * (g + 1))

                def weigh(h):
                    n = h0 + h
                    dve.wait_ge(s_ready, n + 1)
                    S = ssm_S[n % 3][:, :]
                    did(V.tensor_tensor(S, S, cbm[:, :, :].rearrange("p c l -> p (c l)"), ALU.mult), g_ready)

                def y_out(h):
                    n = h0 + h
                    r, j = SSM_P * (h % 2), h // 2
                    dve.wait_ge(y_done, n + 1)
                    did(V.scalar_tensor_tensor(xs[r:r + SSM_P, j, :], xs[r:r + SSM_P, j, :], par[r:r + SSM_P, PAR["ssm_d_2"] + g * TPG + j:PAR["ssm_d_2"] + g * TPG + j + 1],
                                               bank[5 + n % 2][0:SSM_P, :], ALU.mult, ALU.add), y_read)

                weigh(0)
                for h in range(HPG):
                    if h + 1 < HPG:
                        weigh(h + 1)
                    y_out(h)
                    if h % 2:
                        sync()
                        did(V.tensor_tensor(xs[:, h // 2, :], xs[:, h // 2, :], zs[:, h // 2, :], ALU.mult), sq_in)
                for j in range(TPG):
                    add_square(j, TPG)
            norm(z_rstd[:, :], SEQ, SSM_IN // SSM_G)
            for j in range(TPG):
                y_operand(SSM_G - 1, j)
            residual("ssm_out", ("norm_ffn_2", KD))
            ffn(1, None)

        @block.gpsimd
        def _(pool):
            lane = Lane(pool, pool_step)
            did, sync = lane.did, lane.sync
            G = nc.gpsimd
            for g in range(SSM_G):
                h0 = g * HPG

                def weigh_tile(j):
                    pool.wait_ge(x_tok_ready, 5 * g + 2 + j)
                    if g == 0 and j == 0:
                        pool.wait_ge(dt_tok_ready, 3)
                    sync()

                    def heads(v, n):
                        return v[:, 0:n, j * P:(j + 1) * P].rearrange("p c (h d) -> p c h d", d=SSM_P)

                    def per_head(k, n):
                        w = dt_tok[:, k, 0:n, h0 + 2 * j:h0 + 2 * j + 2].rearrange("p c (h o) -> p c h o", o=1)
                        return w.to_broadcast([P, n, 2, SSM_P])

                    did(G.tensor_tensor(heads(x_tok, TB), heads(x_tok, TB), per_head(1, TB), ALU.mult))
                    sync()
                    did(G.tensor_tensor(heads(xw, TB - 1), heads(x_tok, TB - 1), per_head(2, TB - 1), ALU.mult), xw_ready)

                for j, (kind, i) in enumerate(SSM_ORDER):
                    n = GT * g + j
                    dst = {"b": bT[:, :], "c": cT[:, :], "x": xs[:, i, :], "z": zs[:, i, :]}[kind]
                    pool.wait_ge(gate_ready, n + 1)
                    did(G.tensor_tensor(dst, (tmp, tmp2)[n % 2][:, :], sig[:, :], ALU.mult), gated_ready)
                    if SSM_TURN.get(j):
                        weigh_tile(SSM_TURN[j] - 1)
                for h in range(HPG):
                    n = h0 + h
                    E = ssm_E[n % 3][:, P:SEQ]
                    pool.wait_ge(e_ready, n + 1)
                    did(G.tensor_tensor(E, E, cT[:, P:SEQ], ALU.mult), ec_ready)
                sync()


_WEIGHTS = ["w_in", "w_conv_out", "w_sb_out", "w_mem_kv", "w_x_out", "w_out", "w_up", "w_down",
            "attn_w_in_2", "attn_w_out_2", "ssm_w_in_2", "ssm_w_out_2", "ffn_w_in_2", "ffn_w_out_2"]


def kernel(**inputs):
    import numpy as np
    import concourse.bacc as _bacc
    from concourse.bass_utils import run_bass_kernel_spmd as _run

    a = {k: np.asarray(v) for k, v in inputs.items()}

    def columns(v):
        return v.reshape(-1, P).T

    par = {n: columns(a[n]) for n in ("g_mix", "g_mem", "conv_w", "q_norm_g", "k_norm_g", "g_mlp", "norm_mix_2", "norm_ffn_2",
                                      "ffn_conv_w_2", "ffn_conv_b_2", "ssm_conv_w_2", "ssm_conv_b_2", "ssm_norm_2")}
    par["ssm_d_2"] = columns(np.repeat(a["ssm_d_2"].reshape(-1), SSM_P))
    for n in ("q_norm_a_2", "k_norm_a_2", "q_norm_b_2", "k_norm_b_2"):
        v = a[n].reshape(-1)
        par[n] = np.concatenate([v, v]).reshape(P, 1)
    par["sinks_2"] = np.repeat(a["sinks_2"].reshape(1, -1), P, axis=0)
    par["dt_bias"] = np.tile(a["ssm_dt_bias_2"].reshape(-1), P // SSM_HEADS).reshape(P, 1)
    par["a_log"] = np.tile(a["ssm_a_log_2"].reshape(-1), P // SSM_HEADS).reshape(P, 1)
    table = a["relpos_table_2"].reshape(A_HEADS, -1)
    reach = (table.shape[1] - 1) // 2
    rel = table[:, reach + np.clip(SEQ - 1 - np.arange(STRIP_E), -reach, reach)]

    i, j = np.arange(P)[:, None], np.arange(P)[None, :]
    f = np.float32
    m = np.arange(2 * P)[None, :]
    seen = (m // HD <= i // HD + 2) & (m // HD >= i // HD)
    con = {"ident": i == j, "neg_later": -(i >= j).astype(f), "neg_ones": -np.ones((P, P)), "past": i < j,
           "neg_future": -BIG * (i >= j), "ones": np.ones((P, P)), "head_ones": i // HD == j // HD, "causal": i <= j, "neg_before": -BIG * (i > j),
           "dist_b": np.where(seen, -np.abs(i - m + P), -BIG * 256.0), "flip": i + j == P - 1, "eps": np.full((P, 1), EPS)}
    arrays = {
        "xT": np.ascontiguousarray(a["x"].reshape(SEQ, KD, P).transpose(2, 1, 0)),
        "memT": np.ascontiguousarray(a["mem"].reshape(MEM, KD, P).transpose(2, 1, 0)),
        "par": np.ascontiguousarray(np.concatenate([par[n] for n in PAR], axis=1)),
        "con": np.ascontiguousarray(np.concatenate([con[n].astype(f) for n in CON], axis=1)),
        "rel": np.ascontiguousarray(rel),
    }
    for n in _WEIGHTS:
        w = a[n]
        arrays[n] = np.ascontiguousarray(w if n.startswith("ffn") else w.reshape(w.shape[1:]))
    nc = _bacc.Bacc("TRN2", target_bir_lowering=False, num_devices=1, dynamic_dma_scratch_size=2048)
    dram = {n: nc.dram_tensor(n, v.shape, F32, kind="ExternalInput").ap() for n, v in arrays.items()}
    out = nc.dram_tensor("outT", (P, KD, SEQ), F32, kind="ExternalOutput").ap()
    two_block_kernel(nc, dram, out)
    r = _run(nc, [arrays], core_ids=[0])
    return r.results[0]["outT"].transpose(2, 1, 0).reshape(1, SEQ, D)
```
